# Optimizing a Trainium2 kernel written in Bass

```python
import math
import jax
import jax.numpy as jnp
from jax import lax
import numpy as np

D_MODEL = 1024
BATCH = 1
SEQ = 512
DEPTH = 2

CHUNK = 64
N_EVEN = (DEPTH + 1) // 2
N_ODD = DEPTH // 2

GLA_HEADS = 4
GLA_DK = 64
GLA_DV = 128
GLA_GATE_RANK = 16
GLA_TAU = 16.0

SWA_Q_HEADS = 8
SWA_KV_HEADS = 2
SWA_HEAD_DIM = 64
SWA_WINDOW = 128
SWA_WINDOW_CHUNKS = SWA_WINDOW // CHUNK
ROPE_THETA = 10000.0

GDN_HEADS = 8
GDN_DK = 128
GDN_DV = 128
CONV_K = 4
CONV_CH = 2 * GDN_HEADS * GDN_DK + GDN_HEADS * GDN_DV

D_FF = ((8 * D_MODEL + 3 * 256 - 1) // (3 * 256)) * 256

ALPHA = (2 * DEPTH) ** 0.25
BETA_INIT = (8 * DEPTH) ** -0.25
LN_EPS = 1e-5
RMS_EPS = 1e-6

EVEN_WIDTHS = (GLA_HEADS * GLA_DK, GLA_HEADS * GLA_DK, GLA_HEADS * GLA_DV, GLA_GATE_RANK,
               GLA_HEADS * GLA_DV, SWA_Q_HEADS * SWA_HEAD_DIM, SWA_KV_HEADS * SWA_HEAD_DIM,
               SWA_KV_HEADS * SWA_HEAD_DIM)
EVEN_IN = sum(EVEN_WIDTHS)
EVEN_MIX = GLA_HEADS * GLA_DV + SWA_Q_HEADS * SWA_HEAD_DIM
ODD_WIDTHS = (CONV_CH, GDN_HEADS, GDN_HEADS, GDN_HEADS * GDN_DV)
ODD_IN = sum(ODD_WIDTHS)
ODD_MIX = GDN_HEADS * GDN_DV

kernel_name = 'hybrid_gla_swa_gdn_deepnorm_trunk'

def _split_cols(h, widths):
    out, start = [], 0
    for w in widths:
        out.append(h[..., start:start + w])
        start += w
    return out

def _layer_norm(x, g, b):
    xf = x.astype(jnp.float32)
    mu = jnp.mean(xf, -1, keepdims=True)
    xc = xf - mu
    var = jnp.mean(xc * xc, -1, keepdims=True)
    y = xc * lax.rsqrt(var + LN_EPS) * g.astype(jnp.float32) + b.astype(jnp.float32)
    return y.astype(x.dtype)

def _norm_no_affine(t):
    mu = jnp.mean(t, -1, keepdims=True)
    tc = t - mu
    return tc * lax.rsqrt(jnp.mean(tc * tc, -1, keepdims=True) + LN_EPS)

def _rms_norm(t):
    return t * lax.rsqrt(jnp.mean(t * t, -1, keepdims=True) + RMS_EPS)

def _l2norm(t):
    return t * lax.rsqrt(jnp.sum(t * t, -1, keepdims=True) + 1e-6)

def _to_chunks(t, n_heads, d):
    b, s = t.shape[:2]
    return t.reshape(b, s // CHUNK, CHUNK, n_heads, d).transpose(0, 3, 1, 2, 4)

def _from_chunks(o):
    b, h, nc, l, d = o.shape
    return o.transpose(0, 2, 3, 1, 4).reshape(b, nc * l, h, d)

def _rope(t, pos):
    half = t.shape[-1] // 2
    inv = ROPE_THETA ** (-jnp.arange(half, dtype=jnp.float32) / half)
    ang = pos[:, None] * inv[None, :]
    cos = jnp.cos(ang)[:, None, :]
    sin = jnp.sin(ang)[:, None, :]
    tf = t.astype(jnp.float32)
    t1, t2 = tf[..., :half], tf[..., half:]
    return jnp.concatenate([t1 * cos - t2 * sin, t2 * cos + t1 * sin], -1).astype(t.dtype)

def _gla(q, k, v, a_lr, r, w_a2, b_a, norm_g):
    f32 = jnp.float32
    bsz, s = q.shape[:2]
    qc = _to_chunks(q.astype(f32), GLA_HEADS, GLA_DK) * (GLA_DK ** -0.5)
    kc = _to_chunks(k.astype(f32), GLA_HEADS, GLA_DK)
    vc = _to_chunks(v.astype(f32), GLA_HEADS, GLA_DV)
    log_a = jax.nn.log_sigmoid((a_lr @ w_a2 + b_a).astype(f32)) / GLA_TAU
    bcum = jnp.cumsum(_to_chunks(log_a, GLA_HEADS, GLA_DK), axis=3)
    b_last = bcum[:, :, :, -1, :]
    q_g = qc * jnp.exp(bcum)
    k_g = kc * jnp.exp(-bcum)
    k_d = kc * jnp.exp(b_last[:, :, :, None, :] - bcum)
    causal = jnp.tril(jnp.ones((CHUNK, CHUNK), dtype=bool))
    attn = jnp.where(causal, jnp.einsum('bhcid,bhcjd->bhcij', q_g, k_g), 0.0)
    o_intra = jnp.einsum('bhcij,bhcjv->bhciv', attn, vc)

    def step(state, inp):
        q_c, k_c, v_c, bl_c = inp
        o_c = jnp.einsum('bhid,bhdv->bhiv', q_c, state)
        state = state * jnp.exp(bl_c)[..., None] + jnp.einsum('bhjd,bhjv->bhdv', k_c, v_c)
        return state, o_c

    s0 = jnp.zeros((bsz, GLA_HEADS, GLA_DK, GLA_DV), f32)
    mv = lambda t: jnp.moveaxis(t, 2, 0)
    _, o_inter = lax.scan(step, s0, (mv(q_g), mv(k_d), mv(vc), mv(b_last)))
    o = _from_chunks(o_intra + jnp.moveaxis(o_inter, 0, 2))
    o = _norm_no_affine(o).reshape(bsz, s, GLA_HEADS * GLA_DV)
    o = o * norm_g.astype(f32) * jax.nn.silu(r.astype(f32))
    return o.astype(q.dtype)

def _swa(q, k, v, sinks):
    f32 = jnp.float32
    bsz, s = q.shape[:2]
    nc = s // CHUNK
    grp = SWA_Q_HEADS // SWA_KV_HEADS
    nw = SWA_WINDOW_CHUNKS
    pos = jnp.arange(s, dtype=f32)
    q = _rope(q.reshape(bsz, s, SWA_Q_HEADS, SWA_HEAD_DIM), pos)
    k = _rope(k.reshape(bsz, s, SWA_KV_HEADS, SWA_HEAD_DIM), pos)
    qc = q.reshape(bsz, nc, CHUNK, SWA_KV_HEADS, grp, SWA_HEAD_DIM)
    kc = k.reshape(bsz, nc, CHUNK, SWA_KV_HEADS, SWA_HEAD_DIM)
    vc = v.reshape(bsz, nc, CHUNK, SWA_KV_HEADS, SWA_HEAD_DIM)

    def band(t):
        blocks = []
        for sh in range(nw - 1, -1, -1):
            blocks.append(jnp.pad(t, ((0, 0), (sh, 0), (0, 0), (0, 0), (0, 0)))[:, :nc])
        return jnp.concatenate(blocks, axis=2)

    kw, vw = band(kc), band(vc)
    shift = jnp.repeat(jnp.arange(nw - 1, -1, -1), CHUNK)
    valid = jnp.arange(nc)[:, None] >= shift[None, :]
    sc = jnp.einsum('bcikgd,bcjkd->bckgij', qc, kw).astype(f32) * (SWA_HEAD_DIM ** -0.5)
    sc = jnp.where(valid[None, :, None, None, None, :], sc, -jnp.inf)
    sink = jnp.broadcast_to(
        sinks.astype(f32).reshape(SWA_KV_HEADS, grp)[None, None, :, :, None, None],
        sc.shape[:-1] + (1,))
    p = jax.nn.softmax(jnp.concatenate([sc, sink], -1), axis=-1)[..., :-1]
    o = jnp.einsum('bckgij,bcjkd->bcikgd', p.astype(vw.dtype), vw)
    return o.reshape(bsz, s, SWA_Q_HEADS * SWA_HEAD_DIM)

def _even_mixer(x, w_in, w_a2, b_a, gla_norm_g, sinks, w_out):
    h = x @ w_in
    gq, gk, gv, ga, gr, sq, sk, sv = _split_cols(h, EVEN_WIDTHS)
    o = jnp.concatenate([_gla(gq, gk, gv, ga, gr, w_a2, b_a, gla_norm_g),
                         _swa(sq, sk, sv, sinks)], -1)
    return o @ w_out

def _causal_dwconv(t, w):
    return lax.conv_general_dilated(
        t, w.astype(t.dtype)[:, None, :], window_strides=(1,), padding=[(CONV_K - 1, 0)],
        dimension_numbers=('NWC', 'WIO', 'NWC'), feature_group_count=t.shape[-1])

def _gated_delta(q, k, v, beta, g):
    bsz, s = q.shape[:2]
    nc = s // CHUNK
    qc = _to_chunks(q, GDN_HEADS, GDN_DK)
    kc = _to_chunks(k, GDN_HEADS, GDN_DK)
    vc = _to_chunks(v, GDN_HEADS, GDN_DV)
    bc = beta.reshape(bsz, nc, CHUNK, GDN_HEADS).transpose(0, 3, 1, 2)
    gc = g.reshape(bsz, nc, CHUNK, GDN_HEADS).transpose(0, 3, 1, 2)
    decay = jnp.cumsum(gc, axis=-1)
    causal = jnp.tril(jnp.ones((CHUNK, CHUNK), dtype=bool))
    strict = jnp.tril(jnp.ones((CHUNK, CHUNK), dtype=bool), -1)
    gam = jnp.exp(jnp.where(causal, decay[..., :, None] - decay[..., None, :], -jnp.inf))
    kb = kc * bc[..., None]
    vb = vc * bc[..., None]
    a = jnp.where(strict, jnp.einsum('bhcid,bhcjd->bhcij', kb, kc) * gam, 0.0)
    eye = jnp.eye(CHUNK, dtype=a.dtype)
    tmat = lax.linalg.triangular_solve(a + eye, jnp.broadcast_to(eye, a.shape),
                                       left_side=True, lower=True, unit_diagonal=True)
    u = tmat @ vb
    w = tmat @ (kb * jnp.exp(decay)[..., None])
    attn = jnp.einsum('bhcid,bhcjd->bhcij', qc, kc) * gam
    qd = qc * jnp.exp(decay)[..., None]
    dl = decay[..., -1]
    kd = kc * jnp.exp(dl[..., None] - decay)[..., None]

    def step(state, inp):
        qd_c, kd_c, u_c, w_c, attn_c, dl_c = inp
        v_new = u_c - w_c @ state
        o_c = qd_c @ state + attn_c @ v_new
        state = state * jnp.exp(dl_c)[..., None, None] + jnp.einsum('bhjd,bhjv->bhdv', kd_c, v_new)
        return state, o_c

    s0 = jnp.zeros((bsz, GDN_HEADS, GDN_DK, GDN_DV), jnp.float32)
    mv = lambda t: jnp.moveaxis(t, 2, 0)
    _, o = lax.scan(step, s0, (mv(qd), mv(kd), mv(u), mv(w), mv(attn), mv(dl)))
    return _from_chunks(jnp.moveaxis(o, 0, 2))

def _odd_mixer(x, w_in, conv_w, a_log, dt_bias, norm_g, w_out):
    f32 = jnp.float32
    bsz, s, _ = x.shape
    h = x @ w_in
    qkv, beta_l, a, gate = _split_cols(h, ODD_WIDTHS)
    qkv = jax.nn.silu(_causal_dwconv(qkv, conv_w)).astype(f32)
    q, k, v = _split_cols(qkv, (GDN_HEADS * GDN_DK, GDN_HEADS * GDN_DK, GDN_HEADS * GDN_DV))
    q = _l2norm(q.reshape(bsz, s, GDN_HEADS, GDN_DK)) * (GDN_DK ** -0.5)
    k = _l2norm(k.reshape(bsz, s, GDN_HEADS, GDN_DK))
    v = v.reshape(bsz, s, GDN_HEADS, GDN_DV)
    beta = jax.nn.sigmoid(beta_l.astype(f32))
    g = -jnp.exp(a_log.astype(f32)) * jax.nn.softplus(a.astype(f32) + dt_bias.astype(f32))
    o = _gated_delta(q, k, v, beta, g)
    o = _rms_norm(o) * norm_g.astype(f32) * jax.nn.silu(gate.astype(f32).reshape(bsz, s, GDN_HEADS, GDN_DV))
    return o.reshape(bsz, s, ODD_MIX).astype(x.dtype) @ w_out

def _swiglu(x, w_gate, w_up, w_down):
    return (jax.nn.silu(x @ w_gate) * (x @ w_up)) @ w_down

def setup_inputs(seed: int = 0) -> dict:
    key = jax.random.key(seed)
    ks = jax.random.split(key, 24)
    f32 = jnp.float32
    nrm = lambda kk, shape, scale: jax.random.normal(kk, shape, f32) * scale
    dt0 = jnp.exp(jax.random.uniform(ks[10], (N_ODD, GDN_HEADS), f32, math.log(1e-3), math.log(1e-1)))
    return {
        'x': nrm(ks[0], (BATCH, SEQ, D_MODEL), 1.0),
        'ev_w_in': nrm(ks[1], (N_EVEN, D_MODEL, EVEN_IN), D_MODEL ** -0.5),
        'ev_gla_w_a2': nrm(ks[2], (N_EVEN, GLA_GATE_RANK, GLA_HEADS * GLA_DK), GLA_GATE_RANK ** -0.5),
        'ev_gla_b_a': nrm(ks[3], (N_EVEN, GLA_HEADS * GLA_DK), 0.1),
        'ev_gla_norm_g': 1.0 + nrm(ks[4], (N_EVEN, GLA_HEADS * GLA_DV), 0.02),
        'ev_swa_sinks': nrm(ks[5], (N_EVEN, SWA_Q_HEADS), 1.0),
        'ev_w_out': nrm(ks[6], (N_EVEN, EVEN_MIX, D_MODEL), BETA_INIT * EVEN_MIX ** -0.5),
        'od_w_in': nrm(ks[7], (N_ODD, D_MODEL, ODD_IN), D_MODEL ** -0.5),
        'od_conv_w': nrm(ks[8], (N_ODD, CONV_K, CONV_CH), CONV_K ** -0.5),
        'od_a_log': jnp.log(jax.random.uniform(ks[9], (N_ODD, GDN_HEADS), f32, 1.0, 16.0)),
        'od_dt_bias': dt0 + jnp.log(-jnp.expm1(-dt0)),
        'od_norm_g': 1.0 + nrm(ks[11], (N_ODD, GDN_DV), 0.02),
        'od_w_out': nrm(ks[12], (N_ODD, ODD_MIX, D_MODEL), BETA_INIT * ODD_MIX ** -0.5),
        'ffn_w_gate': nrm(ks[13], (DEPTH, D_MODEL, D_FF), D_MODEL ** -0.5),
        'ffn_w_up': nrm(ks[14], (DEPTH, D_MODEL, D_FF), D_MODEL ** -0.5),
        'ffn_w_down': nrm(ks[15], (DEPTH, D_FF, D_MODEL), BETA_INIT * D_FF ** -0.5),
        'ln1_g': 1.0 + nrm(ks[16], (DEPTH, D_MODEL), 0.02),
        'ln1_b': nrm(ks[17], (DEPTH, D_MODEL), 0.02),
        'ln2_g': 1.0 + nrm(ks[18], (DEPTH, D_MODEL), 0.02),
        'ln2_b': nrm(ks[19], (DEPTH, D_MODEL), 0.02),
    }

def reference(x, ev_w_in, ev_gla_w_a2, ev_gla_b_a, ev_gla_norm_g, ev_swa_sinks, ev_w_out,
              od_w_in, od_conv_w, od_a_log, od_dt_bias, od_norm_g, od_w_out,
              ffn_w_gate, ffn_w_up, ffn_w_down, ln1_g, ln1_b, ln2_g, ln2_b):
    for layer in range(DEPTH):
        i = layer // 2
        if layer % 2 == 0:
            mix = _even_mixer(x, ev_w_in[i], ev_gla_w_a2[i], ev_gla_b_a[i], ev_gla_norm_g[i],
                              ev_swa_sinks[i], ev_w_out[i])
        else:
            mix = _odd_mixer(x, od_w_in[i], od_conv_w[i], od_a_log[i], od_dt_bias[i],
                             od_norm_g[i], od_w_out[i])
        x = _layer_norm(ALPHA * x + mix, ln1_g[layer], ln1_b[layer])
        x = _layer_norm(ALPHA * x + _swiglu(x, ffn_w_gate[layer], ffn_w_up[layer], ffn_w_down[layer]),
                        ln2_g[layer], ln2_b[layer])
    return x


_drawn_inputs = setup_inputs


def setup_inputs(seed=0):
    import zlib

    import numpy as np

    out = dict(_drawn_inputs(seed))
    spreads = {}
    factors = {'ev_gla_w_a2': 3.332,
     'ev_gla_b_a': 8.0,
     'ev_gla_norm_g': 8.0,
     'ev_swa_sinks': 8.0,
     'od_norm_g': 67.017}
    for name, (base, spread) in spreads.items():
        noise = np.random.default_rng([zlib.crc32(name.encode()), seed]).standard_normal(out[name].shape)
        drawn = base * np.exp(spread * noise) if base else spread * noise
        out[name] = jnp.asarray(drawn.astype(out[name].dtype))
    for name, factor in factors.items():
        out[name] = (out[name] * factor).astype(out[name].dtype)
    return out
```

```python
from contextlib import ExitStack

import numpy as np

import concourse.bass as bass
from concourse import mybir

F32 = mybir.dt.float32
F32R = mybir.dt.float32r
I32 = mybir.dt.int32
ALU = mybir.AluOpType
ACT = mybir.ActivationFunctionType
AX = mybir.AxisListType.X

P = 128
D = 1024
SEQ = 512
NT = SEQ // P
KD = D // P
CH = 64
NC = SEQ // CH
DFF = ((8 * D + 3 * 256 - 1) // (3 * 256)) * 256
KF = DFF // P
ALPHA = 4.0 ** 0.25
LN_EPS = 1e-5
RMS_EPS = 1e-6

GH, GDK, GDV, GRANK, TAU = 4, 64, 128, 16, 16.0
QH, KVH, HD = 8, 2, 64
RH = HD // 2
GDN_H = 8
CONV_K = 4
CONV_CH = 3 * D
NEG = -1e30

GQ0 = 0
GK0 = GQ0 + GH * GDK
GV0 = GK0 + GH * GDK
GA0 = GV0 + GH * GDV
GR0 = GA0 + GRANK
SQ0 = GR0 + GH * GDV
SKV0 = SQ0 + QH * HD
OQ0, OK0, OV0 = 0, D, 2 * D
BA0 = CONV_CH
OG0 = BA0 + 2 * GDN_H

WCOLS = 2048
LEVELS = (1, 2, 4, 8, 16, 32)


def shape_constants():
    i = np.arange(P)
    same = (i[:, None] // CH) == (i[None, :] // CH)
    upto = (same & (i[:, None] <= i[None, :])).astype(np.float32)
    block = same.astype(np.float32)
    neg_t = np.where(same & (i[:, None] <= i[None, :]), 0.0, NEG).astype(np.float32)
    pos_l = np.where(same & (i[:, None] > i[None, :]), 0.0, -NEG).astype(np.float32)
    r, c = i[:, None] % CH, np.arange(CH)[None, :]
    levels = [((r // (2 * b) == c // (2 * b)) & (r % (2 * b) >= b) & (c % (2 * b) < b)) for b in LEVELS]
    levels = np.concatenate([m.astype(np.float32) for m in levels], 1)
    inv = np.float32(10000.0) ** (-np.arange(RH, dtype=np.float32) / np.float32(RH))
    ang = np.arange(SEQ, dtype=np.float32)[:, None] * inv[None, :]
    rope = np.stack([np.cos(ang), np.sin(ang)], 1).astype(np.float32)
    rope = rope.reshape(NT, P, 2 * RH).transpose(1, 0, 2).reshape(P, -1)
    keep = np.broadcast_to((np.arange(SEQ) % CH != 0).astype(np.float32), (P, SEQ))
    return {
        "c_eye": np.eye(P, dtype=np.float32),
        "c_upto": upto,
        "c_odd": np.ascontiguousarray(np.concatenate([block, neg_t, pos_l, levels], 1)),
        "c_rope": np.ascontiguousarray(rope),
        "c_keep": np.ascontiguousarray(keep),
    }


def weight_plan(A):
    blocks = []

    def add(name, w, k0, nk, c0, width):
        view = w[k0 * P:(k0 + nk) * P, c0:c0 + width].rearrange("(k p) n -> p k n", p=P)
        blocks.append((name, k0, nk, width, view))

    def add_tm(name, w, kt, c0, width):
        for k0 in range(0, kt, 4):
            add(name, w, k0, min(4, kt - k0), c0, width)

    ev, od = A["ev_w_in"][0], A["od_w_in"][0]

    def ffn(layer):
        g, u, d = (A[n][layer] for n in ("ffn_w_gate", "ffn_w_up", "ffn_w_down"))
        for f in range(0, KF, 2):
            add(("gate", layer, f), g, 0, KD, f * P, 256)
            add(("up", layer, f), u, 0, KD, f * P, 256)
        for half in range(2):
            add_tm(("down", layer, half), d, KF, half * 512, 512)

    add(("skv",), ev, 0, KD, SKV0, 2 * KVH * HD)
    add_tm(("sq",), ev, KD, SQ0, 512)
    add(("gq",), ev, 0, KD, GQ0, 256)
    add(("gk",), ev, 0, KD, GK0, 256)
    add(("ga",), ev, 0, KD, GA0, P)
    add_tm(("gv",), ev, KD, GV0, 512)
    add_tm(("gr",), ev, KD, GR0, 512)
    for half in range(2):
        add_tm(("mix", 0, half), A["ev_w_out"][0], KD, half * 512, 512)
    ffn(0)
    add(("ba",), od, 0, KD, BA0, 2 * GDN_H)
    for part, c0 in ((1, OK0), (0, OQ0), (2, OV0)):
        for n in range(0, KD, 2):
            add(("conv", part * KD + n), od, 0, KD, c0 + n * P, 256)
    for half in range(2):
        add_tm(("og", half), od, KD, OG0 + half * 512, 512)
    for half in range(2):
        add_tm(("mix", 1, half), A["od_w_out"][0], KD, half * 512, 512)
    ffn(1)
    return blocks


CONV_ORDER = [part * KD + n for part in (1, 0, 2) for n in range(KD)]


def unit_plan():
    u = [("const", 0), ("const", 1)]
    tiles = range(NT)

    def ln(i):
        u.extend(("xT", i, k) for k in range(KD))

    def ffn(layer):
        for f in range(0, KF, 2):
            u.extend([("gate", layer, f), ("gate", layer, f + 1), ("up", layer, f), ("up", layer, f + 1)])
        for half in range(2):
            u.extend(("down", layer, half, t) for t in tiles)

    ln(0)
    u += [("skv", t) for t in tiles] + [("sq", t) for t in tiles]
    u += [("gq", 0), ("gq", 1), ("gk", 0), ("gk", 1), ("ga",)]
    for t in tiles:
        u += [("qT", t), ("kT", t)]
    u += [("gv", t) for t in tiles] + [("a2", 0), ("a2", 1)]
    u += [("gr", t) for t in tiles]
    for t in tiles:
        u += [("score", t, 0), ("score", t, 1), ("kd", t), ("gattn", t), ("gstate", t, 0), ("gout", t),
              ("gstate", t, 1), ("probT", t, 0), ("probT", t, 1), ("sout", t)]
        if t:
            u += [("oT", 0, t - 1, 0), ("oT", 0, t - 1, 1)]
    u += [("oT", 0, NT - 1, 0), ("oT", 0, NT - 1, 1)]
    u += [("mix", 0, half, t) for half in range(2) for t in tiles]
    ln(1)
    ffn(0)
    ln(2)
    u += [("ba",)]
    for i, n in enumerate(CONV_ORDER):
        u.append(("conv", n))
        if i == 3:
            u.append(("decay",))
        if i >= 2 and CONV_ORDER[i - 2] < 2 * KD:
            u.append(("norm", CONV_ORDER[i - 2]))
    u += [("og", half, t) for half in range(2) for t in tiles]
    for t in tiles:
        for name in ("kTM", "vTM", "drow"):
            u += [(name, t, 0), (name, t, 1)]
        if t:
            u += [("oT", 1, t - 1, 0), ("oT", 1, t - 1, 1)]
        for name in ("khT", "gram", "qk", "s0"):
            u += [(name, t, 0), (name, t, 1)]
        for b in LEVELS[1:]:
            for name in ("m1", "ds") + (("dt",) if b < LEVELS[-1] else ()):
                u += [(name, t, b, 0), (name, t, b, 1)]
        u += [("u", t, 0), ("u", t, 1), ("w", t, 0), ("w", t, 1)]
        u += [("ws", t, 0, 0), ("ws", t, 0, 1), ("o", t, 0), ("o", t, 1), ("kv", t, 0, 0), ("kv", t, 0, 1),
              ("ws", t, 1, 0), ("ws", t, 1, 1), ("kv", t, 1, 0), ("kv", t, 1, 1)]
    u += [("oT", 1, NT - 1, 0), ("oT", 1, NT - 1, 1)]
    u += [("mix", 1, half, t) for half in range(2) for t in tiles]
    ln(3)
    ffn(1)
    return {key: i for i, key in enumerate(u)}


def trunk_kernel(nc, A, out):
    blocks = weight_plan(A)
    NB = len(blocks)
    unit = unit_plan()
    first_block = {}
    for b, blk in enumerate(blocks):
        first_block.setdefault(blk[0], b)

    ctx = ExitStack()
    with ctx:
        base = (nc.sbuf_base + 63) // 64 * 64
        here = [base]

        def sb(name, shape, dt=F32, at=None):
            size = (int(np.prod(shape[1:])) * 4 + 31) // 32 * 32
            off = here[0] if at is None else at
            if at is None:
                here[0] += size
            assert off + size <= nc.sbuf_usable_end, (name, off + size)
            return nc.alloc_sbuf_tensor_at(name, shape, dt, offset=off)

        w_raw = sb("w_raw", [P, 2, WCOLS])
        w_hi = sb("w_hi", [P, 2, WCOLS], F32R)
        w_lo = sb("w_lo", [P, 2, WCOLS], F32R)
        x_hi = sb("x_hi", [P, KD, SEQ], F32R)
        x_lo = sb("x_lo", [P, KD, SEQ], F32R)
        x_tm = sb("x_tm", [P, NT, D])
        eye = sb("eye", [P, P])
        upto = sb("upto", [P, P])
        small0 = here[0]
        lnc = sb("lnc", [P, 66])
        convw = sb("convw", [P, CONV_K * 3 * KD])
        sinks = sb("sinks", [P, QH])
        a_log = sb("a_log", [P, GDN_H])
        dt_bias = sb("dt_bias", [P, GDN_H])
        onorm_row = sb("onorm_row", [P, P])
        stats = sb("stats", [P, NT, 2, 6])
        mv = sb("mv", [P, NT, 2])
        rstd = sb("rstd", [P, NT])
        nmr = sb("nmr", [P, NT])
        TH = NT * GDN_H
        ba = sb("ba", [P, NT, 2 * GDN_H])
        beta = sb("beta", [P, NT, GDN_H])
        gdec = sb("gdec", [P, NT, GDN_H])
        g_tmp = sb("g_tmp", [P, NT, GDN_H])
        dec = sb("dec", [P, 2, NT, GDN_H])
        to_end = sb("to_end", [P, NT, GDN_H])
        bexp = sb("bexp", [P, NT, GDN_H])
        nrm = sb("nrm", [P, 2 * KD, NT])
        edl = sb("edl", [P, GDN_H, 2])
        oms = sb("oms", [P, GDN_H])
        ones = sb("ones", [P, 1])
        eps = sb("eps", [P, 2])
        s_max = sb("s_max", [P, QH])
        s_snk = sb("s_snk", [P, QH])
        s_den = sb("s_den", [P, QH])
        g_mu = sb("g_mu", [P, GH])
        g_var = sb("g_var", [P, GH])
        ARENA = here[0]

        q_pad = sb("q_pad", [P, GH, SEQ])
        g_q = sb("g_q", [P, 2, SEQ])
        g_k = sb("g_k", [P, 2, SEQ])
        g_kd = sb("g_kd", [P, 2, SEQ])
        g_B = sb("g_B", [P, 2, SEQ])
        g_e = sb("g_e", [P, 2, SEQ])
        g_v = sb("g_v", [P, NT, GH * GDV])
        g_r = sb("g_r", [P, NT, GH * GDV])
        g_ga = sb("g_ga", [GRANK, SEQ])
        g_a2 = sb("g_a2", [GRANK, GH * GDK])
        g_keep = sb("g_keep", [P, SEQ])
        g_norm = sb("g_norm", [P, GH * GDV])
        g_at = sb("g_at", [P, GH, P])
        g_kdt = sb("g_kdt", [P, 2, P])
        g_S = sb("g_S", [P, 2, 2, GDV])
        rope = sb("rope", [P, NT, 2, RH])
        r_tmp = sb("r_tmp", [P, 4, QH, RH])
        s_v = sb("s_v", [P, NT, KVH * HD])
        s_vsh = sb("s_vsh", [P, NT, KVH * HD])
        s_qT = sb("s_qT", [P, QH // 2, SEQ])
        s_kT = sb("s_kT", [P, 2 * KVH, CH + SEQ])
        q_rot_at = here[0]
        q_rot = sb("q_rot", [P, NT, QH * HD])
        k_pad = sb("k_pad", [P, NT, 2 * KVH, P])
        s_p = sb("s_p", [P, 2, 512], at=q_rot_at)
        s_pT = sb("s_pT", [P, 2, 512], at=q_rot_at + 4096)
        o_tm = sb("o_tm", [P, 2, D], at=q_rot_at + 8192)

        here[0] = ARENA
        h_hi = sb("h_hi", [P, KF, SEQ], F32R)
        h_lo = sb("h_lo", [P, KF, SEQ], F32R)
        ln_rows = sb("ln_rows", [P, 2, D])
        f_a = sb("f_a", [P, 2, SEQ])
        f_b = sb("f_b", [P, 2, SEQ])
        rows_at = ARENA + 2 * KF * SEQ * 4
        vec_rows = sb("vec_rows", [P, P], at=rows_at)
        conv_rows = sb("conv_rows", [P, P], at=rows_at + 512)

        here[0] = ARENA
        qkv = sb("qkv", [P, 3 * KD, SEQ])
        gate_s = sb("gate_s", [P, NT, D])
        o_block = sb("o_block", [P, P])
        o_negt = sb("o_negt", [P, P])
        o_posl = sb("o_posl", [P, P])
        o_lvl = sb("o_lvl", [P, len(LEVELS), CH])
        KH = sb("KH", [P, GDN_H, P])
        KB = sb("KB", [P, GDN_H, P])
        GU = sb("GU", [P, GDN_H, P])
        EE = sb("EE", [P, GDN_H, P])
        GT = sb("GT", [P, GDN_H, P])
        GA = sb("GA", [P, GDN_H, P])
        TT = sb("TT", [P, GDN_H, P])
        SS = sb("SS", [P, GDN_H, P])
        M1 = sb("M1", [P, GDN_H, P])
        ST = sb("ST", [P, GDN_H, P])

        banks = [ctx.enter_context(nc.psum_tensor(f"bank{i}", [P, 512], F32)) for i in range(8)]

        def sem(name):
            return ctx.enter_context(nc.semaphore(name))

        bank_full = [sem(f"bank_full{i}") for i in range(8)]
        bank_taken = [sem(f"bank_taken{i}") for i in range(8)]
        w_landed = [sem(f"w_landed{i}") for i in range(2)]
        w_hi_ready = sem("w_hi_ready")
        w_lo_ready = sem("w_lo_ready")
        w_used = sem("w_used")
        consts = sem("consts")
        const_cols = sem("const_cols")
        zeroed = sem("zeroed")

        def bank(key):
            return banks[unit[key] % 8]

        def full(e, key):
            if e is nc.vector or e is nc.scalar:
                e.drain()
            e.wait_ge(bank_full[unit[key] % 8], unit[key] // 8 + 1)

        def taken(e, key):
            e.wait_ge(bank_taken[unit[key] % 8], unit[key] // 8 + 1)

        def take(ins, key):
            ins.then_inc(bank_taken[unit[key] % 8], 1)

        block_end = []
        count = 0
        for b, (name, k0, nk, width, _) in enumerate(blocks):
            last = b + 1 == NB or blocks[b + 1][0] != name
            if not last:
                count += 1
                block_end.append((w_used, count))
            else:
                key = {"skv": ("skv", NT - 1), "sq": ("sq", NT - 1), "gv": ("gv", NT - 1), "gr": ("gr", NT - 1),
                       "gq": ("gq", 1), "gk": ("gk", 1), "ga": ("ga",), "ba": ("ba",)}.get(name[0])
                if name[0] in ("gate", "up"):
                    key = (name[0], name[1], name[2] + 1)
                elif name[0] == "conv":
                    key = ("conv", name[1] + 1)
                elif key is None:
                    key = (*name, NT - 1)
                block_end.append((bank_full[unit[key] % 8], unit[key] // 8 + 1))

        s = {n: sem(n) for n in (
            "x_landed", "ln_landed", "x_hi_ready", "x_lo_ready", "z_norm", "ln_stat", "ln_var",
            "x_affine", "out_sent", "act_step", "dve_step", "o_hi_ready", "h_hi_ready", "h_lo_ready",
            "sv_copied", "sv_shifted", "q_rotated", "k_rotated", "a2_exp", "a2_mid", "g_scan", "g_exp", "g_gate",
            "k_decayed", "q_gated", "k_gated", "s_shift", "s_prob", "o_var", "o_rstd", "o_even",
            "ba_exp", "ba_mid", "g_ready", "dec_ready", "dec_exp", "conv_raw", "conv_silu",
            "conv_sq", "rn_ready", "gu_ready", "e_ready", "arg_ready", "gam_ready", "a_ready", "t0_ready", "ab_ready",
            "q_decayed", "kb_ready", "kd_ready", "state0", "ov_ready", "or_ready", "o_odd",
        )}

        block_ = ctx.enter_context(nc.Block())
        Q4 = GDN_H // 2
        def conv_acc(i):
            return KH[:, 4 * (i % 2):4 * (i % 2) + 4, :].rearrange("p a b -> p (a b)")

        def conv_squares(i):
            return KB[:, 4 * (i % 2):4 * (i % 2) + 4, :].rearrange("p a b -> p (a b)")

        tile_cols = [slice(t * P, (t + 1) * P) for t in range(NT)]
        hsl = [slice(0, Q4), slice(Q4, GDN_H)]
        N_CONST = 15

        @block_.sync
        def _(sp):
            def load_block(b):
                name, k0, nk, width, view = blocks[b]
                if b >= 2:
                    sp.wait_ge(w_lo_ready, b - 1)
                dst = w_raw[:, b % 2, 0:nk * width].rearrange("p (k n) -> p k n", k=nk)
                sp.dma_start(dst, view).then_inc(w_landed[b % 2], 16)

            sp.dma_start(x_tm[:, :, :], A["x"][0].rearrange("(t p) d -> p t d", p=P)).then_inc(s["x_landed"], 16)
            sp.dma_start(eye[:, :], A["c_eye"]).then_inc(s["x_landed"], 16)
            load_block(0)
            load_block(1)
            small = [(upto[:, :], A["c_upto"])]
            for i, nm in enumerate(("ln1_g", "ln1_b", "ln2_g", "ln2_b")):
                small.append((vec_rows[16 * i:16 * i + 16, :], A[nm].rearrange("l (k p) -> (l k) p", p=P)))
            small.append((vec_rows[64:66, :], A["ev_gla_b_a"].rearrange("l (k p) -> (l k) p", p=P)))
            small.append((conv_rows[0:96, :], A["od_conv_w"][0].rearrange("c (n p) -> (c n) p", p=P)))
            small.append((sinks[:, :], A["ev_swa_sinks"][0:1, :].broadcast_to([P, QH])))
            small.append((a_log[:, :], A["od_a_log"][0:1, :].broadcast_to([P, GDN_H])))
            small.append((dt_bias[:, :], A["od_dt_bias"][0:1, :].broadcast_to([P, GDN_H])))
            small.append((onorm_row[:, :], A["od_norm_g"][0:1, :].broadcast_to([P, P])))
            small.append((g_a2[:, :], A["ev_gla_w_a2"][0]))
            small.append((g_keep[:, :], A["c_keep"]))
            small.append((g_norm[:, :], A["ev_gla_norm_g"][0:1, :].broadcast_to([P, GH * GDV])))
            small.append((rope[:, :, :, :], A["c_rope"].rearrange("p (t c r) -> p t c r", t=NT, c=2)))
            for dst, src in small:
                sp.dma_start(dst, src).then_inc(consts, 16)
            assert len(small) == N_CONST

            def load_until(b):
                while at[0] < b:
                    load_block(at[0])
                    at[0] += 1

            def load_ln(i):
                g, v = (("ln1_g", "ln1_b"), ("ln2_g", "ln2_b"))[(i + 1) % 2]
                layer = (i - 1) // 2
                for j, nm in enumerate((g, v)):
                    sp.dma_start(ln_rows[:, j, :], A[nm][layer:layer + 1, :].broadcast_to([P, D]))\
                      .then_inc(s["ln_landed"], 16)

            at = [2]
            load_until(first_block[("gate", 0, 0)] + 1)
            taken(sp, ("oT", 0, NT - 1, 1))
            load_ln(1)
            load_until(first_block[("down", 0, 1)])
            sp.wait_ge(s["x_affine"], 2 * NT)
            load_ln(2)
            load_until(first_block[("ba",)] + 1)
            full(sp, ("down", 0, 1, NT - 1))
            for dst, c0, n in ((o_block, 0, P), (o_negt, P, P), (o_posl, 2 * P, P)):
                sp.dma_start(dst[:, :], A["c_odd"][:, c0:c0 + n]).then_inc(consts, 16)
            sp.dma_start(o_lvl[:, :, :], A["c_odd"][:, 3 * P:].rearrange("p (l c) -> p l c", c=CH)).then_inc(consts, 16)
            load_until(first_block[("gate", 1, 0)] + 1)
            taken(sp, ("oT", 1, NT - 1, 1))
            load_ln(3)
            load_until(first_block[("down", 1, 1)])
            sp.wait_ge(s["x_affine"], 6 * NT)
            load_ln(4)
            load_until(NB)
            for t in range(NT):
                sp.wait_ge(s["x_affine"], 6 * NT + 2 * (t + 1))
                sp.dma_start(out[0, t * P:(t + 1) * P, :], x_tm[:, t, :]).then_inc(s["out_sent"], 16)
            sp.wait_ge(s["out_sent"], 16 * NT)

        @block_.gpsimd
        def _(pool):
            def split_lo(b):
                name, k0, nk, width, _v = blocks[b]
                n = nk * width
                pool.wait_ge(w_hi_ready, b + 1)
                pool.tensor_tensor(w_lo[:, b % 2, 0:n], w_raw[:, b % 2, 0:n], w_hi[:, b % 2, 0:n].bitcast(F32),
                                   ALU.subtract).then_inc(w_lo_ready, 1)

            pool.memset(q_pad[:, :, :], 0.0).then_inc(zeroed, 1)
            pool.memset(g_at[:, :, :], 0.0).then_inc(zeroed, 1)
            pool.memset(g_S[:, :, :, :], 0.0).then_inc(zeroed, 1)
            pool.memset(s_kT[:, :, 0:CH], 0.0).then_inc(zeroed, 1)
            pool.memset(s_vsh[:, :, :], 0.0).then_inc(zeroed, 1)
            pool.memset(ones[:, :], 1.0).then_inc(zeroed, 1)
            pool.memset(eps[:, 0:1], LN_EPS).then_inc(zeroed, 1)
            pool.memset(eps[:, 1:2], RMS_EPS).then_inc(zeroed, 1)
            affine = {}
            for i, name in ((1, ("gate", 0, 0)), (2, ("ba",)), (3, ("gate", 1, 0))):
                for t in range(NT):
                    affine[first_block[name] + 1 + t] = (i, t)
            for b in range(NB):
                split_lo(b)
                if b in affine:
                    i, t = affine[b]
                    n = 2 * (NT * (i - 1) + t)
                    full(pool, ("xT", i, KD - 1))
                    pool.wait_ge(s["ln_landed"], 32 * i)
                    pool.tensor_tensor(x_tm[:, t, :], x_tm[:, t, :], ln_rows[:, 0, :], ALU.mult)\
                        .then_inc(s["x_affine"], 1)
                    pool.wait_ge(s["x_affine"], n + 1)
                    pool.tensor_tensor(x_tm[:, t, :], x_tm[:, t, :], ln_rows[:, 1, :], ALU.add)\
                        .then_inc(s["x_affine"], 1)

        @block_.scalar
        def _(act):
            steps = [0]
            split = [0]

            def link(ins):
                steps[0] += 1
                ins.then_inc(s["act_step"], 1)
                act.wait_ge(s["act_step"], steps[0])

            def split_to(b):
                while split[0] <= min(b, NB - 1):
                    i = split[0]
                    n = blocks[i][2] * blocks[i][3]
                    act.wait_ge(w_landed[i % 2], 16 * (i // 2 + 1))
                    if i >= 2:
                        act.wait_ge(*block_end[i - 2])
                        act.wait_ge(w_lo_ready, i - 1)
                    act.activation(w_hi[:, i % 2, 0:n], w_raw[:, i % 2, 0:n], ACT.Copy).then_inc(w_hi_ready, 1)
                    split[0] += 1

            def round_x(i):
                for k in range(KD):
                    taken(act, ("xT", i, k))
                    act.activation(x_hi[:, k, :], f_a[:, k % 2, :], ACT.Copy).then_inc(s["x_hi_ready"], 1)

            def layer_norm(i):
                for t in range(NT):
                    act.wait_ge(s["ln_var"], NT * (i - 1) + t + 1)
                    link(act.activation(rstd[:, t:t + 1], mv[:, t, 1:2], ACT.Ln, bias=eps[:, 0:1]))
                    act.activation(rstd[:, t:t + 1], rstd[:, t:t + 1], ACT.Exp, scale=-0.5).then_inc(s["ln_stat"], 1)

            def round_o(layer, t):
                for i in range(2):
                    full(act, ("oT", layer, t, i))
                    act.activation(x_hi[:, 4 * i:4 * i + 4, tile_cols[t]], fm4(("oT", layer, t, i)),
                                   ACT.Copy).then_inc(s["o_hi_ready"], 1)

            def ffn(layer):
                for f in range(0, KF, 2):
                    b = first_block[("gate", layer, f)]
                    split_to(b + 1)
                    for j in range(2):
                        full(act, ("gate", layer, f + j))
                        if f:
                            taken(act, ("up", layer, f + j - 2))
                        take(act.activation(f_a[:, j, :], bank(("gate", layer, f + j))[:, :], ACT.Silu),
                             ("gate", layer, f + j))
                    split_to(b + 2)
                    for j in range(2):
                        taken(act, ("up", layer, f + j))
                        act.activation(h_hi[:, f + j, :], f_b[:, j, :], ACT.Copy).then_inc(s["h_hi_ready"], 1)
                    split_to(b + 3)

            def fm4(key):
                return bank(key)[:, :].rearrange("p (k n) -> p k n", k=4)

            act.wait_ge(zeroed, 8)
            split_to(0)
            round_x(0)
            split_to(first_block[("sq",)] + 1)
            for t in range(NT):
                full(act, ("skv", t))
                act.activation(s_v[:, t, :], bank(("skv", t))[:, KVH * HD:2 * KVH * HD], ACT.Copy)\
                   .then_inc(s["sv_copied"], 1)
            act.wait_ge(s["sv_copied"], NT)
            act.dma_start(s_vsh[CH:P, :, :], s_v[0:CH, :, :]).then_inc(s["sv_shifted"], 16)
            act.dma_start(s_vsh[0:CH, 1:NT, :], s_v[CH:P, 0:NT - 1, :]).then_inc(s["sv_shifted"], 16)
            split_to(first_block[("gk",)])
            for n in range(2):
                full(act, ("gq", n))
                take(act.activation(g_q[:, n, :], bank(("gq", n))[:, :], ACT.Copy, scale=GDK ** -0.5), ("gq", n))
            split_to(first_block[("ga",)])
            for n in range(2):
                full(act, ("gk", n))
                take(act.activation(g_k[:, n, :], bank(("gk", n))[:, :], ACT.Copy), ("gk", n))
            split_to(first_block[("gv",)])
            full(act, ("ga",))
            take(act.activation(g_ga[:, :], bank(("ga",))[0:GRANK, :], ACT.Copy), ("ga",))
            split_to(first_block[("gv",)] + 1)
            for t in range(NT):
                full(act, ("qT", t))
                take(act.activation(s_qT[:, :, tile_cols[t]], fm4(("qT", t)), ACT.Copy), ("qT", t))
                full(act, ("kT", t))
                take(act.activation(s_kT[:, :, CH + t * P:CH + (t + 1) * P], fm4(("kT", t)), ACT.Copy), ("kT", t))
            split_to(first_block[("gr",)])
            for t in range(NT):
                full(act, ("gv", t))
                take(act.activation(g_v[:, t, :], bank(("gv", t))[:, :], ACT.Copy), ("gv", t))
            split_to(first_block[("gr",)] + 1)
            act.wait_ge(s["a2_mid"], 2)
            link(act.activation(g_e[:, :, :], g_kd[:, :, :], ACT.Exp))
            act.activation(g_e[:, :, :], g_e[:, :, :], ACT.Ln, bias=1.0).then_inc(s["a2_exp"], 1)
            act.wait_ge(s["g_scan"], 2)
            act.activation(g_e[:, :, :], g_B[:, :, :], ACT.Exp, scale=1.0 / TAU).then_inc(s["g_exp"], 1)
            act.wait_ge(s["g_gate"], 1)
            act.activation(s_p[:, :, :], s_p[:, :, :], ACT.Exp, scale=1.0 / TAU).then_inc(s["g_exp"], 1)
            act.wait_ge(s["k_decayed"], 1)
            act.activation(s_p[:, :, :], g_B[:, :, :], ACT.Exp, scale=-1.0 / TAU).then_inc(s["g_exp"], 1)
            for t in range(NT):
                full(act, ("gr", t))
                take(act.activation(g_r[:, t, :], bank(("gr", t))[:, :], ACT.Silu), ("gr", t))
            split_to(first_block[("mix", 0, 0)] + 1)
            for t in range(NT):
                for g in range(KVH):
                    act.wait_ge(s["s_shift"], KVH * t + g + 1)
                    act.activation(s_snk[:, 4 * g:4 * g + 4], s_snk[:, 4 * g:4 * g + 4], ACT.Exp)
                    act.activation(s_p[:, g, :], s_p[:, g, :], ACT.Exp).then_inc(s["s_prob"], 1)
                full(act, ("kd", t))
                take(act.activation(g_kdt[:, :, :], bank(("kd", t))[:, 0:2 * P].rearrange("p (k n) -> p k n", k=2),
                                    ACT.Copy), ("kd", t))
                for g in range(KVH):
                    full(act, ("probT", t, g))
                    take(act.activation(s_pT[:, g, :], bank(("probT", t, g))[:, :], ACT.Copy), ("probT", t, g))
                act.wait_ge(s["o_var"], t + 1)
                link(act.activation(g_var[:, :], g_var[:, :], ACT.Ln, scale=1.0 / GDV, bias=eps[:, 0:1]))
                act.activation(g_var[:, :], g_var[:, :], ACT.Exp, scale=-0.5).then_inc(s["o_rstd"], 1)
                if t:
                    round_o(0, t - 1)
            round_o(0, NT - 1)
            split_to(first_block[("mix", 0, 1)])
            full(act, ("mix", 0, 0, 0))
            split_to(first_block[("gate", 0, 0)])
            layer_norm(1)
            round_x(1)
            ffn(0)
            split_to(first_block[("ba",)])
            layer_norm(2)
            round_x(2)
            split_to(first_block[("ba",)] + 2)
            act.wait_ge(s["ba_mid"], 1)
            act.activation(beta[:, :, :], ba[:, :, 0:GDN_H], ACT.Exp, scale=-1.0)
            link(act.activation(g_tmp[:, :, :], g_tmp[:, :, :], ACT.Exp))
            act.activation(g_tmp[:, :, :], g_tmp[:, :, :], ACT.Ln, bias=1.0)
            act.activation(a_log[:, :], a_log[:, :], ACT.Exp).then_inc(s["ba_exp"], 1)

            def silu_conv(i):
                n = CONV_ORDER[i]
                taken(act, ("conv", n))
                act.activation(qkv[:, n, :], conv_acc(i), ACT.Silu).then_inc(s["conv_silu"], 1)
                if n < 2 * KD:
                    act.wait_ge(s["conv_silu"], i + 1)
                    if i >= 2:
                        full(act, ("norm", CONV_ORDER[i - 2]))
                    act.activation(conv_squares(i), qkv[:, n, :], ACT.Square).then_inc(s["conv_sq"], 1)

            for i, n in enumerate(CONV_ORDER):
                split_to(first_block[("conv", n - n % 2)] + 1)
                full(act, ("conv", n))
                act.activation(conv_acc(i), bank(("conv", n))[:, :], ACT.Copy,
                               scale=convw[:, 9 * KD + n:9 * KD + n + 1]).then_inc(s["conv_raw"], 1)
                if i:
                    silu_conv(i - 1)
                if i == 6:
                    act.wait_ge(s["dec_ready"], 1)
                    act.activation(to_end[:, :, :], to_end[:, :, :], ACT.Exp)
                    act.activation(bexp[:, :, :], dec[:, 0, :, :], ACT.Exp).then_inc(s["dec_exp"], 1)
            silu_conv(len(CONV_ORDER) - 1)
            split_to(first_block[("og", 0)] + 1)
            for half in range(2):
                split_to(first_block[("og", half)] + 2)
                for t in range(NT):
                    full(act, ("og", half, t))
                    take(act.activation(gate_s[:, t, half * 512:(half + 1) * 512], bank(("og", half, t))[:, :],
                                        ACT.Silu), ("og", half, t))
                split_to(first_block[("og", half)] + 3)
            taken(act, ("norm", CONV_ORDER[2 * KD - 1]))
            link(act.activation(nrm[:, :, :], nrm[:, :, :], ACT.Ln, bias=eps[:, 1:2]))
            act.activation(nrm[:, :, :], nrm[:, :, :], ACT.Exp, scale=-0.5).then_inc(s["rn_ready"], 1)
            for t in range(NT):
                for hg in range(2):
                    full(act, ("drow", t, hg))
                    act.activation(EE[:, hsl[hg], :], fm4(("drow", t, hg)), ACT.Exp).then_inc(s["e_ready"], 1)
                if t:
                    round_o(1, t - 1)
                for hg in range(2):
                    act.wait_ge(s["arg_ready"], 2 * t + hg + 1)
                    act.activation(GT[:, hsl[hg], :], GT[:, hsl[hg], :], ACT.Exp)
                    act.activation(GA[:, hsl[hg], :], GA[:, hsl[hg], :], ACT.Exp, scale=-1.0)\
                       .then_inc(s["gam_ready"], 1)
                for hg in range(2):
                    full(act, ("khT", t, hg))
                    take(act.activation(qkv[:, KD + 4 * hg:KD + 4 * hg + 4, tile_cols[t]], fm4(("khT", t, hg)),
                                        ACT.Copy), ("khT", t, hg))
                for hg in range(2):
                    full(act, ("s0", t, hg))
                    take(act.activation(SS[:, hsl[hg], :], fm4(("s0", t, hg)), ACT.Copy), ("s0", t, hg))
                for lv in LEVELS[1:]:
                    for hg in range(2):
                        full(act, ("m1", t, lv, hg))
                        take(act.activation(M1[:, hsl[hg], :], fm4(("m1", t, lv, hg)), ACT.Copy), ("m1", t, lv, hg))
                for name, dst in (("u", GU), ("w", TT)):
                    for hg in range(2):
                        full(act, (name, t, hg))
                        take(act.activation(dst[:, hsl[hg], :], fm4((name, t, hg)), ACT.Copy), (name, t, hg))
                for hg in range(2):
                    act.wait_ge(s["ov_ready"], 2 * t + hg + 1)
                    link(act.activation(oms[:, hsl[hg]], oms[:, hsl[hg]], ACT.Ln, scale=1.0 / P, bias=eps[:, 1:2]))
                    act.activation(oms[:, hsl[hg]], oms[:, hsl[hg]], ACT.Exp, scale=-0.5).then_inc(s["or_ready"], 1)
            round_o(1, NT - 1)
            split_to(first_block[("mix", 1, 1)])
            full(act, ("mix", 1, 0, 0))
            split_to(first_block[("gate", 1, 0)])
            layer_norm(3)
            round_x(3)
            ffn(1)
            split_to(NB - 1)
            layer_norm(4)

        @block_.vector
        def _(dve):
            steps = [0]

            def link(ins):
                steps[0] += 1
                ins.then_inc(s["dve_step"], 1)
                dve.wait_ge(s["dve_step"], steps[0])

            def k4(key):
                return bank(key)[:, :].rearrange("p (k n) -> p k n", k=4)

            def across(col, n):
                return col.unsqueeze(2).broadcast_to([col.shape[0], col.shape[1], n])

            def over_heads(mat, heads):
                return mat.unsqueeze(1).broadcast_to([mat.shape[0], heads, mat.shape[1]])

            def round_x(i):
                gcol = 32 * ((i + 1) % 2) + 8 * ((i - 1) // 2)

                def low(k):
                    dve.wait_ge(s["x_hi_ready"], KD * i + k + 1)
                    dve.tensor_tensor(x_lo[:, k, :], f_a[:, k % 2, :], x_hi[:, k, :].bitcast(F32), ALU.subtract)\
                       .then_inc(s["x_lo_ready"], 1)

                for k in range(KD):
                    full(dve, ("xT", i, k))
                    src = bank(("xT", i, k))[:, :]
                    if i == 0:
                        take(dve.tensor_copy(f_a[:, k % 2, :], src), ("xT", i, k))
                    else:
                        take(dve.tensor_scalar(f_a[:, k % 2, :], src, lnc[:, gcol + k:gcol + k + 1],
                                               lnc[:, gcol + 16 + k:gcol + 17 + k], ALU.mult, ALU.add), ("xT", i, k))
                    if k:
                        low(k - 1)
                low(KD - 1)

            def round_o(layer, t):
                for i in range(2):
                    dve.wait_ge(s["o_hi_ready"], 2 * (NT * layer + t) + i + 1)
                    cols = x_hi[:, 4 * i:4 * i + 4, tile_cols[t]].bitcast(F32)
                    take(dve.tensor_tensor(x_lo[:, 4 * i:4 * i + 4, tile_cols[t]], k4(("oT", layer, t, i)), cols,
                                           ALU.subtract), ("oT", layer, t, i))

            def layer_norm(i, group, layer):
                def normalise(t):
                    dve.wait_ge(s["ln_stat"], NT * (i - 1) + t + 1)
                    dve.tensor_scalar(x_tm[:, t, :], x_tm[:, t, :], mv[:, t, 0:1], rstd[:, t:t + 1],
                                      ALU.subtract, ALU.mult).then_inc(s["z_norm"], 1)

                for half in range(2):
                    for t in range(NT):
                        key = (group, layer, half, t)
                        if i > 1:
                            dve.wait_ge(s["x_affine"], 2 * NT * (i - 2) + 2 * (t + 1))
                        full(dve, key)
                        cols = x_tm[:, t, half * 512:(half + 1) * 512]
                        take(dve.scalar_tensor_tensor(cols, cols, ALPHA, bank(key)[:, :], ALU.mult, ALU.add), key)
                        if half:
                            taken(dve, key)
                            for j in range(2):
                                ins = dve.bn_stats(stats[:, t, j, :], x_tm[:, t, j * 512:(j + 1) * 512])
                            link(ins)
                            dve.bn_aggr(mv[:, t, :], stats[:, t, :, :].rearrange("p a b -> p (a b)"))\
                               .then_inc(s["ln_var"], 1)
                            if t:
                                normalise(t - 1)
                normalise(NT - 1)

            def ffn(layer):
                for f in range(KF):
                    n = layer * KF + f
                    taken(dve, ("gate", layer, f))
                    full(dve, ("up", layer, f))
                    take(dve.tensor_tensor(f_b[:, f % 2, :], bank(("up", layer, f))[:, :], f_a[:, f % 2, :],
                                           ALU.mult), ("up", layer, f))
                    dve.wait_ge(s["h_hi_ready"], n + 1)
                    dve.tensor_tensor(h_lo[:, f, :], f_b[:, f % 2, :], h_hi[:, f, :].bitcast(F32), ALU.subtract)\
                       .then_inc(s["h_lo_ready"], 1)

            for i, (dst, n) in enumerate(((lnc, 66), (convw, 96))):
                full(dve, ("const", i))
                take(dve.tensor_copy(dst[:, 0:n], bank(("const", i))[:, 0:n]), ("const", i))
            round_x(0)
            dve.wait_ge(s["x_lo_ready"], KD)
            dve.memset(k_pad[:, :, :, :].rearrange("p a b c -> p (a b c)"), 0.0).then_inc(zeroed, 1)
            dve.wait_ge(zeroed, 9)
            dve.wait_ge(consts, 16 * N_CONST)

            def rotate(src, dst, t, heads):
                cos = over_heads(rope[:, t, 0, :], heads)
                sin = over_heads(rope[:, t, 1, :], heads)
                a, b, c, d = (r_tmp[:, i, 0:heads, :] for i in range(4))
                dve.tensor_tensor(a, src[:, :, 0:RH], cos, ALU.mult)
                dve.tensor_tensor(b, src[:, :, RH:HD], sin, ALU.mult)
                dve.tensor_tensor(c, src[:, :, RH:HD], cos, ALU.mult)
                link(dve.tensor_tensor(d, src[:, :, 0:RH], sin, ALU.mult))
                dve.tensor_tensor(dst[:, :, 0:RH], a, b, ALU.subtract)
                return dve.tensor_tensor(dst[:, :, RH:HD], c, d, ALU.add)

            for t in range(NT):
                dve.wait_ge(s["sv_copied"], t + 1)
                even = k_pad[:, t, :, :].rearrange("p (g e) c -> p g e c", e=2)
                src = bank(("skv", t))[:, 0:KVH * HD].rearrange("p (h d) -> p h d", h=KVH)
                last = rotate(src, even[:, :, 0, 0:HD], t, KVH)
                take(last, ("skv", t))
                taken(dve, ("skv", t))
                dve.tensor_copy(even[:, :, 1, HD:P], even[:, :, 0, 0:HD]).then_inc(s["k_rotated"], 1)
            for t in range(NT):
                full(dve, ("sq", t))
                dst = q_rot[:, t, :].rearrange("p (h d) -> p h d", h=QH)
                take(rotate(bank(("sq", t))[:, :].rearrange("p (h d) -> p h d", h=QH), dst, t, QH), ("sq", t))
            for n in range(2):
                full(dve, ("a2", n))
                take(dve.tensor_scalar(g_B[:, n, :], bank(("a2", n))[:, :], lnc[:, 64 + n:65 + n], None, ALU.add),
                     ("a2", n))
                taken(dve, ("a2", n))
                dve.scalar_tensor_tensor(g_kd[:, n, :], g_B[:, n, :], -1.0, g_B[:, n, :], ALU.mult, ALU.min)\
                   .then_inc(s["a2_mid"], 1)
            dve.wait_ge(s["a2_exp"], 1)
            link(dve.scalar_tensor_tensor(g_kd[:, :, :], g_B[:, :, :], 0.0, g_e[:, :, :], ALU.min, ALU.subtract))
            for n in range(2):
                dve.tensor_tensor_scan(g_B[:, n, :], g_keep[:, :], g_kd[:, n, :], 0.0, ALU.mult, ALU.add)\
                   .then_inc(s["g_scan"], 1)
            dve.wait_ge(s["g_scan"], 2)
            full(dve, ("kT", NT - 1))
            for n in range(2):
                bv = g_B[:, n, :].rearrange("p (c l) -> p c l", l=CH)
                ins = dve.tensor_tensor(s_p[:, n, :].rearrange("p (c l) -> p c l", l=CH),
                                        bv[:, :, CH - 1:CH].broadcast_to([P, NC, CH]), bv, ALU.subtract)
            ins.then_inc(s["g_gate"], 1)
            dve.wait_ge(s["g_exp"], 1)
            taken(dve, ("gq", 1))
            for e in range(2):
                rows = slice(e * GDK, (e + 1) * GDK)
                dve.tensor_tensor(q_pad[rows, e:GH:2, :], g_q[rows, :, :], g_e[rows, :, :], ALU.mult)\
                   .then_inc(s["q_gated"], 1)
            dve.wait_ge(s["g_exp"], 2)
            taken(dve, ("gk", 1))
            dve.tensor_tensor(g_kd[:, :, :], g_k[:, :, :], s_p[:, :, :], ALU.mult).then_inc(s["k_decayed"], 1)
            dve.wait_ge(s["g_exp"], 3)
            dve.tensor_tensor(g_k[:, :, :], g_k[:, :, :], s_p[:, :, :], ALU.mult).then_inc(s["k_gated"], 1)

            def heads4(ap):
                return ap.rearrange("p (h n) -> p h n", h=4)

            for t in range(NT):
                for g in range(KVH):
                    key = ("score", t, g)
                    hs = slice(4 * g, 4 * g + 4)
                    full(dve, key)
                    if t == 0:
                        link(dve.memset(k4(key)[0:CH, :, 0:CH], NEG))
                    link(dve.tensor_reduce(s_max[:, hs], k4(key), AX, ALU.max))
                    link(dve.scalar_tensor_tensor(s_max[:, hs], s_max[:, hs], HD ** -0.5, sinks[:, hs],
                                                  ALU.mult, ALU.max))
                    take(dve.scalar_tensor_tensor(heads4(s_p[:, g, :]), k4(key), HD ** -0.5,
                                                  across(s_max[:, hs], P), ALU.mult, ALU.subtract), key)
                    dve.tensor_tensor(s_snk[:, hs], sinks[:, hs], s_max[:, hs], ALU.subtract)\
                       .then_inc(s["s_shift"], 1)
                full(dve, ("gattn", t))
                take(dve.copy_predicated(g_at[:, :, :], over_heads(upto[:, :].bitcast(I32), GH), k4(("gattn", t))),
                     ("gattn", t))
                for c in range(2):
                    key = ("gstate", t, c)
                    full(dve, key)
                    v = 2 * t + c
                    for h in range(GH):
                        rows = slice((h % 2) * GDK, (h % 2 + 1) * GDK)
                        col = (2 * t + c + 1) * CH - 1
                        ins = dve.scalar_tensor_tensor(
                            g_S[rows, (v + 1) % 2, h // 2, :], g_S[rows, v % 2, h // 2, :],
                            g_e[rows, h // 2, col:col + 1], bank(key)[rows, h * GDV:(h + 1) * GDV],
                            ALU.mult, ALU.add)
                    take(ins, key)
                    taken(dve, key)
                for g in range(KVH):
                    hs = slice(4 * g, 4 * g + 4)
                    dve.wait_ge(s["s_prob"], KVH * t + g + 1)
                    link(dve.tensor_reduce(s_den[:, hs], heads4(s_p[:, g, :]), AX, ALU.add))
                link(dve.tensor_tensor(s_den[:, :], s_den[:, :], s_snk[:, :], ALU.add))
                link(dve.reciprocal(s_den[:, :], s_den[:, :]))
                taken(dve, ("gr", t))
                dve.tensor_tensor(g_r[:, t, :], g_r[:, t, :], g_norm[:, :], ALU.mult)
                key = ("gout", t)
                full(dve, key)
                og = heads4(o_tm[:, t % 2, 0:512])
                link(dve.tensor_reduce(g_mu[:, :], k4(key), AX, ALU.add))
                link(dve.tensor_scalar(g_mu[:, :], g_mu[:, :], 1.0 / GDV, None, ALU.mult))
                take(dve.tensor_tensor(og, k4(key), across(g_mu[:, :], GDV), ALU.subtract), key)
                taken(dve, key)
                sq = r_tmp[:, 0:2, :, :].rearrange("p a b c -> p (a b c)")
                link(dve.tensor_tensor(sq, o_tm[:, t % 2, 0:512], o_tm[:, t % 2, 0:512], ALU.mult))
                dve.tensor_reduce(g_var[:, :], heads4(sq), AX, ALU.add).then_inc(s["o_var"], 1)
                dve.wait_ge(s["o_rstd"], t + 1)
                link(dve.tensor_tensor(og, og, across(g_var[:, :], GDV), ALU.mult))
                dve.tensor_tensor(o_tm[:, t % 2, 0:512], o_tm[:, t % 2, 0:512], g_r[:, t, :], ALU.mult)\
                   .then_inc(s["o_even"], 1)
                key = ("sout", t)
                full(dve, key)
                take(dve.tensor_tensor(o_tm[:, t % 2, 512:D].rearrange("p (h n) -> p h n", h=QH),
                                       bank(key)[:, :].rearrange("p (h n) -> p h n", h=QH),
                                       across(s_den[:, :], HD), ALU.mult), key)
                if t:
                    round_o(0, t - 1)
            round_o(0, NT - 1)
            layer_norm(1, "mix", 0)
            round_x(1)
            ffn(0)
            layer_norm(2, "down", 0)
            round_x(2)
            dve.wait_ge(s["x_lo_ready"], 3 * KD)
            dve.memset(ST[:, :, :].rearrange("p a b -> p (a b)"), 0.0).then_inc(s["state0"], 1)
            full(dve, ("ba",))
            take(dve.tensor_copy(ba[:, :, :], bank(("ba",))[:, 0:NT * 2 * GDN_H].rearrange("p (t c) -> p t c", t=NT)),
                 ("ba",))
            taken(dve, ("ba",))
            link(dve.tensor_tensor(gdec[:, :, :], ba[:, :, GDN_H:], over_heads(dt_bias[:, :], NT), ALU.add))
            dve.scalar_tensor_tensor(g_tmp[:, :, :], gdec[:, :, :], -1.0, gdec[:, :, :], ALU.mult, ALU.min)\
               .then_inc(s["ba_mid"], 1)
            dve.wait_ge(s["ba_exp"], 1)
            link(dve.tensor_scalar(beta[:, :, :], beta[:, :, :], 1.0, None, ALU.add))
            link(dve.reciprocal(beta[:, :, :], beta[:, :, :]))
            link(dve.scalar_tensor_tensor(gdec[:, :, :], gdec[:, :, :], 0.0, g_tmp[:, :, :], ALU.max, ALU.add))
            dve.scalar_tensor_tensor(gdec[:, :, :], gdec[:, :, :], -1.0, over_heads(a_log[:, :], NT),
                                     ALU.mult, ALU.mult).then_inc(s["g_ready"], 1)
            for i, n in enumerate(CONV_ORDER):
                key = ("conv", n)
                dve.wait_ge(s["conv_raw"], i + 1)
                full(dve, key)
                for back in range(1, CONV_K):
                    tap = (CONV_K - 1 - back) * 3 * KD + n
                    dst = conv_acc(i)[:, back:]
                    ins = dve.scalar_tensor_tensor(dst, bank(key)[:, 0:SEQ - back], convw[:, tap:tap + 1], dst,
                                                   ALU.mult, ALU.add)
                    if back < CONV_K - 1:
                        link(ins)
                take(ins, key)
                if i == 3:
                    full(dve, ("decay",))
                    take(dve.tensor_copy(dec[:, :, :, :].rearrange("p a t h -> p (a t h)"),
                                         bank(("decay",))[:, 0:2 * TH]), ("decay",))
                    taken(dve, ("decay",))
                    dve.tensor_tensor(to_end[:, :, :], dec[:, 1, :, :], dec[:, 0, :, :], ALU.subtract)\
                       .then_inc(s["dec_ready"], 1)
                if i >= 3 and CONV_ORDER[i - 3] < 2 * KD:
                    m = CONV_ORDER[i - 3]
                    full(dve, ("norm", m))
                    take(dve.tensor_copy(nrm[:, m, :], bank(("norm", m))[:, 0:NT]), ("norm", m))
            dve.wait_ge(s["dec_exp"], 1)
            link(dve.tensor_tensor(bexp[:, :, :], bexp[:, :, :], beta[:, :, :], ALU.mult))
            for half in range(2):
                for t in range(NT):
                    taken(dve, ("og", half, t))
                    gs = heads4(gate_s[:, t, half * 512:(half + 1) * 512])
                    ins = dve.tensor_tensor(gs, gs, over_heads(onorm_row[:, :], 4), ALU.mult)
            link(ins)
            dve.wait_ge(s["rn_ready"], 1)
            link(dve.tensor_scalar(nrm[:, 0:GDN_H, :], nrm[:, 0:GDN_H, :], float(P) ** -0.5, None, ALU.mult))

            def out_scale(t):
                for hg in range(2):
                    dve.wait_ge(s["or_ready"], 2 * t + hg + 1)
                    m = M1[:, hsl[hg], :]
                    link(dve.tensor_tensor(m, m, across(oms[:, hsl[hg]], P), ALU.mult))
                    dve.tensor_tensor(m, m, heads4(gate_s[:, t, hg * 512:(hg + 1) * 512]), ALU.mult)\
                       .then_inc(s["o_odd"], 1)

            dve.wait_ge(s["x_affine"], 4 * NT)
            for t in range(NT):
                H = range(2)
                for hg in H:
                    hs = hsl[hg]
                    dve.tensor_tensor(GU[:, hs, :], over_heads(upto[:, :], 4), across(gdec[:, t, hs], P), ALU.mult)\
                       .then_inc(s["gu_ready"], 1)
                for hg in H:
                    full(dve, ("kTM", t, hg))
                    rk = nrm[:, KD + 4 * hg:KD + 4 * hg + 4, t]
                    take(dve.tensor_tensor(KH[:, hsl[hg], :], k4(("kTM", t, hg)), across(rk, P), ALU.mult),
                         ("kTM", t, hg))
                for hg in H:
                    full(dve, ("vTM", t, hg))
                    take(dve.tensor_tensor(qkv[:, 2 * KD + 4 * hg:2 * KD + 4 * hg + 4, tile_cols[t]],
                                           k4(("vTM", t, hg)), across(beta[:, t, hsl[hg]], P), ALU.mult),
                         ("vTM", t, hg))
                if t:
                    out_scale(t - 1)
                for hg in H:
                    hs = hsl[hg]
                    dve.wait_ge(s["e_ready"], 2 * t + hg + 1)
                    take(dve.tensor_tensor(GU[:, hs, :], k4(("drow", t, hg)), across(dec[:, 0, t, hs], P),
                                           ALU.subtract), ("drow", t, hg))
                    taken(dve, ("drow", t, hg))
                    dve.tensor_tensor(GT[:, hs, :], GU[:, hs, :], over_heads(o_negt[:, :], 4), ALU.add)
                    dve.tensor_tensor(GA[:, hs, :], GU[:, hs, :], over_heads(o_posl[:, :], 4), ALU.add)\
                       .then_inc(s["arg_ready"], 1)
                if t:
                    round_o(1, t - 1)
                dve.tensor_copy(edl[:, :, :], EE[:, :, CH - 1:P:CH])
                for hg in H:
                    hs = hsl[hg]
                    full(dve, ("gram", t, hg))
                    dve.wait_ge(s["gam_ready"], 2 * t + hg + 1)
                    take(dve.tensor_tensor(GA[:, hs, :], k4(("gram", t, hg)), GA[:, hs, :], ALU.mult),
                         ("gram", t, hg))
                    taken(dve, ("gram", t, hg))
                    link(dve.tensor_tensor(GA[:, hs, :], GA[:, hs, :], across(beta[:, t, hs], P), ALU.mult))

                def level(l, hg):
                    cs = [P, 4, 2, CH]
                    a = GA[:, hsl[hg], :].rearrange("p h (c l) -> p h c l", l=CH)
                    m = o_lvl[:, l, :].unsqueeze(1).unsqueeze(1).broadcast_to(cs)
                    return dve.tensor_tensor(KB[:, hsl[hg], :].rearrange("p h (c l) -> p h c l", l=CH), a, m, ALU.mult)

                for hg in H:
                    link(level(0, hg))
                    dve.tensor_tensor(TT[:, hsl[hg], :], over_heads(eye[:, :], 4), KB[:, hsl[hg], :], ALU.subtract)\
                       .then_inc(s["t0_ready"], 1)
                for hg in H:
                    full(dve, ("qk", t, hg))
                    take(dve.tensor_tensor(GT[:, hsl[hg], :], k4(("qk", t, hg)), GT[:, hsl[hg], :], ALU.mult),
                         ("qk", t, hg))
                    q = qkv[:, 4 * hg:4 * hg + 4, tile_cols[t]]
                    dve.tensor_tensor(q, q, EE[:, hsl[hg], :], ALU.mult).then_inc(s["q_decayed"], 1)
                for l, lv in enumerate(LEVELS[1:], 1):
                    for hg in H:
                        level(l, hg).then_inc(s["ab_ready"], 1)
                    for hg in H:
                        key = ("ds", t, lv, hg)
                        full(dve, key)
                        take(dve.tensor_tensor(SS[:, hsl[hg], :], SS[:, hsl[hg], :], k4(key), ALU.subtract), key)
                    if lv < LEVELS[-1]:
                        for hg in H:
                            key = ("dt", t, lv, hg)
                            full(dve, key)
                            take(dve.tensor_tensor(TT[:, hsl[hg], :], TT[:, hsl[hg], :], k4(key), ALU.subtract), key)
                for hg in H:
                    hs = hsl[hg]
                    dve.tensor_tensor(KB[:, hs, :], KH[:, hs, :], across(bexp[:, t, hs], P), ALU.mult)\
                       .then_inc(s["kb_ready"], 1)
                for hg in H:
                    hs = hsl[hg]
                    dve.tensor_tensor(KH[:, hs, :], KH[:, hs, :], across(to_end[:, t, hs], P), ALU.mult)\
                       .then_inc(s["kd_ready"], 1)
                for c in range(2):
                    rows = slice(c * CH, (c + 1) * CH)
                    old, new = (ST, GA) if c == 0 else (GA, ST)
                    for hg in H:
                        key = ("ws", t, c, hg)
                        full(dve, key)
                        taken(dve, ("u", t, hg))
                        take(dve.tensor_tensor(EE[rows, hsl[hg], :], GU[rows, hsl[hg], :], k4(key)[rows],
                                               ALU.subtract), key)
                    for hg in H:
                        key = ("kv", t, c, hg)
                        full(dve, key)
                        for h in range(4 * hg, 4 * hg + 4):
                            ins = dve.scalar_tensor_tensor(new[:, h, :], old[:, h, :], edl[:, h, c:c + 1],
                                                           k4(key)[:, h % 4, :], ALU.mult, ALU.add)
                        take(ins, key)
                        taken(dve, key)
                for hg in H:
                    key = ("o", t, hg)
                    full(dve, key)
                    m = M1[:, hsl[hg], :]
                    take(dve.tensor_tensor(m, k4(key), across(nrm[:, 4 * hg:4 * hg + 4, t], P), ALU.mult), key)
                    taken(dve, key)
                    link(dve.tensor_tensor(SS[:, hsl[hg], :], m, m, ALU.mult))
                    dve.tensor_reduce(oms[:, hsl[hg]], SS[:, hsl[hg], :], AX, ALU.add).then_inc(s["ov_ready"], 1)
            out_scale(NT - 1)
            round_o(1, NT - 1)
            layer_norm(3, "mix", 1)
            round_x(3)
            ffn(1)
            layer_norm(4, "down", 1)
            for t in range(NT):
                dve.wait_ge(s["z_norm"], NT * 3 + t + 1)
                dve.wait_ge(s["ln_landed"], 32 * 4)
                n = 2 * (NT * 3 + t)
                dve.tensor_tensor(x_tm[:, t, :], x_tm[:, t, :], ln_rows[:, 0, :], ALU.mult)\
                   .then_inc(s["x_affine"], 1)
                dve.wait_ge(s["x_affine"], n + 1)
                dve.tensor_tensor(x_tm[:, t, :], x_tm[:, t, :], ln_rows[:, 1, :], ALU.add)\
                   .then_inc(s["x_affine"], 1)

        @block_.tensor
        def _(pe):
            def fill(key):
                u = unit[key]
                if u >= 8:
                    pe.wait_ge(bank_taken[u % 8], u // 8)
                return bank(key)

            def done(ins, key):
                ins.then_inc(bank_full[unit[key] % 8], 1)

            def mm3(out_ap, st, mv_, start, stop):
                pe.matmul(out_ap, st[0], mv_[0], start=start, stop=False)
                pe.matmul(out_ap, st[0], mv_[1], start=False, stop=False)
                return pe.matmul(out_ap, st[1], mv_[0], start=False, stop=stop)

            def weights(b, kk, c0, width):
                n = blocks[b][3]
                at_ = kk * n + c0
                return tuple(w[:, b % 2, at_:at_ + width] for w in (w_hi, w_lo))

            def xcols(k, cols):
                return x_hi[:, k, cols], x_lo[:, k, cols]

            def hcols(k, cols):
                return h_hi[:, k, cols], h_lo[:, k, cols]

            ALL = slice(0, SEQ)

            def fm_block(b, keys, fresh=None, width=P):
                pe.wait_ge(w_lo_ready, b + 1)
                for n, key in enumerate(keys):
                    ps = fill(key)
                    for k in range(KD):
                        if fresh is not None and n == 0:
                            pe.wait_ge(s["x_lo_ready"], KD * fresh + k + 1)
                        ins = mm3(ps[:, :], weights(b, k, n * P, P), xcols(k, ALL), k == 0, k == KD - 1)
                    done(ins, key)

            def tm_group(name, wait_k, src=xcols, kt=KD):
                b = first_block[name]
                while b < NB and blocks[b][0] == name:
                    _, k0, nk, width, _v = blocks[b]
                    pe.wait_ge(w_lo_ready, b + 1)
                    for kk in range(nk):
                        wait_k(k0 + kk)
                        for t in range(NT):
                            key = (*name, t)
                            ps = fill(key) if k0 + kk == 0 else bank(key)
                            ins = mm3(ps[:, 0:width], src(k0 + kk, tile_cols[t]), weights(b, kk, 0, width),
                                      k0 + kk == 0, k0 + kk == kt - 1)
                            if k0 + kk == kt - 1:
                                done(ins, key)
                    if k0 + nk < kt:
                        ins.then_inc(w_used, 1)
                    b += 1

            def no_wait(k):
                pass

            def turn_x(i):
                if i == 0:
                    pe.wait_ge(s["x_landed"], 32)
                else:
                    pe.wait_ge(s["z_norm"], NT * i)
                for k in range(KD):
                    ps = fill(("xT", i, k))
                    for t in range(NT):
                        ins = pe.transpose(ps[:, tile_cols[t]], x_tm[:, t, k * P:(k + 1) * P], eye[:, :])
                    done(ins, ("xT", i, k))

            def turn_o(layer, t):
                for i in range(2):
                    if layer == 0:
                        pe.wait_ge(s["o_even"], t + 1)
                        taken(pe, ("sout", t))
                    else:
                        pe.wait_ge(s["o_odd"], 2 * t + i + 1)
                    ps = fill(("oT", layer, t, i))
                    for j in range(4):
                        k = 4 * i + j
                        src = o_tm[:, t % 2, k * P:(k + 1) * P] if layer == 0 else M1[:, k, :]
                        ins = pe.transpose(ps[:, j * P:(j + 1) * P], src, eye[:, :])
                    done(ins, ("oT", layer, t, i))

            def mix_and_norm(layer):
                def have(k):
                    taken(pe, ("oT", layer, NT - 1, k // 4))
                for half in range(2):
                    tm_group(("mix", layer, half), have)
                turn_x(2 * layer + 1)

            def ffn(layer):
                for f in range(0, KF, 2):
                    fresh = 2 * layer + 1 if f == 0 else None
                    b = first_block[("gate", layer, f)]
                    fm_block(b, [("gate", layer, f), ("gate", layer, f + 1)], fresh)
                    fm_block(b + 1, [("up", layer, f), ("up", layer, f + 1)])

                def have(k):
                    pe.wait_ge(s["h_lo_ready"], layer * KF + k + 1)
                for half in range(2):
                    tm_group(("down", layer, half), have, hcols, KF)

            pe.wait_ge(consts, 16 * N_CONST)
            pe.wait_ge(s["x_landed"], 32)
            for i, (src, n) in enumerate(((vec_rows, 66), (conv_rows, 96))):
                ps = fill(("const", i))
                done(pe.transpose(ps[:, 0:n], src[0:n, :], eye[0:n, 0:n]), ("const", i))
            turn_x(0)
            tm_group(("skv",), lambda k: pe.wait_ge(s["x_lo_ready"], k + 1))
            tm_group(("sq",), no_wait)
            fm_block(first_block[("gq",)], [("gq", 0), ("gq", 1)])
            fm_block(first_block[("gk",)], [("gk", 0), ("gk", 1)])
            fm_block(first_block[("ga",)], [("ga",)])
            for t in range(NT):
                ps = fill(("qT", t))
                taken(pe, ("sq", t))
                for j in range(4):
                    ins = pe.transpose(ps[:, j * P:(j + 1) * P], q_rot[:, t, j * P:(j + 1) * P], eye[:, :])
                done(ins, ("qT", t))
                ps = fill(("kT", t))
                pe.wait_ge(s["k_rotated"], t + 1)
                for j in range(4):
                    ins = pe.transpose(ps[:, j * P:(j + 1) * P], k_pad[:, t, j, :], eye[:, :])
                done(ins, ("kT", t))
            tm_group(("gv",), no_wait)
            taken(pe, ("ga",))
            for n in range(2):
                ps = fill(("a2", n))
                done(pe.matmul(ps[:, :], g_a2[:, n * P:(n + 1) * P], g_ga[:, :], start=True, stop=True), ("a2", n))
            tm_group(("gr",), no_wait)
            pe.wait_ge(s["k_gated"], 1)
            pe.wait_ge(s["k_decayed"], 1)
            pe.wait_ge(s["q_gated"], 2)
            pe.wait_ge(s["sv_shifted"], 32)
            taken(pe, ("kT", NT - 1))
            taken(pe, ("qT", NT - 1))
            taken(pe, ("gv", NT - 1))

            def across_chunks(t, c, ps, start):
                rows = slice(c * CH, (c + 1) * CH)
                cols = slice(t * P + c * CH, t * P + (c + 1) * CH)
                for h in range(GH):
                    pe.matmul(ps[rows, h * GDV:(h + 1) * GDV], q_pad[:, h, cols], g_S[:, c, h // 2, :],
                              start=h == 0, stop=False, skip_group_check=True)

            def chunk_state(t, c):
                rows = slice(c * CH, (c + 1) * CH)
                ps = fill(("gstate", t, c))
                for h in range(GH):
                    ins = pe.matmul(ps[:, h * GDV:(h + 1) * GDV], g_kdt[rows, h // 2, :],
                                    g_v[rows, t, h * GDV:(h + 1) * GDV], start=True, stop=True)
                done(ins, ("gstate", t, c))

            for t in range(NT):
                for g in range(KVH):
                    ps = fill(("score", t, g))
                    for hh in range(4):
                        h = 4 * g + hh
                        for c in range(2):
                            chunk = 2 * t + c
                            ins = pe.matmul(ps[c * CH:(c + 1) * CH, hh * P:(hh + 1) * P],
                                            s_qT[:, h // 2, chunk * CH:(chunk + 1) * CH],
                                            s_kT[:, 2 * g + h % 2, chunk * CH:chunk * CH + 2 * CH],
                                            start=True, stop=True)
                    done(ins, ("score", t, g))
                ps = fill(("kd", t))
                for n in range(2):
                    ins = pe.transpose(ps[:, n * P:(n + 1) * P], g_kd[:, n, tile_cols[t]], eye[:, :])
                done(ins, ("kd", t))
                ps = fill(("gattn", t))
                for h in range(GH):
                    ins = pe.matmul(ps[:, h * P:(h + 1) * P], g_k[:, h // 2, tile_cols[t]],
                                    q_pad[:, h, tile_cols[t]], start=True, stop=True)
                done(ins, ("gattn", t))
                taken(pe, ("kd", t))
                chunk_state(t, 0)
                go = fill(("gout", t))
                if t:
                    taken(pe, ("gstate", t - 1, 1))
                across_chunks(t, 0, go, True)
                chunk_state(t, 1)
                taken(pe, ("gstate", t, 0))
                across_chunks(t, 1, go, True)
                taken(pe, ("gattn", t))
                for h in range(GH):
                    ins = pe.matmul(go[:, h * GDV:(h + 1) * GDV], g_at[:, h, :], g_v[:, t, h * GDV:(h + 1) * GDV],
                                    start=False, stop=h == GH - 1, skip_group_check=True)
                done(ins, ("gout", t))
                for g in range(KVH):
                    pe.wait_ge(s["s_prob"], KVH * t + g + 1)
                    ps = fill(("probT", t, g))
                    for j in range(4):
                        ins = pe.transpose(ps[:, j * P:(j + 1) * P], s_p[:, g, j * P:(j + 1) * P], eye[:, :])
                    done(ins, ("probT", t, g))
                ps = fill(("sout", t))
                for g in range(KVH):
                    taken(pe, ("probT", t, g))
                    for hh in range(4):
                        h = 4 * g + hh
                        for c in range(2):
                            vals = s_vsh if c == 0 else s_v
                            ins = pe.matmul(ps[c * CH:(c + 1) * CH, h * HD:(h + 1) * HD],
                                            s_pT[:, g, hh * P + c * CH:hh * P + (c + 1) * CH],
                                            vals[:, t, g * HD:(g + 1) * HD], start=True, stop=True)
                done(ins, ("sout", t))
                if t:
                    turn_o(0, t - 1)
            turn_o(0, NT - 1)
            mix_and_norm(0)
            ffn(0)
            turn_x(2)
            b = first_block[("ba",)]
            ps = fill(("ba",))
            pe.wait_ge(w_lo_ready, b + 1)
            for t in range(NT):
                for k in range(KD):
                    if t == 0:
                        pe.wait_ge(s["x_lo_ready"], 2 * KD + k + 1)
                    ins = mm3(ps[:, t * 2 * GDN_H:(t + 1) * 2 * GDN_H], xcols(k, tile_cols[t]),
                              weights(b, k, 0, 2 * GDN_H), k == 0, k == KD - 1)
            done(ins, ("ba",))
            for i, n in enumerate(CONV_ORDER):
                b = first_block[("conv", n - n % 2)]
                pe.wait_ge(w_lo_ready, b + 1)
                ps = fill(("conv", n))
                for k in range(KD):
                    ins = mm3(ps[:, :], weights(b, k, (n % 2) * P, P), xcols(k, ALL), k == 0, k == KD - 1)
                done(ins, ("conv", n))
                if i == 3:
                    ps = fill(("decay",))
                    pe.wait_ge(s["g_ready"], 1)
                    pe.wait_ge(consts, 16 * (N_CONST + 4))
                    g = gdec[:, :, :].rearrange("p t h -> p (t h)")
                    pe.matmul(ps[:, 0:TH], upto[:, :], g, start=True, stop=True)
                    done(pe.matmul(ps[:, TH:2 * TH], o_block[:, :], g, start=True, stop=True), ("decay",))
                if i >= 2 and CONV_ORDER[i - 2] < 2 * KD:
                    m = CONV_ORDER[i - 2]
                    ps = fill(("norm", m))
                    pe.wait_ge(s["conv_sq"], i - 1)
                    for t in range(NT):
                        ins = pe.matmul(ps[:, t:t + 1], conv_squares(i - 2)[:, tile_cols[t]], ones[:, :],
                                        start=True, stop=True)
                    done(ins, ("norm", m))
            for half in range(2):
                tm_group(("og", half), no_wait)
            pe.wait_ge(s["conv_silu"], len(CONV_ORDER))

            def per_head(key, fn):
                ps = fill(key)
                for q in range(4):
                    ins = fn(ps[:, q * P:(q + 1) * P], 4 * key[-1] + q)
                done(ins, key)

            def mul(o, a, b_):
                return pe.matmul(o, a, b_, start=True, stop=True)

            for t in range(NT):
                tc_ = tile_cols[t]
                H = range(2)
                for hg in H:
                    per_head(("kTM", t, hg), lambda o, h: pe.transpose(o, qkv[:, KD + h, tc_], eye[:, :]))
                for hg in H:
                    per_head(("vTM", t, hg), lambda o, h: pe.transpose(o, qkv[:, 2 * KD + h, tc_], eye[:, :]))
                for hg in H:
                    pe.wait_ge(s["gu_ready"], 2 * t + hg + 1)
                    ps = fill(("drow", t, hg))
                    done(mul(ps[:, :], ones[:, :].broadcast_to([P, P]),
                             GU[:, hsl[hg], :].rearrange("p a b -> p (a b)")), ("drow", t, hg))
                if t:
                    turn_o(1, t - 1)
                for hg in H:
                    taken(pe, ("kTM", t, hg))
                    per_head(("khT", t, hg), lambda o, h: pe.transpose(o, KH[:, h, :], eye[:, :]))
                for hg in H:
                    taken(pe, ("khT", t, hg))
                    per_head(("gram", t, hg), lambda o, h: mul(o, qkv[:, KD + h, tc_], qkv[:, KD + h, tc_]))
                for hg in H:
                    per_head(("qk", t, hg), lambda o, h: mul(o, qkv[:, KD + h, tc_], qkv[:, h, tc_]))
                for hg in H:
                    pe.wait_ge(s["t0_ready"], 2 * t + hg + 1)
                    per_head(("s0", t, hg), lambda o, h: pe.transpose(o, TT[:, h, :], eye[:, :]))
                for l, lv in enumerate(LEVELS[1:]):
                    for hg in H:
                        pe.wait_ge(s["ab_ready"], 2 * ((len(LEVELS) - 1) * t + l) + hg + 1)
                        if l == 0:
                            taken(pe, ("s0", t, hg))
                        else:
                            taken(pe, ("ds", t, LEVELS[l], hg))
                            taken(pe, ("dt", t, LEVELS[l], hg))
                        per_head(("m1", t, lv, hg), lambda o, h: mul(o, KB[:, h, :], SS[:, h, :]))
                    for hg in H:
                        taken(pe, ("m1", t, lv, hg))
                        per_head(("ds", t, lv, hg), lambda o, h: mul(o, TT[:, h, :], M1[:, h, :]))
                    if lv < LEVELS[-1]:
                        for hg in H:
                            per_head(("dt", t, lv, hg), lambda o, h: mul(o, M1[:, h, :], TT[:, h, :]))
                for hg in H:
                    taken(pe, ("ds", t, LEVELS[-1], hg))
                    taken(pe, ("vTM", t, hg))
                    per_head(("u", t, hg), lambda o, h: mul(o, SS[:, h, :], qkv[:, 2 * KD + h, tc_]))
                for hg in H:
                    pe.wait_ge(s["kb_ready"], 2 * t + hg + 1)
                    per_head(("w", t, hg), lambda o, h: mul(o, KB[:, h, :], SS[:, h, :]))
                for c in range(2):
                    rows = slice(c * CH, (c + 1) * CH)
                    state = ST if c == 0 else GA
                    for hg in H:
                        if c:
                            taken(pe, ("kv", t, 0, hg))
                        elif t:
                            taken(pe, ("kv", t - 1, 1, hg))
                        else:
                            pe.wait_ge(s["state0"], 1)
                        taken(pe, ("w", t, hg))
                        per_head(("ws", t, c, hg), lambda o, h: mul(o[rows], TT[:, h, rows], state[:, h, :]))
                    pe.wait_ge(s["q_decayed"], 2 * t + 2)
                    for hg in H:
                        ps = fill(("o", t, hg)) if c == 0 else bank(("o", t, hg))
                        for q in range(4):
                            h = 4 * hg + q
                            cols = slice(t * P + c * CH, t * P + (c + 1) * CH)
                            pe.matmul(ps[rows, q * P:(q + 1) * P], qkv[:, h, cols], state[:, h, :],
                                      start=q == 0, stop=False, skip_group_check=True)
                    for hg in H:
                        taken(pe, ("ws", t, c, hg))
                        pe.wait_ge(s["kd_ready"], 2 * t + hg + 1)
                        per_head(("kv", t, c, hg), lambda o, h: mul(o, KH[rows, h, :], EE[rows, h, :]))
                for hg in H:
                    ps = bank(("o", t, hg))
                    for q in range(4):
                        h = 4 * hg + q
                        ins = pe.matmul(ps[:, q * P:(q + 1) * P], GT[:, h, :], EE[:, h, :],
                                        start=False, stop=q == 3, skip_group_check=True)
                    done(ins, ("o", t, hg))
            turn_o(1, NT - 1)
            mix_and_norm(1)
            ffn(1)


_INS = ["x", "ev_w_in", "ev_gla_w_a2", "ev_gla_b_a", "ev_gla_norm_g", "ev_swa_sinks", "ev_w_out", "od_w_in",
        "od_conv_w", "od_a_log", "od_dt_bias", "od_norm_g", "od_w_out", "ffn_w_gate", "ffn_w_up", "ffn_w_down",
        "ln1_g", "ln1_b", "ln2_g", "ln2_b"]


def kernel(**inputs):
    import concourse.bacc as bacc
    from concourse.bass_utils import run_bass_kernel_spmd

    nc = bacc.Bacc("TRN2", target_bir_lowering=False, num_devices=1)
    arrays, views = {}, {}
    given = {n: np.ascontiguousarray(inputs[n]) for n in _INS}
    given.update(shape_constants())
    for name, a in given.items():
        arrays[name + "_dram"] = a
        views[name] = nc.dram_tensor(name + "_dram", a.shape, mybir.dt.from_np(a.dtype), kind="ExternalInput").ap()
    out = nc.dram_tensor("out_dram", (1, SEQ, D), F32, kind="ExternalOutput").ap()
    trunk_kernel(nc, views, out)
    r = run_bass_kernel_spmd(nc, [arrays], core_ids=[0])
    return r.results[0]["out_dram"]
```

```python
from contextlib import ExitStack

import numpy as np

import concourse.bass as bass
from concourse import mybir

F32 = mybir.dt.float32
F32R = mybir.dt.float32r
I32 = mybir.dt.int32
ALU = mybir.AluOpType
ACT = mybir.ActivationFunctionType
AX = mybir.AxisListType.X

P = 128
D = 1024
SEQ = 512
NT = SEQ // P
KD = D // P
CH = 64
NC = SEQ // CH
DFF = ((8 * D + 3 * 256 - 1) // (3 * 256)) * 256
KF = DFF // P
ALPHA = 4.0 ** 0.25
LN_EPS = 1e-5
RMS_EPS = 1e-6

GH, GDK, GDV, GRANK, TAU = 4, 64, 128, 16, 16.0
QH, KVH, HD = 8, 2, 64
RH = HD // 2
GDN_H = 8
CONV_K = 4
CONV_CH = 3 * D
NEG = -1e30

GQ0 = 0
GK0 = GQ0 + GH * GDK
GV0 = GK0 + GH * GDK
GA0 = GV0 + GH * GDV
GR0 = GA0 + GRANK
SQ0 = GR0 + GH * GDV
SKV0 = SQ0 + QH * HD
OQ0, OK0, OV0 = 0, D, 2 * D
BA0 = CONV_CH
OG0 = BA0 + 2 * GDN_H

WCOLS = 2048
LEVELS = (1, 2, 4, 8, 16, 32)
QK_AFTER, TURN_AFTER = 2, 8


def shape_constants():
    i = np.arange(P)
    same = (i[:, None] // CH) == (i[None, :] // CH)
    upto = (same & (i[:, None] <= i[None, :])).astype(np.float32)
    block = same.astype(np.float32)
    neg_t = np.where(same & (i[:, None] <= i[None, :]), 0.0, NEG).astype(np.float32)
    pos_l = np.where(same & (i[:, None] > i[None, :]), 0.0, -NEG).astype(np.float32)
    r, levels = i[:, None] % CH, []
    for b in LEVELS:
        up = np.array([n for n in range(CH) if n % (2 * b) >= b])[None, :]
        levels.append((r // (2 * b) == up // (2 * b)) & (r % (2 * b) < b))
    levels = np.concatenate([m.astype(np.float32) for m in levels], 1)
    inv = np.float32(10000.0) ** (-np.arange(RH, dtype=np.float32) / np.float32(RH))
    ang = np.arange(SEQ, dtype=np.float32)[:, None] * inv[None, :]
    rope = np.stack([np.cos(ang), np.sin(ang)], 1).astype(np.float32)
    rope = rope.reshape(NT, P, 2 * RH).transpose(1, 0, 2).reshape(P, -1)
    keep = np.broadcast_to((np.arange(SEQ) % CH != 0).astype(np.float32), (P, SEQ))
    return {
        "c_eye": np.eye(P, dtype=np.float32),
        "c_upto": upto,
        "c_odd": np.ascontiguousarray(np.concatenate([block, neg_t, pos_l, levels], 1)),
        "c_rope": np.ascontiguousarray(rope),
        "c_keep": np.ascontiguousarray(keep),
    }


def weight_plan(A):
    blocks = []

    def add(name, w, k0, nk, c0, width):
        view = w[k0 * P:(k0 + nk) * P, c0:c0 + width].rearrange("(k p) n -> p k n", p=P)
        blocks.append((name, k0, nk, width, view))

    def add_tm(name, w, kt, c0, width):
        for k0 in range(0, kt, 4):
            add(name, w, k0, min(4, kt - k0), c0, width)

    ev, od = A["ev_w_in"][0], A["od_w_in"][0]

    def ffn(layer):
        g, u, d = (A[n][layer] for n in ("ffn_w_gate", "ffn_w_up", "ffn_w_down"))
        for f in range(0, KF, 2):
            add(("gate", layer, f), g, 0, KD, f * P, 256)
            add(("up", layer, f), u, 0, KD, f * P, 256)
        for half in range(2):
            add_tm(("down", layer, half), d, KF, half * 512, 512)

    add(("skv",), ev, 0, KD, SKV0, 2 * KVH * HD)
    add_tm(("sq",), ev, KD, SQ0, 512)
    add(("gq",), ev, 0, KD, GQ0, 256)
    add(("gk",), ev, 0, KD, GK0, 256)
    add(("ga",), ev, 0, KD, GA0, P)
    add_tm(("gv",), ev, KD, GV0, 512)
    add_tm(("gr",), ev, KD, GR0, 512)
    for half in range(2):
        add_tm(("mix", 0, half), A["ev_w_out"][0], KD, half * 512, 512)
    ffn(0)
    for part, c0 in ((1, OK0), (0, OQ0), (2, OV0)):
        for n in range(0, KD, 2):
            add(("conv", part * KD + n), od, 0, KD, c0 + n * P, 256)
            if (part, n) == (1, 0):
                add(("ba",), od, 0, KD, BA0, 2 * GDN_H)
    for half in range(2):
        add_tm(("og", half), od, KD, OG0 + half * 512, 512)
    for half in range(2):
        add_tm(("mix", 1, half), A["od_w_out"][0], KD, half * 512, 512)
    ffn(1)
    return blocks


DECAY_AT = 5
CONV_ORDER = [part * KD + n for part in (1, 0, 2) for n in range(KD)]


FILLERS = {(0, 0): ("og", 0, 0), (0, 1): ("og", 0, 1), (0, 2): ("og", 0, 2), (0, 3): ("og", 0, 3),
           (1, 0): ("og", 1, 0), (1, 1): ("og", 1, 1), (2, 0): ("og", 1, 2), (2, 1): ("og", 1, 3),
           (3, 0): ("mix", 1, 0, 0), (3, 1): ("mix", 1, 0, 1)}
OG_ORDER = [FILLERS[k] for k in sorted(FILLERS) if FILLERS[k][0] == "og"]


def unit_plan():
    u = []
    tiles = range(NT)

    def ln(i):
        u.extend(("xT", i, k) for k in range(KD))

    def ffn(layer):
        for f in range(0, KF, 2):
            u.extend([("gate", layer, f), ("gate", layer, f + 1), ("up", layer, f), ("up", layer, f + 1)])
        for half in range(2):
            u.extend(("down", layer, half, t) for t in tiles)

    ln(0)
    u += [("skv", t) for t in tiles] + [("const", 0), ("const", 1)] + [("sq", t) for t in tiles]
    u += [("gq", 0), ("gq", 1), ("gk", 0), ("gk", 1), ("ga",)]
    for t in tiles:
        u += [("qT", t), ("kT", t)]
    u += [("gv", t) for t in tiles] + [("a2", 0), ("a2", 1)]
    u += [("gr", t) for t in tiles]
    for t in tiles:
        u += [("score", t, 0), ("score", t, 1), ("kd", t), ("gattn", t), ("gstate", t, 0), ("gout", t),
              ("gstate", t, 1), ("probT", t, 0), ("probT", t, 1), ("sout", t)]
        if t:
            u += [("oT", 0, t - 1, 0), ("oT", 0, t - 1, 1)]
    u += [("oT", 0, NT - 1, 0), ("oT", 0, NT - 1, 1)]
    u += [("mix", 0, half, t) for half in range(2) for t in tiles]
    ln(1)
    ffn(0)
    ln(2)
    for i, n in enumerate(CONV_ORDER):
        u.append(("conv", n))
        if i == 1:
            u.append(("ba",))
        if i == DECAY_AT:
            u.append(("decay",))
        if i >= 2 and CONV_ORDER[i - 2] < 2 * KD:
            u.append(("norm", CONV_ORDER[i - 2]))
    for t in tiles:
        def filler(place):
            return [FILLERS[t, place]] if (t, place) in FILLERS else []

        def both(*names):
            return [(name, t, hg) for name in names for hg in range(2)]

        u += both("kTM", "vTM", "drow") + filler(0) + both("khT", "gram") + filler(1) + both("at") + filler(2)
        for b in LEVELS[1:]:
            for hg in range(2):
                u += [("m1", t, b, hg), ("tt", t, b, hg)]
            u += [("ds", t, b, 0), ("ds", t, b, 1)]
            if b == QK_AFTER:
                u += both("qk")
            if t and b == TURN_AFTER:
                u += [("oT", 1, t - 1, 0), ("oT", 1, t - 1, 1)]
        u += filler(3) + both("u", "w")
        u += [("ws", t, 0, 0), ("ws", t, 0, 1), ("o", t, 0), ("o", t, 1), ("kv", t, 0, 0), ("kv", t, 0, 1),
              ("ws", t, 1, 0), ("ws", t, 1, 1), ("kv", t, 1, 0), ("kv", t, 1, 1)]
    u += [("oT", 1, NT - 1, 0), ("oT", 1, NT - 1, 1)]
    u += [("mix", 1, half, t) for half in range(2) for t in tiles if ("mix", 1, half, t) not in FILLERS.values()]
    ln(3)
    ffn(1)
    return {key: i for i, key in enumerate(u)}


def trunk_kernel(nc, A, out):
    blocks = weight_plan(A)
    NB = len(blocks)
    unit = unit_plan()
    first_block = {}
    for b, blk in enumerate(blocks):
        first_block.setdefault(blk[0], b)

    ctx = ExitStack()
    with ctx:
        base = (nc.sbuf_base + 63) // 64 * 64
        here = [base]

        def sb(name, shape, dt=F32, at=None):
            size = (int(np.prod(shape[1:])) * 4 + 31) // 32 * 32
            off = here[0] if at is None else at
            if at is None:
                here[0] += size
            assert off + size <= nc.sbuf_usable_end, (name, off + size)
            return nc.alloc_sbuf_tensor_at(name, shape, dt, offset=off)

        w_raw = sb("w_raw", [P, 2, WCOLS])
        w_hi = sb("w_hi", [P, 2, WCOLS], F32R)
        w_lo = sb("w_lo", [P, 2, WCOLS], F32R)
        x_hi = sb("x_hi", [P, KD, SEQ], F32R)
        x_lo = sb("x_lo", [P, KD, SEQ], F32R)
        x_tm = sb("x_tm", [P, NT, D])
        eye = sb("eye", [P, P])
        upto = sb("upto", [P, P])
        small0 = here[0]
        lnc = sb("lnc", [P, 66])
        convw = sb("convw", [P, CONV_K * 3 * KD])
        sinks = sb("sinks", [P, QH])
        a_log = sb("a_log", [P, GDN_H])
        dt_bias = sb("dt_bias", [P, GDN_H])
        onorm_row = sb("onorm_row", [P, P])
        stats = sb("stats", [P, NT, 2, 6])
        mv = sb("mv", [P, NT, 2])
        rstd = sb("rstd", [P, NT])
        nmr = sb("nmr", [P, NT])
        TH = NT * GDN_H
        ba = sb("ba", [P, NT, 2 * GDN_H])
        beta = sb("beta", [P, NT, GDN_H])
        gdec = sb("gdec", [P, NT, GDN_H])
        g_tmp = sb("g_tmp", [P, NT, GDN_H])
        dec = sb("dec", [P, 2, NT, GDN_H])
        to_end = sb("to_end", [P, NT, GDN_H])
        bexp = sb("bexp", [P, NT, GDN_H])
        nrm = sb("nrm", [P, 2 * KD, NT])
        edl = sb("edl", [P, GDN_H, 2])
        oms = sb("oms", [P, GDN_H])
        ones = sb("ones", [P, 1])
        eps = sb("eps", [P, 2])
        s_max = sb("s_max", [P, QH])
        s_snk = sb("s_snk", [P, QH])
        s_den = sb("s_den", [P, QH])
        g_mu = sb("g_mu", [P, GH])
        g_var = sb("g_var", [P, GH])
        ARENA = here[0]

        q_pad = sb("q_pad", [P, GH, SEQ])
        g_q = sb("g_q", [P, 2, SEQ])
        g_k = sb("g_k", [P, 2, SEQ])
        g_kd = sb("g_kd", [P, 2, SEQ])
        g_B = sb("g_B", [P, 2, SEQ])
        g_e = sb("g_e", [P, 2, SEQ])
        g_v = sb("g_v", [P, NT, GH * GDV])
        g_r = sb("g_r", [P, NT, GH * GDV])
        g_ga = sb("g_ga", [GRANK, SEQ])
        g_a2 = sb("g_a2", [GRANK, GH * GDK])
        g_keep = sb("g_keep", [P, SEQ])
        g_norm = sb("g_norm", [P, GH * GDV])
        g_at = sb("g_at", [P, GH, P])
        g_kdt = sb("g_kdt", [P, 2, P])
        g_S = sb("g_S", [P, 2, 2, GDV])
        rope = sb("rope", [P, NT, 2, RH])
        r_tmp = sb("r_tmp", [P, 4, QH, RH])
        s_v = sb("s_v", [P, NT, KVH * HD])
        s_vsh = sb("s_vsh", [P, NT, KVH * HD])
        s_qT = sb("s_qT", [P, QH // 2, SEQ])
        s_kT = sb("s_kT", [P, 2 * KVH, CH + SEQ])
        q_rot_at = here[0]
        q_rot = sb("q_rot", [P, NT, QH * HD])
        k_pad = sb("k_pad", [P, NT, 2 * KVH, P])
        s_p = sb("s_p", [P, 2, 512], at=q_rot_at)
        s_pT = sb("s_pT", [P, 2, 512], at=q_rot_at + 4096)
        o_tm = sb("o_tm", [P, 2, D], at=q_rot_at + 8192)

        here[0] = ARENA
        h_hi = sb("h_hi", [P, KF, SEQ], F32R)
        h_lo = sb("h_lo", [P, KF, SEQ], F32R)
        ln_rows = sb("ln_rows", [P, 2, D])
        f_ab = sb("f_ab", [P, 4, SEQ])
        rows_at = ARENA + 2 * KF * SEQ * 4
        vec_rows = sb("vec_rows", [P, P], at=rows_at)
        conv_rows = sb("conv_rows", [P, P], at=rows_at + 512)

        here[0] = ARENA
        qkv = sb("qkv", [P, 3 * KD, SEQ])
        gate_s = sb("gate_s", [P, NT, D])
        o_block = sb("o_block", [P, P])
        o_negt = sb("o_negt", [P, P])
        o_posl = sb("o_posl", [P, P])
        o_lvl = sb("o_lvl", [P, len(LEVELS), CH // 2])
        KH = sb("KH", [P, GDN_H, P])
        GU = sb("GU", [P, GDN_H, P])
        EE = sb("EE", [P, GDN_H, P])
        GT = sb("GT", [P, GDN_H, P])
        GA = sb("GA", [P, GDN_H, P])
        TT = sb("TT", [P, GDN_H, P])
        SS = sb("SS", [P, GDN_H, P])
        M1 = sb("M1", [P, GDN_H, P])
        ST = sb("ST", [P, GDN_H, P])
        OO = sb("OO", [P, GDN_H, P])

        banks = [ctx.enter_context(nc.psum_tensor(f"bank{i}", [P, 512], F32)) for i in range(8)]

        def sem(name):
            return ctx.enter_context(nc.semaphore(name))

        bank_full = [sem(f"bank_full{i}") for i in range(8)]
        bank_taken = [sem(f"bank_taken{i}") for i in range(8)]
        w_landed = [sem(f"w_landed{i}") for i in range(2)]
        x_landed = [sem(f"x_landed{t}") for t in range(NT)]
        w_hi_ready = sem("w_hi_ready")
        w_lo_ready = sem("w_lo_ready")
        w_used = sem("w_used")
        consts = sem("consts")
        const_cols = sem("const_cols")
        zeroed = sem("zeroed")

        def bank(key):
            return banks[unit[key] % 8]

        def full(e, key):
            if e is nc.vector or e is nc.scalar:
                e.drain()
            e.wait_ge(bank_full[unit[key] % 8], unit[key] // 8 + 1)

        def taken(e, key):
            e.wait_ge(bank_taken[unit[key] % 8], unit[key] // 8 + 1)

        def take(ins, key):
            ins.then_inc(bank_taken[unit[key] % 8], 1)

        def low_part_there(e, i, k):
            e.wait_ge(s[("x_lo_even", "x_lo_odd")[k % 2]], KD // 2 * i + k // 2 + 1)

        block_end = []
        count = 0
        for b, (name, k0, nk, width, _) in enumerate(blocks):
            last = b + 1 == NB or blocks[b + 1][0] != name
            if name[0] == "og":
                key = max((f for f in OG_ORDER if f[1] == name[1]), key=lambda f: unit[f])
                block_end.append((bank_full[unit[key] % 8], unit[key] // 8 + 1))
            elif not last:
                count += 1
                block_end.append((w_used, count))
            else:
                key = {"skv": ("skv", NT - 1), "sq": ("sq", NT - 1), "gv": ("gv", NT - 1), "gr": ("gr", NT - 1),
                       "gq": ("gq", 1), "gk": ("gk", 1), "ga": ("ga",), "ba": ("ba",)}.get(name[0])
                if name[0] in ("gate", "up"):
                    key = (name[0], name[1], name[2] + 1)
                elif name[0] == "conv":
                    key = ("conv", name[1] + 1)
                elif key is None:
                    key = (*name, NT - 1)
                block_end.append((bank_full[unit[key] % 8], unit[key] // 8 + 1))

        s = {n: sem(n) for n in (
            "eye_landed", "ln_landed", "x_hi_ready", "x_lo_even", "x_lo_odd", "z_norm", "half_stats", "ln_stat", "ln_var",
            "x_affine", "out_sent", "act_step", "dve_step", "o_hi_ready", "h_hi_ready", "h_lo_ready",
            "sv_copied", "sv_shifted", "q_rotated", "k_rotated", "a2_exp", "a2_mid", "g_scan", "g_exp", "g_gate",
            "k_decayed", "q_gated", "k_gated", "s_shift", "s_prob", "o_var", "o_rstd", "o_even",
            "ba_exp", "ba_mid", "g_ready", "dec_ready", "dec_exp", "conv_raw", "conv_silu",
            "conv_sq", "rn_ready", "gu_ready", "e_ready", "ga_arg", "gt_arg", "ga_exp", "gt_exp", "gate_ready", "eye_ready", "s0_ready", "o_sq",
            "q_decayed", "kb_ready", "kd_ready", "state0", "ov_ready", "or_ready", "o_scaled", "o_odd",
        )}

        block_ = ctx.enter_context(nc.Block())
        Q4 = GDN_H // 2
        def conv_acc(i):
            return KH[:, 4 * (i % 2):4 * (i % 2) + 4, :].rearrange("p a b -> p (a b)")

        def upper_halves(ap, b):
            return ap.rearrange("p (m two b) -> p m two b", two=2, b=b)[:, :, 1, :]

        def half_product(hg):
            return M1[:, 2 * hg:2 * hg + 2, :].rearrange("p a b -> p (a b)")

        def by_chunk(ap, hg):
            return ap[:, hsl[hg], :].rearrange("p h (c l) -> p h c l", l=CH)

        def conv_squares(i):
            return GU[:, 4 * (i % 2):4 * (i % 2) + 4, :].rearrange("p a b -> p (a b)")

        SPLIT_IN = {("og", 1): 0, ("mix", 1, 0): 2}
        tile_cols = [slice(t * P, (t + 1) * P) for t in range(NT)]
        hsl = [slice(0, Q4), slice(Q4, GDN_H)]
        N_CONST, N_CONST_ODD = 15, 4

        @block_.sync
        def _(sp):
            def load_block(b):
                name, k0, nk, width, view = blocks[b]
                if b >= 2:
                    sp.wait_ge(w_lo_ready, b - 1)
                dst = w_raw[:, b % 2, 0:nk * width].rearrange("p (k n) -> p k n", k=nk)
                sp.dma_start(dst, view).then_inc(w_landed[b % 2], 16)

            load_block(0)
            sp.dma_start(eye[:, :], A["c_eye"]).then_inc(s["eye_landed"], 16)
            for t in range(NT):
                sp.dma_start(x_tm[:, t, :], A["x"][0, t * P:(t + 1) * P, :]).then_inc(x_landed[t], 16)
            load_block(1)
            small = [(upto[:, :], A["c_upto"])]
            for i, nm in enumerate(("ln1_g", "ln1_b", "ln2_g", "ln2_b")):
                small.append((vec_rows[16 * i:16 * i + 16, :], A[nm].rearrange("l (k p) -> (l k) p", p=P)))
            small.append((vec_rows[64:66, :], A["ev_gla_b_a"].rearrange("l (k p) -> (l k) p", p=P)))
            small.append((conv_rows[0:96, :], A["od_conv_w"][0].rearrange("c (n p) -> (c n) p", p=P)))
            small.append((sinks[:, :], A["ev_swa_sinks"][0:1, :].broadcast_to([P, QH])))
            small.append((a_log[:, :], A["od_a_log"][0:1, :].broadcast_to([P, GDN_H])))
            small.append((dt_bias[:, :], A["od_dt_bias"][0:1, :].broadcast_to([P, GDN_H])))
            small.append((onorm_row[:, :], A["od_norm_g"][0:1, :].broadcast_to([P, P])))
            small.append((g_a2[:, :], A["ev_gla_w_a2"][0]))
            small.append((g_keep[:, :], A["c_keep"]))
            small.append((g_norm[:, :], A["ev_gla_norm_g"][0:1, :].broadcast_to([P, GH * GDV])))
            small.append((rope[:, :, :, :], A["c_rope"].rearrange("p (t c r) -> p t c r", t=NT, c=2)))
            for dst, src in small:
                sp.dma_start(dst, src).then_inc(consts, 16)
            assert len(small) == N_CONST

            def load_until(b):
                while at[0] < b:
                    load_block(at[0])
                    at[0] += 1

            def load_ln(i):
                g, v = (("ln1_g", "ln1_b"), ("ln2_g", "ln2_b"))[(i + 1) % 2]
                layer = (i - 1) // 2
                for j, nm in enumerate((g, v)):
                    sp.dma_start(ln_rows[:, j, :], A[nm][layer:layer + 1, :].broadcast_to([P, D]))\
                      .then_inc(s["ln_landed"], 16)

            at = [2]
            load_until(first_block[("gate", 0, 0)] + 1)
            taken(sp, ("oT", 0, NT - 1, 1))
            load_ln(1)
            load_until(first_block[("down", 0, 1)])
            sp.wait_ge(s["x_affine"], 2 * NT)
            load_ln(2)
            load_until(first_block[("gate", 1, 0)] + 1)
            taken(sp, ("oT", 1, NT - 1, 1))
            load_ln(3)
            load_until(first_block[("down", 1, 1)])
            sp.wait_ge(s["x_affine"], 6 * NT)
            load_ln(4)
            load_until(NB)
            for t in range(NT):
                sp.wait_ge(s["x_affine"], 6 * NT + 2 * (t + 1))
                sp.dma_start(out[0, t * P:(t + 1) * P, :], x_tm[:, t, :]).then_inc(s["out_sent"], 16)
            sp.wait_ge(s["out_sent"], 16 * NT)

        @block_.gpsimd
        def _(pool):
            def split_lo(b):
                name, k0, nk, width, _v = blocks[b]
                n = nk * width
                pool.wait_ge(w_hi_ready, b + 1)
                pool.tensor_tensor(w_lo[:, b % 2, 0:n], w_raw[:, b % 2, 0:n], w_hi[:, b % 2, 0:n].bitcast(F32),
                                   ALU.subtract).then_inc(w_lo_ready, 1)

            def low_parts(i):
                for k in range(1, KD, 2):
                    pool.wait_ge(s["x_hi_ready"], KD * i + k + 1)
                    pool.tensor_tensor(x_lo[:, k, :], f_ab[:, k % 4, :], x_hi[:, k, :].bitcast(F32), ALU.subtract)\
                        .then_inc(s["x_lo_odd"], 1)

            pool.memset(q_pad[:, :, :], 0.0).then_inc(zeroed, 1)
            pool.memset(g_at[:, :, :], 0.0).then_inc(zeroed, 1)
            pool.memset(g_S[:, :, :, :], 0.0).then_inc(zeroed, 1)
            pool.memset(s_kT[:, :, 0:CH], 0.0).then_inc(zeroed, 1)
            pool.memset(s_vsh[:, :, :], 0.0).then_inc(zeroed, 1)
            pool.memset(ones[:, :], 1.0).then_inc(zeroed, 1)
            pool.memset(eps[:, 0:1], LN_EPS).then_inc(zeroed, 1)
            pool.memset(eps[:, 1:2], RMS_EPS).then_inc(zeroed, 1)
            affine, turned = {}, {0: 0}
            for i, name in ((1, ("gate", 0, 0)), (2, ("conv", KD)), (3, ("gate", 1, 0))):
                turned[first_block[name]] = i
                for t in range(NT):
                    affine[first_block[name] + 1 + t] = (i, t)
            def gate_times_norm(place, t):
                name = FILLERS.get((t, place))
                if name is not None and name[0] == "og":
                    taken(pool, name)
                    gs = gate_s[:, name[2], name[1] * 512:(name[1] + 1) * 512].rearrange("p (h n) -> p h n", h=4)
                    pool.tensor_tensor(gs, gs, onorm_row[:, :].unsqueeze(1).broadcast_to([P, 4, P]), ALU.mult)\
                        .then_inc(s["gate_ready"], 1)

            def gate_output(t):
                for hg in range(2):
                    pool.wait_ge(s["o_scaled"], 2 * t + hg + 1)
                    pool.wait_ge(s["gate_ready"], OG_ORDER.index(("og", hg, t)) + 1)
                    o = OO[:, hsl[hg], :]
                    gs = gate_s[:, t, hg * 512:(hg + 1) * 512].rearrange("p (h n) -> p h n", h=4)
                    pool.tensor_tensor(o, o, gs, ALU.mult).then_inc(s["o_odd"], 1)

            def prepare(t):
                if t:
                    full(pool, ("w", t - 1, 1))
                else:
                    full(pool, ("norm", CONV_ORDER[2 * KD - 1]))
                pool.tensor_copy(SS[:, :, :], eye[:, :].unsqueeze(1).broadcast_to([P, GDN_H, P]))\
                    .then_inc(s["eye_ready"], 1)
                for hg in range(2):
                    if t:
                        taken(pool, ("ws", t - 1, 1, hg))
                    hs = hsl[hg]
                    pool.tensor_tensor(GU[:, hs, :], upto[:, :].unsqueeze(1).broadcast_to([P, 4, P]),
                                       gdec[:, t, hs].unsqueeze(2).broadcast_to([P, 4, P]), ALU.mult)\
                        .then_inc(s["gu_ready"], 1)

            def delta_rule():
                pool.wait_ge(s["x_affine"], 4 * NT)
                prepare(0)
                for t in range(NT):
                    for hg in range(2):
                        taken(pool, ("drow", t, hg))
                        pool.tensor_tensor(GT[:, hsl[hg], :], GU[:, hsl[hg], :],
                                           o_negt[:, :].unsqueeze(1).broadcast_to([P, 4, P]), ALU.add)\
                            .then_inc(s["gt_arg"], 1)
                    for place in range(3):
                        gate_times_norm(place, t)
                    for hg in range(2):
                        full(pool, ("qk", t, hg))
                        pool.wait_ge(s["e_ready"], 2 * t + hg + 1)
                        q = qkv[:, 4 * hg:4 * hg + 4, tile_cols[t]]
                        pool.tensor_tensor(q, q, EE[:, hsl[hg], :], ALU.mult).then_inc(s["q_decayed"], 1)
                    if t:
                        gate_output(t - 1)
                    gate_times_norm(3, t)
                    for name in (("og", 1), ("mix", 1, 0)):
                        if t == SPLIT_IN[name]:
                            split_lo(first_block[name])
                            split_lo(first_block[name] + 1)
                    if t + 1 < NT:
                        prepare(t + 1)
                gate_output(NT - 1)

            for b in range(NB):
                if first_block[("og", 1)] <= b < first_block[("mix", 1, 1)]:
                    continue
                split_lo(b)
                if b in turned:
                    low_parts(turned[b])
                if b in affine:
                    i, t = affine[b]
                    n = 2 * (NT * (i - 1) + t)
                    full(pool, ("xT", i, KD - 1))
                    pool.wait_ge(s["ln_landed"], 32 * i)
                    pool.tensor_tensor(x_tm[:, t, :], x_tm[:, t, :], ln_rows[:, 0, :], ALU.mult)\
                        .then_inc(s["x_affine"], 1)
                    pool.wait_ge(s["x_affine"], n + 1)
                    pool.tensor_tensor(x_tm[:, t, :], x_tm[:, t, :], ln_rows[:, 1, :], ALU.add)\
                        .then_inc(s["x_affine"], 1)
                if b + 1 == first_block[("og", 1)]:
                    delta_rule()

        @block_.scalar
        def _(act):
            steps = [0]
            split = [0]

            def link(ins):
                steps[0] += 1
                ins.then_inc(s["act_step"], 1)
                act.wait_ge(s["act_step"], steps[0])

            def split_to(b):
                while split[0] <= min(b, NB - 1):
                    i = split[0]
                    n = blocks[i][2] * blocks[i][3]
                    act.wait_ge(w_landed[i % 2], 16 * (i // 2 + 1))
                    if i >= 2:
                        act.wait_ge(*block_end[i - 2])
                        act.wait_ge(w_lo_ready, i - 1)
                    act.activation(w_hi[:, i % 2, 0:n], w_raw[:, i % 2, 0:n], ACT.Copy).then_inc(w_hi_ready, 1)
                    split[0] += 1

            def round_x(i):
                for k in range(KD):
                    taken(act, ("xT", i, k))
                    act.activation(x_hi[:, k, :], f_ab[:, k % 4, :], ACT.Copy).then_inc(s["x_hi_ready"], 1)

            def layer_norm(i):
                for t in range(NT):
                    act.wait_ge(s["ln_var"], NT * (i - 1) + t + 1)
                    link(act.activation(rstd[:, t:t + 1], mv[:, t, 1:2], ACT.Ln, bias=eps[:, 0:1]))
                    act.activation(rstd[:, t:t + 1], rstd[:, t:t + 1], ACT.Exp, scale=-0.5).then_inc(s["ln_stat"], 1)

            def round_o(layer, t):
                for i in range(2):
                    full(act, ("oT", layer, t, i))
                    act.activation(x_hi[:, 4 * i:4 * i + 4, tile_cols[t]], fm4(("oT", layer, t, i)),
                                   ACT.Copy).then_inc(s["o_hi_ready"], 1)

            def ffn(layer):
                for f in range(0, KF, 2):
                    b = first_block[("gate", layer, f)]
                    split_to(b + 1)
                    for j in range(2):
                        full(act, ("gate", layer, f + j))
                        if f:
                            taken(act, ("up", layer, f + j - 2))
                        take(act.activation(f_ab[:, j, :], bank(("gate", layer, f + j))[:, :], ACT.Silu),
                             ("gate", layer, f + j))
                    split_to(b + 2)
                    for j in range(2):
                        taken(act, ("up", layer, f + j))
                        act.activation(h_hi[:, f + j, :], f_ab[:, 2 + j, :], ACT.Copy).then_inc(s["h_hi_ready"], 1)
                    split_to(b + 3)

            def fm4(key):
                return bank(key)[:, :].rearrange("p (k n) -> p k n", k=4)

            act.wait_ge(zeroed, 8)
            split_to(0)
            round_x(0)
            split_to(first_block[("sq",)] + 1)
            for t in range(NT):
                full(act, ("skv", t))
                act.activation(s_v[:, t, :], bank(("skv", t))[:, KVH * HD:2 * KVH * HD], ACT.Copy)\
                   .then_inc(s["sv_copied"], 1)
            act.wait_ge(s["sv_copied"], NT)
            act.dma_start(s_vsh[CH:P, :, :], s_v[0:CH, :, :]).then_inc(s["sv_shifted"], 16)
            act.dma_start(s_vsh[0:CH, 1:NT, :], s_v[CH:P, 0:NT - 1, :]).then_inc(s["sv_shifted"], 16)
            split_to(first_block[("gk",)])
            for n in range(2):
                full(act, ("gq", n))
                take(act.activation(g_q[:, n, :], bank(("gq", n))[:, :], ACT.Copy, scale=GDK ** -0.5), ("gq", n))
            split_to(first_block[("ga",)])
            for n in range(2):
                full(act, ("gk", n))
                take(act.activation(g_k[:, n, :], bank(("gk", n))[:, :], ACT.Copy), ("gk", n))
            split_to(first_block[("gv",)])
            full(act, ("ga",))
            take(act.activation(g_ga[:, :], bank(("ga",))[0:GRANK, :], ACT.Copy), ("ga",))
            split_to(first_block[("gv",)] + 1)
            for t in range(NT):
                full(act, ("qT", t))
                take(act.activation(s_qT[:, :, tile_cols[t]], fm4(("qT", t)), ACT.Copy), ("qT", t))
                full(act, ("kT", t))
                take(act.activation(s_kT[:, :, CH + t * P:CH + (t + 1) * P], fm4(("kT", t)), ACT.Copy), ("kT", t))
            split_to(first_block[("gr",)])
            for t in range(NT):
                full(act, ("gv", t))
                take(act.activation(g_v[:, t, :], bank(("gv", t))[:, :], ACT.Copy), ("gv", t))
            split_to(first_block[("gr",)] + 1)
            act.wait_ge(s["a2_mid"], 2)
            link(act.activation(g_e[:, :, :], g_kd[:, :, :], ACT.Exp))
            act.activation(g_e[:, :, :], g_e[:, :, :], ACT.Ln, bias=1.0).then_inc(s["a2_exp"], 1)
            act.wait_ge(s["g_scan"], 2)
            act.activation(g_e[:, :, :], g_B[:, :, :], ACT.Exp, scale=1.0 / TAU).then_inc(s["g_exp"], 1)
            act.wait_ge(s["g_gate"], 1)
            act.activation(s_p[:, :, :], s_p[:, :, :], ACT.Exp, scale=1.0 / TAU).then_inc(s["g_exp"], 1)
            act.wait_ge(s["k_decayed"], 1)
            act.activation(s_p[:, :, :], g_B[:, :, :], ACT.Exp, scale=-1.0 / TAU).then_inc(s["g_exp"], 1)
            for t in range(NT):
                full(act, ("gr", t))
                take(act.activation(g_r[:, t, :], bank(("gr", t))[:, :], ACT.Silu), ("gr", t))
            split_to(first_block[("mix", 0, 0)] + 1)
            for t in range(NT):
                for g in range(KVH):
                    act.wait_ge(s["s_shift"], KVH * t + g + 1)
                    act.activation(s_snk[:, 4 * g:4 * g + 4], s_snk[:, 4 * g:4 * g + 4], ACT.Exp)
                    act.activation(s_p[:, g, :], s_p[:, g, :], ACT.Exp).then_inc(s["s_prob"], 1)
                full(act, ("kd", t))
                take(act.activation(g_kdt[:, :, :], bank(("kd", t))[:, 0:2 * P].rearrange("p (k n) -> p k n", k=2),
                                    ACT.Copy), ("kd", t))
                for g in range(KVH):
                    full(act, ("probT", t, g))
                    take(act.activation(s_pT[:, g, :], bank(("probT", t, g))[:, :], ACT.Copy), ("probT", t, g))
                act.wait_ge(s["o_var"], t + 1)
                link(act.activation(g_var[:, :], g_var[:, :], ACT.Ln, scale=1.0 / GDV, bias=eps[:, 0:1]))
                act.activation(g_var[:, :], g_var[:, :], ACT.Exp, scale=-0.5).then_inc(s["o_rstd"], 1)
                if t:
                    round_o(0, t - 1)
            round_o(0, NT - 1)
            split_to(first_block[("mix", 0, 1)])
            full(act, ("mix", 0, 0, 0))
            split_to(first_block[("gate", 0, 0)])
            layer_norm(1)
            round_x(1)
            ffn(0)
            split_to(first_block[("conv", KD)])
            layer_norm(2)
            for dst, c0, n in ((o_block, 0, P), (o_negt, P, P), (o_posl, 2 * P, P)):
                act.dma_start(dst[:, :], A["c_odd"][:, c0:c0 + n]).then_inc(consts, 16)
            act.dma_start(o_lvl[:, :, :], A["c_odd"][:, 3 * P:].rearrange("p (l c) -> p l c", c=CH // 2))\
               .then_inc(consts, 16)
            round_x(2)

            def silu_conv(i):
                n = CONV_ORDER[i]
                taken(act, ("conv", n))
                act.activation(qkv[:, n, :], conv_acc(i), ACT.Silu).then_inc(s["conv_silu"], 1)
                if n < 2 * KD:
                    act.wait_ge(s["conv_silu"], i + 1)
                    if i >= 2:
                        full(act, ("norm", CONV_ORDER[i - 2]))
                    act.activation(conv_squares(i), qkv[:, n, :], ACT.Square).then_inc(s["conv_sq"], 1)

            for i, n in enumerate(CONV_ORDER):
                split_to(first_block[("conv", n - n % 2)] + 1)
                full(act, ("conv", n))
                act.activation(conv_acc(i), bank(("conv", n))[:, :], ACT.Copy,
                               scale=convw[:, 9 * KD + n:9 * KD + n + 1]).then_inc(s["conv_raw"], 1)
                if i:
                    silu_conv(i - 1)
                if i == 2:
                    act.wait_ge(s["ba_mid"], 1)
                    act.activation(beta[:, :, :], ba[:, :, 0:GDN_H], ACT.Exp, scale=-1.0)
                    link(act.activation(g_tmp[:, :, :], g_tmp[:, :, :], ACT.Exp))
                    act.activation(g_tmp[:, :, :], g_tmp[:, :, :], ACT.Ln, bias=1.0)
                    act.activation(a_log[:, :], a_log[:, :], ACT.Exp).then_inc(s["ba_exp"], 1)
                if i == DECAY_AT + 3:
                    act.wait_ge(s["dec_ready"], 1)
                    act.activation(to_end[:, :, :], to_end[:, :, :], ACT.Exp)
                    act.activation(bexp[:, :, :], dec[:, 0, :, :], ACT.Exp).then_inc(s["dec_exp"], 1)
            silu_conv(len(CONV_ORDER) - 1)
            split_to(first_block[("og", 0)] + 1)
            taken(act, ("norm", CONV_ORDER[2 * KD - 1]))
            link(act.activation(nrm[:, :, :], nrm[:, :, :], ACT.Ln, bias=eps[:, 1:2]))
            act.activation(nrm[:, :, :], nrm[:, :, :], ACT.Exp, scale=-0.5).then_inc(s["rn_ready"], 1)
            def filler(t, place):
                name = FILLERS.get((t, place))
                if name is not None and name[0] == "og":
                    full(act, name)
                    take(act.activation(gate_s[:, name[2], name[1] * 512:(name[1] + 1) * 512], bank(name)[:, :],
                                        ACT.Silu), name)

            def output_rstd(t):
                act.wait_ge(s["ov_ready"], 2 * (t + 1))
                link(act.activation(oms[:, :], oms[:, :], ACT.Ln, scale=1.0 / P, bias=eps[:, 1:2]))
                act.activation(oms[:, :], oms[:, :], ACT.Exp, scale=-0.5).then_inc(s["or_ready"], 1)

            for t in range(NT):
                for hg in range(2):
                    full(act, ("drow", t, hg))
                    act.activation(EE[:, hsl[hg], :], fm4(("drow", t, hg)), ACT.Exp).then_inc(s["e_ready"], 1)
                for hg in range(2):
                    act.wait_ge(s["ga_arg"], 2 * t + hg + 1)
                    act.activation(GA[:, hsl[hg], :], GA[:, hsl[hg], :], ACT.Exp, scale=-1.0)\
                       .then_inc(s["ga_exp"], 1)
                for hg in range(2):
                    act.wait_ge(s["gt_arg"], 2 * t + hg + 1)
                    act.activation(GT[:, hsl[hg], :], GT[:, hsl[hg], :], ACT.Exp).then_inc(s["gt_exp"], 1)
                filler(t, 0)
                for hg in range(2):
                    full(act, ("khT", t, hg))
                    take(act.activation(qkv[:, KD + 4 * hg:KD + 4 * hg + 4, tile_cols[t]], fm4(("khT", t, hg)),
                                        ACT.Copy), ("khT", t, hg))
                if t:
                    output_rstd(t - 1)
                filler(t, 1)
                filler(t, 2)
                for lv in LEVELS[1:]:
                    for hg in range(2):
                        full(act, ("tt", t, lv, hg))
                        take(act.activation(TT[:, hsl[hg], :], fm4(("tt", t, lv, hg)), ACT.Copy), ("tt", t, lv, hg))
                    if t and lv == 2 * TURN_AFTER:
                        round_o(1, t - 1)
                    if lv == 8 and t == SPLIT_IN[("mix", 1, 0)]:
                        split_to(first_block[("mix", 1, 0)] + 1)
                filler(t, 3)
                if t == SPLIT_IN[("og", 1)]:
                    split_to(first_block[("og", 1)] + 1)
                for name, dst in (("u", GU), ("w", TT)):
                    for hg in range(2):
                        full(act, (name, t, hg))
                        take(act.activation(dst[:, hsl[hg], :], fm4((name, t, hg)), ACT.Copy), (name, t, hg))
                for hg in range(2):
                    taken(act, ("o", t, hg))
                    act.activation(M1[:, hsl[hg], :], OO[:, hsl[hg], :], ACT.Square).then_inc(s["o_sq"], 1)
            output_rstd(NT - 1)
            round_o(1, NT - 1)
            split_to(first_block[("mix", 1, 1)])
            full(act, ("mix", 1, 0, 0))
            split_to(first_block[("gate", 1, 0)])
            layer_norm(3)
            round_x(3)
            ffn(1)
            split_to(NB - 1)
            layer_norm(4)

        @block_.vector
        def _(dve):
            steps = [0]

            def link(ins):
                steps[0] += 1
                ins.then_inc(s["dve_step"], 1)
                dve.wait_ge(s["dve_step"], steps[0])

            def k4(key):
                return bank(key)[:, :].rearrange("p (k n) -> p k n", k=4)

            def across(col, n):
                return col.unsqueeze(2).broadcast_to([col.shape[0], col.shape[1], n])

            def over_heads(mat, heads):
                return mat.unsqueeze(1).broadcast_to([mat.shape[0], heads, mat.shape[1]])

            def round_x(i):
                gcol = 32 * ((i + 1) % 2) + 8 * ((i - 1) // 2)

                def low(k):
                    dve.wait_ge(s["x_hi_ready"], KD * i + k + 1)
                    dve.tensor_tensor(x_lo[:, k, :], f_ab[:, k % 4, :], x_hi[:, k, :].bitcast(F32), ALU.subtract)\
                       .then_inc(s["x_lo_even"], 1)

                for k in range(KD):
                    full(dve, ("xT", i, k))
                    if k >= 4:
                        low_part_there(dve, i, k - 4)
                    src = bank(("xT", i, k))[:, :]
                    if i == 0:
                        take(dve.tensor_copy(f_ab[:, k % 4, :], src), ("xT", i, k))
                    else:
                        take(dve.tensor_scalar(f_ab[:, k % 4, :], src, lnc[:, gcol + k:gcol + k + 1],
                                               lnc[:, gcol + 16 + k:gcol + 17 + k], ALU.mult, ALU.add), ("xT", i, k))
                    if k % 2:
                        low(k - 1)

            def round_o(layer, t):
                for i in range(2):
                    dve.wait_ge(s["o_hi_ready"], 2 * (NT * layer + t) + i + 1)
                    cols = x_hi[:, 4 * i:4 * i + 4, tile_cols[t]].bitcast(F32)
                    take(dve.tensor_tensor(x_lo[:, 4 * i:4 * i + 4, tile_cols[t]], k4(("oT", layer, t, i)), cols,
                                           ALU.subtract), ("oT", layer, t, i))

            def layer_norm(i, group, layer):
                def normalise(t):
                    dve.wait_ge(s["ln_stat"], NT * (i - 1) + t + 1)
                    dve.tensor_scalar(x_tm[:, t, :], x_tm[:, t, :], mv[:, t, 0:1], rstd[:, t:t + 1],
                                      ALU.subtract, ALU.mult).then_inc(s["z_norm"], 1)

                for half in range(2):
                    for t in range(NT):
                        if (group, layer, half, t) not in FILLERS.values():
                            add_sublayer(i, group, layer, half, t)
                        if half:
                            dve.wait_ge(s["half_stats"], 2 * NT * (i - 1) + NT + t + 1)
                            dve.bn_aggr(mv[:, t, :], stats[:, t, :, :].rearrange("p a b -> p (a b)"))\
                               .then_inc(s["ln_var"], 1)
                            if t:
                                normalise(t - 1)
                normalise(NT - 1)

            def add_sublayer(i, group, layer, half, t):
                key = (group, layer, half, t)
                if i > 1:
                    dve.wait_ge(s["x_affine"], 2 * NT * (i - 2) + 2 * (t + 1))
                full(dve, key)
                cols = x_tm[:, t, half * 512:(half + 1) * 512]
                take(dve.scalar_tensor_tensor(cols, cols, ALPHA, bank(key)[:, :], ALU.mult, ALU.add), key)
                taken(dve, key)
                dve.bn_stats(stats[:, t, half, :], cols).then_inc(s["half_stats"], 1)

            def ffn(layer):
                for f in range(KF):
                    n = layer * KF + f
                    taken(dve, ("gate", layer, f))
                    full(dve, ("up", layer, f))
                    take(dve.tensor_tensor(f_ab[:, 2 + f % 2, :], bank(("up", layer, f))[:, :], f_ab[:, f % 2, :],
                                           ALU.mult), ("up", layer, f))
                    dve.wait_ge(s["h_hi_ready"], n + 1)
                    dve.tensor_tensor(h_lo[:, f, :], f_ab[:, 2 + f % 2, :], h_hi[:, f, :].bitcast(F32), ALU.subtract)\
                       .then_inc(s["h_lo_ready"], 1)

            round_x(0)
            low_part_there(dve, 0, KD - 2)
            low_part_there(dve, 0, KD - 1)
            dve.memset(k_pad[:, :, :, :].rearrange("p a b c -> p (a b c)"), 0.0).then_inc(zeroed, 1)
            dve.wait_ge(zeroed, 9)
            dve.wait_ge(consts, 16 * N_CONST)

            def rotate(src, dst, t, heads):
                cos = over_heads(rope[:, t, 0, :], heads)
                sin = over_heads(rope[:, t, 1, :], heads)
                a, b, c, d = (r_tmp[:, i, 0:heads, :] for i in range(4))
                dve.tensor_tensor(a, src[:, :, 0:RH], cos, ALU.mult)
                dve.tensor_tensor(b, src[:, :, RH:HD], sin, ALU.mult)
                dve.tensor_tensor(c, src[:, :, RH:HD], cos, ALU.mult)
                link(dve.tensor_tensor(d, src[:, :, 0:RH], sin, ALU.mult))
                dve.tensor_tensor(dst[:, :, 0:RH], a, b, ALU.subtract)
                return dve.tensor_tensor(dst[:, :, RH:HD], c, d, ALU.add)

            for t in range(NT):
                dve.wait_ge(s["sv_copied"], t + 1)
                even = k_pad[:, t, :, :].rearrange("p (g e) c -> p g e c", e=2)
                src = bank(("skv", t))[:, 0:KVH * HD].rearrange("p (h d) -> p h d", h=KVH)
                last = rotate(src, even[:, :, 0, 0:HD], t, KVH)
                take(last, ("skv", t))
                taken(dve, ("skv", t))
                dve.tensor_copy(even[:, :, 1, HD:P], even[:, :, 0, 0:HD]).then_inc(s["k_rotated"], 1)
            for i, (dst, n) in enumerate(((lnc, 66), (convw, 96))):
                full(dve, ("const", i))
                take(dve.tensor_copy(dst[:, 0:n], bank(("const", i))[:, 0:n]), ("const", i))
            for t in range(NT):
                full(dve, ("sq", t))
                dst = q_rot[:, t, :].rearrange("p (h d) -> p h d", h=QH)
                take(rotate(bank(("sq", t))[:, :].rearrange("p (h d) -> p h d", h=QH), dst, t, QH), ("sq", t))
            for n in range(2):
                full(dve, ("a2", n))
                take(dve.tensor_scalar(g_B[:, n, :], bank(("a2", n))[:, :], lnc[:, 64 + n:65 + n], None, ALU.add),
                     ("a2", n))
                taken(dve, ("a2", n))
                dve.scalar_tensor_tensor(g_kd[:, n, :], g_B[:, n, :], -1.0, g_B[:, n, :], ALU.mult, ALU.min)\
                   .then_inc(s["a2_mid"], 1)
            dve.wait_ge(s["a2_exp"], 1)
            link(dve.scalar_tensor_tensor(g_kd[:, :, :], g_B[:, :, :], 0.0, g_e[:, :, :], ALU.min, ALU.subtract))
            for n in range(2):
                dve.tensor_tensor_scan(g_B[:, n, :], g_keep[:, :], g_kd[:, n, :], 0.0, ALU.mult, ALU.add)\
                   .then_inc(s["g_scan"], 1)
            dve.wait_ge(s["g_scan"], 2)
            full(dve, ("kT", NT - 1))
            for n in range(2):
                bv = g_B[:, n, :].rearrange("p (c l) -> p c l", l=CH)
                ins = dve.tensor_tensor(s_p[:, n, :].rearrange("p (c l) -> p c l", l=CH),
                                        bv[:, :, CH - 1:CH].broadcast_to([P, NC, CH]), bv, ALU.subtract)
            ins.then_inc(s["g_gate"], 1)
            dve.wait_ge(s["g_exp"], 1)
            taken(dve, ("gq", 1))
            for e in range(2):
                rows = slice(e * GDK, (e + 1) * GDK)
                dve.tensor_tensor(q_pad[rows, e:GH:2, :], g_q[rows, :, :], g_e[rows, :, :], ALU.mult)\
                   .then_inc(s["q_gated"], 1)
            dve.wait_ge(s["g_exp"], 2)
            taken(dve, ("gk", 1))
            dve.tensor_tensor(g_kd[:, :, :], g_k[:, :, :], s_p[:, :, :], ALU.mult).then_inc(s["k_decayed"], 1)
            dve.wait_ge(s["g_exp"], 3)
            dve.tensor_tensor(g_k[:, :, :], g_k[:, :, :], s_p[:, :, :], ALU.mult).then_inc(s["k_gated"], 1)

            def heads4(ap):
                return ap.rearrange("p (h n) -> p h n", h=4)

            for t in range(NT):
                for g in range(KVH):
                    key = ("score", t, g)
                    hs = slice(4 * g, 4 * g + 4)
                    full(dve, key)
                    if t == 0:
                        link(dve.memset(k4(key)[0:CH, :, 0:CH], NEG))
                    link(dve.tensor_reduce(s_max[:, hs], k4(key), AX, ALU.max))
                    link(dve.scalar_tensor_tensor(s_max[:, hs], s_max[:, hs], HD ** -0.5, sinks[:, hs],
                                                  ALU.mult, ALU.max))
                    take(dve.scalar_tensor_tensor(heads4(s_p[:, g, :]), k4(key), HD ** -0.5,
                                                  across(s_max[:, hs], P), ALU.mult, ALU.subtract), key)
                    dve.tensor_tensor(s_snk[:, hs], sinks[:, hs], s_max[:, hs], ALU.subtract)\
                       .then_inc(s["s_shift"], 1)
                full(dve, ("gattn", t))
                take(dve.copy_predicated(g_at[:, :, :], over_heads(upto[:, :].bitcast(I32), GH), k4(("gattn", t))),
                     ("gattn", t))
                for c in range(2):
                    key = ("gstate", t, c)
                    full(dve, key)
                    v = 2 * t + c
                    for h in range(GH):
                        rows = slice((h % 2) * GDK, (h % 2 + 1) * GDK)
                        col = (2 * t + c + 1) * CH - 1
                        ins = dve.scalar_tensor_tensor(
                            g_S[rows, (v + 1) % 2, h // 2, :], g_S[rows, v % 2, h // 2, :],
                            g_e[rows, h // 2, col:col + 1], bank(key)[rows, h * GDV:(h + 1) * GDV],
                            ALU.mult, ALU.add)
                    take(ins, key)
                    taken(dve, key)
                for g in range(KVH):
                    hs = slice(4 * g, 4 * g + 4)
                    dve.wait_ge(s["s_prob"], KVH * t + g + 1)
                    link(dve.tensor_reduce(s_den[:, hs], heads4(s_p[:, g, :]), AX, ALU.add))
                link(dve.tensor_tensor(s_den[:, :], s_den[:, :], s_snk[:, :], ALU.add))
                link(dve.reciprocal(s_den[:, :], s_den[:, :]))
                taken(dve, ("gr", t))
                dve.tensor_tensor(g_r[:, t, :], g_r[:, t, :], g_norm[:, :], ALU.mult)
                key = ("gout", t)
                full(dve, key)
                og = heads4(o_tm[:, t % 2, 0:512])
                link(dve.tensor_reduce(g_mu[:, :], k4(key), AX, ALU.add))
                link(dve.tensor_scalar(g_mu[:, :], g_mu[:, :], 1.0 / GDV, None, ALU.mult))
                take(dve.tensor_tensor(og, k4(key), across(g_mu[:, :], GDV), ALU.subtract), key)
                taken(dve, key)
                sq = r_tmp[:, 0:2, :, :].rearrange("p a b c -> p (a b c)")
                link(dve.tensor_tensor(sq, o_tm[:, t % 2, 0:512], o_tm[:, t % 2, 0:512], ALU.mult))
                dve.tensor_reduce(g_var[:, :], heads4(sq), AX, ALU.add).then_inc(s["o_var"], 1)
                dve.wait_ge(s["o_rstd"], t + 1)
                link(dve.tensor_tensor(og, og, across(g_var[:, :], GDV), ALU.mult))
                dve.tensor_tensor(o_tm[:, t % 2, 0:512], o_tm[:, t % 2, 0:512], g_r[:, t, :], ALU.mult)\
                   .then_inc(s["o_even"], 1)
                key = ("sout", t)
                full(dve, key)
                take(dve.tensor_tensor(o_tm[:, t % 2, 512:D].rearrange("p (h n) -> p h n", h=QH),
                                       bank(key)[:, :].rearrange("p (h n) -> p h n", h=QH),
                                       across(s_den[:, :], HD), ALU.mult), key)
                if t:
                    round_o(0, t - 1)
            round_o(0, NT - 1)
            layer_norm(1, "mix", 0)
            round_x(1)
            ffn(0)
            layer_norm(2, "down", 0)
            round_x(2)
            low_part_there(dve, 2, KD - 2)
            low_part_there(dve, 2, KD - 1)
            dve.memset(ST[:, :, :].rearrange("p a b -> p (a b)"), 0.0).then_inc(s["state0"], 1)
            for i, n in enumerate(CONV_ORDER):
                key = ("conv", n)
                dve.wait_ge(s["conv_raw"], i + 1)
                full(dve, key)
                for back in range(1, CONV_K):
                    tap = (CONV_K - 1 - back) * 3 * KD + n
                    dst = conv_acc(i)[:, back:]
                    ins = dve.scalar_tensor_tensor(dst, bank(key)[:, 0:SEQ - back], convw[:, tap:tap + 1], dst,
                                                   ALU.mult, ALU.add)
                    if back < CONV_K - 1:
                        link(ins)
                take(ins, key)
                if i == 1:
                    full(dve, ("ba",))
                    take(dve.tensor_copy(ba[:, :, :], bank(("ba",))[:, 0:NT * 2 * GDN_H].rearrange("p (t c) -> p t c", t=NT)),
                         ("ba",))
                    taken(dve, ("ba",))
                    link(dve.tensor_tensor(gdec[:, :, :], ba[:, :, GDN_H:], over_heads(dt_bias[:, :], NT), ALU.add))
                    dve.scalar_tensor_tensor(g_tmp[:, :, :], gdec[:, :, :], -1.0, gdec[:, :, :], ALU.mult, ALU.min)\
                       .then_inc(s["ba_mid"], 1)
                if i == 3:
                    dve.wait_ge(s["ba_exp"], 1)
                    link(dve.tensor_scalar(beta[:, :, :], beta[:, :, :], 1.0, None, ALU.add))
                    link(dve.reciprocal(beta[:, :, :], beta[:, :, :]))
                    link(dve.scalar_tensor_tensor(gdec[:, :, :], gdec[:, :, :], 0.0, g_tmp[:, :, :], ALU.max, ALU.add))
                    dve.scalar_tensor_tensor(gdec[:, :, :], gdec[:, :, :], -1.0, over_heads(a_log[:, :], NT),
                                             ALU.mult, ALU.mult).then_inc(s["g_ready"], 1)
                if i == DECAY_AT:
                    full(dve, ("decay",))
                    take(dve.tensor_copy(dec[:, :, :, :].rearrange("p a t h -> p (a t h)"),
                                         bank(("decay",))[:, 0:2 * TH]), ("decay",))
                    taken(dve, ("decay",))
                    dve.tensor_tensor(to_end[:, :, :], dec[:, 1, :, :], dec[:, 0, :, :], ALU.subtract)\
                       .then_inc(s["dec_ready"], 1)
                if i >= 3 and CONV_ORDER[i - 3] < 2 * KD:
                    m = CONV_ORDER[i - 3]
                    full(dve, ("norm", m))
                    take(dve.tensor_copy(nrm[:, m, :], bank(("norm", m))[:, 0:NT]), ("norm", m))
            dve.wait_ge(s["dec_exp"], 1)
            link(dve.tensor_tensor(bexp[:, :, :], bexp[:, :, :], beta[:, :, :], ALU.mult))
            dve.wait_ge(s["rn_ready"], 1)
            link(dve.tensor_scalar(nrm[:, 0:GDN_H, :], nrm[:, 0:GDN_H, :], float(P) ** -0.5, None, ALU.mult))

            def out_scale(t, hg):
                dve.wait_ge(s["or_ready"], t + 1)
                o = OO[:, hsl[hg], :]
                dve.tensor_tensor(o, o, across(oms[:, hsl[hg]], P), ALU.mult).then_inc(s["o_scaled"], 1)

            def out_square_sum(t):
                for hg in range(2):
                    dve.wait_ge(s["o_sq"], 2 * t + hg + 1)
                    dve.tensor_reduce(oms[:, hsl[hg]], M1[:, hsl[hg], :], AX, ALU.add).then_inc(s["ov_ready"], 1)

            def filler(t, place):
                name = FILLERS.get((t, place))
                if name is not None and name[0] == "mix":
                    add_sublayer(3, *name)

            dve.wait_ge(s["x_affine"], 4 * NT)
            for t in range(NT):
                H = range(2)
                for hg in H:
                    full(dve, ("kTM", t, hg))
                    rk = nrm[:, KD + 4 * hg:KD + 4 * hg + 4, t]
                    take(dve.tensor_tensor(KH[:, hsl[hg], :], k4(("kTM", t, hg)), across(rk, P), ALU.mult),
                         ("kTM", t, hg))
                if t:
                    out_square_sum(t - 1)
                for hg in H:
                    hs = hsl[hg]
                    dve.wait_ge(s["e_ready"], 2 * t + hg + 1)
                    full(dve, ("drow", t, hg))
                    take(dve.tensor_tensor(GU[:, hs, :], k4(("drow", t, hg)), across(dec[:, 0, t, hs], P),
                                           ALU.subtract), ("drow", t, hg))
                    taken(dve, ("drow", t, hg))
                    dve.tensor_tensor(GA[:, hs, :], GU[:, hs, :], over_heads(o_posl[:, :], 4), ALU.add)\
                       .then_inc(s["ga_arg"], 1)
                for hg in H:
                    full(dve, ("vTM", t, hg))
                    take(dve.tensor_tensor(qkv[:, 2 * KD + 4 * hg:2 * KD + 4 * hg + 4, tile_cols[t]],
                                           k4(("vTM", t, hg)), across(beta[:, t, hsl[hg]], P), ALU.mult),
                         ("vTM", t, hg))
                dve.tensor_copy(edl[:, :, :], EE[:, :, CH - 1:P:CH])
                filler(t, 0)
                for hg in H:
                    full(dve, ("gram", t, hg))
                    dve.wait_ge(s["ga_exp"], 2 * t + hg + 1)
                    for h in range(4 * hg, 4 * hg + 4):
                        ins = dve.scalar_tensor_tensor(GA[:, h, :], k4(("gram", t, hg))[:, h % 4, :],
                                                       beta[:, t, h:h + 1], GA[:, h, :], ALU.mult, ALU.mult)
                    take(ins, ("gram", t, hg))
                filler(t, 1)

                def masked(ps, l, hg):
                    lv = LEVELS[l]
                    m = o_lvl[:, l, :].rearrange("p (q b) -> p q b", b=lv).unsqueeze(1)\
                        .broadcast_to([P, 8, CH // 2 // lv, lv])
                    return dve.tensor_tensor(half_product(hg).rearrange("p (g q b) -> p g q b", g=8, b=lv), ps, m,
                                             ALU.mult)

                def level_step(hg, lv, product):
                    sv = upper_halves(SS[:, hsl[hg], :].rearrange("p h c -> p (h c)"), lv)
                    return dve.tensor_tensor(sv, sv, product.rearrange("p (m b) -> p m b", b=lv), ALU.subtract)

                dve.wait_ge(s["eye_ready"], t + 1)
                for hg in H:
                    key = ("at", t, hg)
                    full(dve, key)
                    ps = upper_halves(bank(key)[:, :], 1).rearrange("p (g q) b -> p g q b", g=8)
                    take(masked(ps, 0, hg), key)
                    taken(dve, key)
                    level_step(hg, 1, half_product(hg)).then_inc(s["s0_ready"], 1)
                for l, lv in enumerate(LEVELS[1:], 1):
                    for hg in H:
                        key = ("m1", t, lv, hg)
                        full(dve, key)
                        take(masked(bank(key)[:, 0:4 * CH].rearrange("p (g q b) -> p g q b", g=8, b=lv), l, hg), key)
                    if lv == 2 * QK_AFTER:
                        for hg in H:
                            full(dve, ("qk", t, hg))
                            dve.wait_ge(s["gt_exp"], 2 * t + hg + 1)
                            take(dve.tensor_tensor(GT[:, hsl[hg], :], k4(("qk", t, hg)), GT[:, hsl[hg], :],
                                                   ALU.mult), ("qk", t, hg))
                    for hg in H:
                        key = ("ds", t, lv, hg)
                        full(dve, key)
                        take(level_step(hg, lv, bank(key)[:, 0:4 * CH]), key)
                    if t and lv in (2, 4):
                        out_scale(t - 1, lv // 4)
                    if t and lv == 2 * TURN_AFTER:
                        round_o(1, t - 1)
                for hg in H:
                    hs = hsl[hg]
                    dve.tensor_tensor(M1[:, hs, :], KH[:, hs, :], across(bexp[:, t, hs], P), ALU.mult)\
                       .then_inc(s["kb_ready"], 1)
                for hg in H:
                    hs = hsl[hg]
                    dve.tensor_tensor(KH[:, hs, :], KH[:, hs, :], across(to_end[:, t, hs], P), ALU.mult)\
                       .then_inc(s["kd_ready"], 1)
                dve.wait_ge(s["q_decayed"], 2 * t + 2)
                for c in range(2):
                    rows = slice(c * CH, (c + 1) * CH)
                    old, new = (ST, GA) if c == 0 else (GA, ST)
                    for hg in H:
                        key = ("ws", t, c, hg)
                        full(dve, key)
                        taken(dve, ("u", t, hg))
                        take(dve.tensor_tensor(EE[rows, hsl[hg], :], GU[rows, hsl[hg], :], k4(key)[rows],
                                               ALU.subtract), key)
                    for hg in H:
                        key = ("kv", t, c, hg)
                        full(dve, key)
                        for h in range(4 * hg, 4 * hg + 4):
                            ins = dve.scalar_tensor_tensor(new[:, h, :], old[:, h, :], edl[:, h, c:c + 1],
                                                           k4(key)[:, h % 4, :], ALU.mult, ALU.add)
                        take(ins, key)
                        taken(dve, key)
                for hg in H:
                    key = ("o", t, hg)
                    full(dve, key)
                    take(dve.tensor_tensor(OO[:, hsl[hg], :], k4(key), across(nrm[:, 4 * hg:4 * hg + 4, t], P),
                                           ALU.mult), key)
            out_square_sum(NT - 1)
            for hg in range(2):
                out_scale(NT - 1, hg)
            round_o(1, NT - 1)
            layer_norm(3, "mix", 1)
            round_x(3)
            ffn(1)
            layer_norm(4, "down", 1)
            for t in range(NT):
                dve.wait_ge(s["z_norm"], NT * 3 + t + 1)
                dve.wait_ge(s["ln_landed"], 32 * 4)
                n = 2 * (NT * 3 + t)
                dve.tensor_tensor(x_tm[:, t, :], x_tm[:, t, :], ln_rows[:, 0, :], ALU.mult)\
                   .then_inc(s["x_affine"], 1)
                dve.wait_ge(s["x_affine"], n + 1)
                dve.tensor_tensor(x_tm[:, t, :], x_tm[:, t, :], ln_rows[:, 1, :], ALU.add)\
                   .then_inc(s["x_affine"], 1)

        @block_.tensor
        def _(pe):
            def fill(key):
                u = unit[key]
                if u >= 8:
                    pe.wait_ge(bank_taken[u % 8], u // 8)
                return bank(key)

            def done(ins, key):
                ins.then_inc(bank_full[unit[key] % 8], 1)

            def mm3(out_ap, st, mv_, start, stop):
                pe.matmul(out_ap, st[0], mv_[0], start=start, stop=False)
                pe.matmul(out_ap, st[0], mv_[1], start=False, stop=False)
                return pe.matmul(out_ap, st[1], mv_[0], start=False, stop=stop)

            def weights(b, kk, c0, width):
                n = blocks[b][3]
                at_ = kk * n + c0
                return tuple(w[:, b % 2, at_:at_ + width] for w in (w_hi, w_lo))

            def xcols(k, cols):
                return x_hi[:, k, cols], x_lo[:, k, cols]

            def hcols(k, cols):
                return h_hi[:, k, cols], h_lo[:, k, cols]

            ALL = slice(0, SEQ)

            def fm_block(b, keys, fresh=None, width=P):
                pe.wait_ge(w_lo_ready, b + 1)
                steps = [(n, k) for n in range(len(keys)) for k in range(KD)]
                if fresh is not None:
                    steps = [(n, k) for k in range(KD) for n in range(len(keys))]
                for n, k in steps:
                    if fresh is not None and n == 0:
                        low_part_there(pe, fresh, k)
                    ps = fill(keys[n]) if k == 0 else bank(keys[n])
                    ins = mm3(ps[:, :], weights(b, k, n * P, P), xcols(k, ALL), k == 0, k == KD - 1)
                    if k == KD - 1:
                        done(ins, keys[n])

            def tm_group(name, wait_k, src=xcols, kt=KD, in_turn=False, tiles=range(NT)):
                b = first_block[name]
                while b < NB and blocks[b][0] == name:
                    _, k0, nk, width, _v = blocks[b]
                    pe.wait_ge(w_lo_ready, b + 1)
                    steps = [(kk, t) for kk in range(nk) for t in tiles]
                    if in_turn and k0 + nk == kt:
                        steps = [(kk, t) for t in tiles for kk in range(nk)]
                    waited = -1
                    for kk, t in steps:
                        if kk > waited:
                            wait_k(k0 + kk)
                            waited = kk
                        key = (*name, t)
                        ps = fill(key) if k0 + kk == 0 else bank(key)
                        ins = mm3(ps[:, 0:width], src(k0 + kk, tile_cols[t]), weights(b, kk, 0, width),
                                  k0 + kk == 0, k0 + kk == kt - 1)
                        if k0 + kk == kt - 1:
                            done(ins, key)
                    if k0 + nk < kt:
                        ins.then_inc(w_used, 1)
                    b += 1

            def no_wait(k):
                pass

            def filler(t, place):
                key = FILLERS.get((t, place))
                if key is None:
                    return
                b = first_block[key[:-1]]
                pe.wait_ge(w_lo_ready, b + 2)
                if key[0] == "mix":
                    for i in range(2):
                        taken(pe, ("oT", 1, key[-1], i))
                ps = fill(key)
                for k in range(KD):
                    ins = mm3(ps[:, :], xcols(k, tile_cols[key[-1]]), weights(b + k // 4, k % 4, 0, 512),
                              k == 0, k == KD - 1)
                done(ins, key)

            def turn_x(i):
                for t in range(NT):
                    if i == 0:
                        pe.wait_ge(x_landed[t], 16)
                    else:
                        pe.wait_ge(s["z_norm"], NT * (i - 1) + t + 1)
                    for k in range(KD):
                        ps = fill(("xT", i, k)) if t == 0 else bank(("xT", i, k))
                        ins = pe.transpose(ps[:, tile_cols[t]], x_tm[:, t, k * P:(k + 1) * P], eye[:, :])
                        if t == NT - 1:
                            done(ins, ("xT", i, k))

            def turn_o(layer, t):
                for i in range(2):
                    if layer == 0:
                        pe.wait_ge(s["o_even"], t + 1)
                        taken(pe, ("sout", t))
                    else:
                        pe.wait_ge(s["o_odd"], 2 * t + i + 1)
                    ps = fill(("oT", layer, t, i))
                    for j in range(4):
                        k = 4 * i + j
                        src = o_tm[:, t % 2, k * P:(k + 1) * P] if layer == 0 else OO[:, k, :]
                        ins = pe.transpose(ps[:, j * P:(j + 1) * P], src, eye[:, :])
                    done(ins, ("oT", layer, t, i))

            def mix_and_norm(layer):
                def have(k):
                    taken(pe, ("oT", layer, NT - 1, k // 4))
                for half in range(2):
                    tiles = [t for t in range(NT) if ("mix", layer, half, t) not in FILLERS.values()]
                    tm_group(("mix", layer, half), have, in_turn=half == 1, tiles=tiles)
                turn_x(2 * layer + 1)

            def ffn(layer):
                for f in range(0, KF, 2):
                    fresh = 2 * layer + 1 if f == 0 else None
                    b = first_block[("gate", layer, f)]
                    fm_block(b, [("gate", layer, f), ("gate", layer, f + 1)], fresh)
                    fm_block(b + 1, [("up", layer, f), ("up", layer, f + 1)])

                def have(k):
                    pe.wait_ge(s["h_lo_ready"], layer * KF + k + 1)
                for half in range(2):
                    tm_group(("down", layer, half), have, hcols, KF, in_turn=half == 1)

            pe.wait_ge(s["eye_landed"], 16)
            turn_x(0)
            tm_group(("skv",), lambda k: low_part_there(pe, 0, k))
            pe.wait_ge(consts, 16 * N_CONST)
            for i, (src, n) in enumerate(((vec_rows, 66), (conv_rows, 96))):
                ps = fill(("const", i))
                done(pe.transpose(ps[:, 0:n], src[0:n, :], eye[0:n, 0:n]), ("const", i))
            tm_group(("sq",), no_wait)
            fm_block(first_block[("gq",)], [("gq", 0), ("gq", 1)])
            fm_block(first_block[("gk",)], [("gk", 0), ("gk", 1)])
            fm_block(first_block[("ga",)], [("ga",)])
            for t in range(NT):
                ps = fill(("qT", t))
                taken(pe, ("sq", t))
                for j in range(4):
                    ins = pe.transpose(ps[:, j * P:(j + 1) * P], q_rot[:, t, j * P:(j + 1) * P], eye[:, :])
                done(ins, ("qT", t))
                ps = fill(("kT", t))
                pe.wait_ge(s["k_rotated"], t + 1)
                for j in range(4):
                    ins = pe.transpose(ps[:, j * P:(j + 1) * P], k_pad[:, t, j, :], eye[:, :])
                done(ins, ("kT", t))
            tm_group(("gv",), no_wait)
            taken(pe, ("ga",))
            for n in range(2):
                ps = fill(("a2", n))
                done(pe.matmul(ps[:, :], g_a2[:, n * P:(n + 1) * P], g_ga[:, :], start=True, stop=True), ("a2", n))
            tm_group(("gr",), no_wait)
            pe.wait_ge(s["k_gated"], 1)
            pe.wait_ge(s["k_decayed"], 1)
            pe.wait_ge(s["q_gated"], 2)
            pe.wait_ge(s["sv_shifted"], 32)
            taken(pe, ("kT", NT - 1))
            taken(pe, ("qT", NT - 1))
            taken(pe, ("gv", NT - 1))

            def across_chunks(t, c, ps, start):
                rows = slice(c * CH, (c + 1) * CH)
                cols = slice(t * P + c * CH, t * P + (c + 1) * CH)
                for h in range(GH):
                    pe.matmul(ps[rows, h * GDV:(h + 1) * GDV], q_pad[:, h, cols], g_S[:, c, h // 2, :],
                              start=h == 0, stop=False, skip_group_check=True)

            def chunk_state(t, c):
                rows = slice(c * CH, (c + 1) * CH)
                ps = fill(("gstate", t, c))
                for h in range(GH):
                    ins = pe.matmul(ps[:, h * GDV:(h + 1) * GDV], g_kdt[rows, h // 2, :],
                                    g_v[rows, t, h * GDV:(h + 1) * GDV], start=True, stop=True)
                done(ins, ("gstate", t, c))

            for t in range(NT):
                for g in range(KVH):
                    ps = fill(("score", t, g))
                    for hh in range(4):
                        h = 4 * g + hh
                        for c in range(2):
                            chunk = 2 * t + c
                            ins = pe.matmul(ps[c * CH:(c + 1) * CH, hh * P:(hh + 1) * P],
                                            s_qT[:, h // 2, chunk * CH:(chunk + 1) * CH],
                                            s_kT[:, 2 * g + h % 2, chunk * CH:chunk * CH + 2 * CH],
                                            start=True, stop=True)
                    done(ins, ("score", t, g))
                ps = fill(("kd", t))
                for n in range(2):
                    ins = pe.transpose(ps[:, n * P:(n + 1) * P], g_kd[:, n, tile_cols[t]], eye[:, :])
                done(ins, ("kd", t))
                ps = fill(("gattn", t))
                for h in range(GH):
                    ins = pe.matmul(ps[:, h * P:(h + 1) * P], g_k[:, h // 2, tile_cols[t]],
                                    q_pad[:, h, tile_cols[t]], start=True, stop=True)
                done(ins, ("gattn", t))
                taken(pe, ("kd", t))
                chunk_state(t, 0)
                go = fill(("gout", t))
                if t:
                    taken(pe, ("gstate", t - 1, 1))
                across_chunks(t, 0, go, True)
                chunk_state(t, 1)
                taken(pe, ("gstate", t, 0))
                across_chunks(t, 1, go, True)
                taken(pe, ("gattn", t))
                for h in range(GH):
                    ins = pe.matmul(go[:, h * GDV:(h + 1) * GDV], g_at[:, h, :], g_v[:, t, h * GDV:(h + 1) * GDV],
                                    start=False, stop=h == GH - 1, skip_group_check=True)
                done(ins, ("gout", t))
                for g in range(KVH):
                    pe.wait_ge(s["s_prob"], KVH * t + g + 1)
                    ps = fill(("probT", t, g))
                    for j in range(4):
                        ins = pe.transpose(ps[:, j * P:(j + 1) * P], s_p[:, g, j * P:(j + 1) * P], eye[:, :])
                    done(ins, ("probT", t, g))
                ps = fill(("sout", t))
                for g in range(KVH):
                    taken(pe, ("probT", t, g))
                    for hh in range(4):
                        h = 4 * g + hh
                        for c in range(2):
                            vals = s_vsh if c == 0 else s_v
                            ins = pe.matmul(ps[c * CH:(c + 1) * CH, h * HD:(h + 1) * HD],
                                            s_pT[:, g, hh * P + c * CH:hh * P + (c + 1) * CH],
                                            vals[:, t, g * HD:(g + 1) * HD], start=True, stop=True)
                done(ins, ("sout", t))
                if t:
                    turn_o(0, t - 1)
            turn_o(0, NT - 1)
            mix_and_norm(0)
            ffn(0)
            turn_x(2)
            fm_block(first_block[("conv", KD)], [("conv", KD), ("conv", KD + 1)], fresh=2)
            for i, n in enumerate(CONV_ORDER):
                b = first_block[("conv", n - n % 2)]
                if i >= 2:
                    pe.wait_ge(w_lo_ready, b + 1)
                    ps = fill(("conv", n))
                    for k in range(KD):
                        ins = mm3(ps[:, :], weights(b, k, (n % 2) * P, P), xcols(k, ALL), k == 0, k == KD - 1)
                    done(ins, ("conv", n))
                if i == 1:
                    b = first_block[("ba",)]
                    ps = fill(("ba",))
                    pe.wait_ge(w_lo_ready, b + 1)
                    for t in range(NT):
                        for k in range(KD):
                            ins = mm3(ps[:, t * 2 * GDN_H:(t + 1) * 2 * GDN_H], xcols(k, tile_cols[t]),
                                      weights(b, k, 0, 2 * GDN_H), k == 0, k == KD - 1)
                    done(ins, ("ba",))
                if i == DECAY_AT:
                    ps = fill(("decay",))
                    pe.wait_ge(s["g_ready"], 1)
                    pe.wait_ge(consts, 16 * (N_CONST + N_CONST_ODD))
                    g = gdec[:, :, :].rearrange("p t h -> p (t h)")
                    pe.matmul(ps[:, 0:TH], upto[:, :], g, start=True, stop=True)
                    done(pe.matmul(ps[:, TH:2 * TH], o_block[:, :], g, start=True, stop=True), ("decay",))
                if i >= 2 and CONV_ORDER[i - 2] < 2 * KD:
                    m = CONV_ORDER[i - 2]
                    ps = fill(("norm", m))
                    pe.wait_ge(s["conv_sq"], i - 1)
                    for t in range(NT):
                        ins = pe.matmul(ps[:, t:t + 1], conv_squares(i - 2)[:, tile_cols[t]], ones[:, :],
                                        start=True, stop=True)
                    done(ins, ("norm", m))
            pe.wait_ge(s["conv_silu"], len(CONV_ORDER))

            def per_head(key, fn):
                ps = fill(key)
                for q in range(4):
                    ins = fn(ps[:, q * P:(q + 1) * P], 4 * key[-1] + q)
                done(ins, key)

            def mul(o, a, b_):
                return pe.matmul(o, a, b_, start=True, stop=True)

            for t in range(NT):
                tc_ = tile_cols[t]
                H = range(2)
                for hg in H:
                    per_head(("kTM", t, hg), lambda o, h: pe.transpose(o, qkv[:, KD + h, tc_], eye[:, :]))
                for hg in H:
                    per_head(("vTM", t, hg), lambda o, h: pe.transpose(o, qkv[:, 2 * KD + h, tc_], eye[:, :]))
                for hg in H:
                    pe.wait_ge(s["gu_ready"], 2 * t + hg + 1)
                    ps = fill(("drow", t, hg))
                    done(mul(ps[:, :], ones[:, :].broadcast_to([P, P]),
                             GU[:, hsl[hg], :].rearrange("p a b -> p (a b)")), ("drow", t, hg))
                filler(t, 0)
                for hg in H:
                    taken(pe, ("kTM", t, hg))
                    per_head(("khT", t, hg), lambda o, h: pe.transpose(o, KH[:, h, :], eye[:, :]))
                for hg in H:
                    taken(pe, ("khT", t, hg))
                    per_head(("gram", t, hg), lambda o, h: mul(o, qkv[:, KD + h, tc_], qkv[:, KD + h, tc_]))
                filler(t, 1)
                for hg in H:
                    taken(pe, ("gram", t, hg))
                    per_head(("at", t, hg), lambda o, h: pe.transpose(o, GA[:, h, :], eye[:, :]))
                filler(t, 2)
                for l, lv in enumerate(LEVELS[1:]):
                    for hg in H:
                        if l:
                            taken(pe, ("ds", t, LEVELS[l], hg))
                        else:
                            pe.wait_ge(s["s0_ready"], 2 * t + hg + 1)
                        ps = fill(("m1", t, lv, hg))
                        for q in range(4):
                            ins = mul(ps[:, q * CH:(q + 1) * CH], GA[:, 4 * hg + q, :],
                                      upper_halves(SS[:, 4 * hg + q, :], lv))
                        done(ins, ("m1", t, lv, hg))
                        per_head(("tt", t, lv, hg), lambda o, h: pe.transpose(o, SS[:, h, :], eye[:, :]))
                    for hg in H:
                        taken(pe, ("m1", t, lv, hg))
                        taken(pe, ("tt", t, lv, hg))
                        ps = fill(("ds", t, lv, hg))
                        for q in range(4):
                            ins = mul(ps[:, q * CH:(q + 1) * CH], TT[:, 4 * hg + q, :],
                                      half_product(hg)[:, q * CH:(q + 1) * CH])
                        done(ins, ("ds", t, lv, hg))
                    if lv == QK_AFTER:
                        for hg in H:
                            per_head(("qk", t, hg), lambda o, h: mul(o, qkv[:, KD + h, tc_], qkv[:, h, tc_]))
                    if t and lv == TURN_AFTER:
                        turn_o(1, t - 1)
                filler(t, 3)
                for hg in H:
                    taken(pe, ("ds", t, LEVELS[-1], hg))
                    taken(pe, ("vTM", t, hg))
                    per_head(("u", t, hg), lambda o, h: mul(o, SS[:, h, :], qkv[:, 2 * KD + h, tc_]))
                for hg in H:
                    pe.wait_ge(s["kb_ready"], 2 * t + hg + 1)
                    per_head(("w", t, hg), lambda o, h: mul(o, M1[:, h, :], SS[:, h, :]))
                for c in range(2):
                    rows = slice(c * CH, (c + 1) * CH)
                    state = ST if c == 0 else GA
                    for hg in H:
                        if c:
                            taken(pe, ("kv", t, 0, hg))
                        elif t:
                            taken(pe, ("kv", t - 1, 1, hg))
                        else:
                            pe.wait_ge(s["state0"], 1)
                        taken(pe, ("w", t, hg))
                        per_head(("ws", t, c, hg), lambda o, h: mul(o[rows], TT[:, h, rows], state[:, h, :]))
                    pe.wait_ge(s["q_decayed"], 2 * t + 2)
                    for hg in H:
                        ps = fill(("o", t, hg)) if c == 0 else bank(("o", t, hg))
                        for q in range(4):
                            h = 4 * hg + q
                            cols = slice(t * P + c * CH, t * P + (c + 1) * CH)
                            pe.matmul(ps[rows, q * P:(q + 1) * P], qkv[:, h, cols], state[:, h, :],
                                      start=q == 0, stop=False, skip_group_check=True)
                    for hg in H:
                        taken(pe, ("ws", t, c, hg))
                        pe.wait_ge(s["kd_ready"], 2 * t + hg + 1)
                        per_head(("kv", t, c, hg), lambda o, h: mul(o, KH[rows, h, :], EE[rows, h, :]))
                for hg in H:
                    taken(pe, ("qk", t, hg))
                    ps = bank(("o", t, hg))
                    for q in range(4):
                        h = 4 * hg + q
                        ins = pe.matmul(ps[:, q * P:(q + 1) * P], GT[:, h, :], EE[:, h, :],
                                        start=False, stop=q == 3, skip_group_check=True)
                    done(ins, ("o", t, hg))
            turn_o(1, NT - 1)
            mix_and_norm(1)
            ffn(1)


_INS = ["x", "ev_w_in", "ev_gla_w_a2", "ev_gla_b_a", "ev_gla_norm_g", "ev_swa_sinks", "ev_w_out", "od_w_in",
        "od_conv_w", "od_a_log", "od_dt_bias", "od_norm_g", "od_w_out", "ffn_w_gate", "ffn_w_up", "ffn_w_down",
        "ln1_g", "ln1_b", "ln2_g", "ln2_b"]


def kernel(**inputs):
    import concourse.bacc as bacc
    from concourse.bass_utils import run_bass_kernel_spmd

    nc = bacc.Bacc("TRN2", target_bir_lowering=False, num_devices=1)
    arrays, views = {}, {}
    given = {n: np.ascontiguousarray(inputs[n]) for n in _INS}
    given.update(shape_constants())
    for name, a in given.items():
        arrays[name + "_dram"] = a
        views[name] = nc.dram_tensor(name + "_dram", a.shape, mybir.dt.from_np(a.dtype), kind="ExternalInput").ap()
    out = nc.dram_tensor("out_dram", (1, SEQ, D), F32, kind="ExternalOutput").ap()
    trunk_kernel(nc, views, out)
    r = run_bass_kernel_spmd(nc, [arrays], core_ids=[0])
    return r.results[0]["out_dram"]
```

```python
from contextlib import ExitStack

import numpy as np

import concourse.bass as bass
from concourse import mybir

F32 = mybir.dt.float32
F32R = mybir.dt.float32r
I32 = mybir.dt.int32
ALU = mybir.AluOpType
ACT = mybir.ActivationFunctionType
AX = mybir.AxisListType.X

P = 128
D = 1024
SEQ = 512
NT = SEQ // P
KD = D // P
CH = 64
NC = SEQ // CH
DFF = ((8 * D + 3 * 256 - 1) // (3 * 256)) * 256
KF = DFF // P
ALPHA = 4.0 ** 0.25
LN_EPS = 1e-5
RMS_EPS = 1e-6

GH, GDK, GDV, GRANK, TAU = 4, 64, 128, 16, 16.0
QH, KVH, HD = 8, 2, 64
RH = HD // 2
GDN_H = 8
CONV_K = 4
CONV_CH = 3 * D
NEG = -1e30

GQ0 = 0
GK0 = GQ0 + GH * GDK
GV0 = GK0 + GH * GDK
GA0 = GV0 + GH * GDV
GR0 = GA0 + GRANK
SQ0 = GR0 + GH * GDV
SKV0 = SQ0 + QH * HD
OQ0, OK0, OV0 = 0, D, 2 * D
BA0 = CONV_CH
OG0 = BA0 + 2 * GDN_H

WCOLS = 2048
LEVELS = (1, 2, 4, 8, 16, 32, 64)
QK_AFTER = 2


def shape_constants():
    i = np.arange(P)
    same = (i[:, None] // CH) == (i[None, :] // CH)
    upto = (same & (i[:, None] <= i[None, :])).astype(np.float32)
    neg_t = np.where(i[:, None] <= i[None, :], 0.0, NEG).astype(np.float32)
    pos_l = np.where(i[:, None] > i[None, :], 0.0, -NEG).astype(np.float32)
    r, levels = i[:, None], []
    for b in LEVELS:
        up = np.array([n for n in range(P) if n % (2 * b) >= b])[None, :]
        levels.append((r // (2 * b) == up // (2 * b)) & (r % (2 * b) < b))
    levels = np.concatenate([m.astype(np.float32) for m in levels], 1)
    inv = np.float32(10000.0) ** (-np.arange(RH, dtype=np.float32) / np.float32(RH))
    ang = np.arange(SEQ, dtype=np.float32)[:, None] * inv[None, :]
    rope = np.stack([np.cos(ang), np.sin(ang)], 1).astype(np.float32)
    rope = rope.reshape(NT, P, 2 * RH).transpose(1, 0, 2).reshape(P, -1)
    keep = np.broadcast_to((np.arange(SEQ) % CH != 0).astype(np.float32), (P, SEQ))
    return {
        "c_eye": np.eye(P, dtype=np.float32),
        "c_upto": upto,
        "c_odd": np.ascontiguousarray(np.concatenate([(neg_t == 0.0).astype(np.float32), neg_t, pos_l, levels], 1)),
        "c_rope": np.ascontiguousarray(rope),
        "c_keep": np.ascontiguousarray(keep),
    }


def weight_plan(A):
    blocks = []

    def add(name, w, k0, nk, c0, width):
        view = w[k0 * P:(k0 + nk) * P, c0:c0 + width].rearrange("(k p) n -> p k n", p=P)
        blocks.append((name, k0, nk, width, view))

    def add_tm(name, w, kt, c0, width):
        k0 = 0
        while k0 < kt:
            nk = (kt - k0) % 4 or 4
            add(name, w, k0, nk, c0, width)
            k0 += nk

    ev, od = A["ev_w_in"][0], A["od_w_in"][0]

    def ffn(layer):
        g, u, d = (A[n][layer] for n in ("ffn_w_gate", "ffn_w_up", "ffn_w_down"))
        for f in range(0, KF, 2):
            add(("gate", layer, f), g, 0, KD, f * P, 256)
            add(("up", layer, f), u, 0, KD, f * P, 256)
        for half in range(2):
            add_tm(("down", layer, half), d, KF, half * 512, 512)

    add(("skv",), ev, 0, KD, SKV0, 2 * KVH * HD)
    add_tm(("sq",), ev, KD, SQ0, 512)
    add(("gq",), ev, 0, KD, GQ0, 256)
    add(("gk",), ev, 0, KD, GK0, 256)
    add(("ga",), ev, 0, KD, GA0, P)
    add_tm(("gv",), ev, KD, GV0, 512)
    add_tm(("gr",), ev, KD, GR0, 512)
    for half in range(2):
        add_tm(("mix", 0, half), A["ev_w_out"][0], KD, half * 512, 512)
    ffn(0)
    for part, c0 in ((1, OK0), (0, OQ0), (2, OV0)):
        for n in range(0, KD, 2):
            add(("conv", part * KD + n), od, 0, KD, c0 + n * P, 256)
    for half in range(2):
        add_tm(("og", half), od, KD, OG0 + half * 512, 512)
    for half in range(2):
        add_tm(("mix", 1, half), A["od_w_out"][0], KD, half * 512, 512)
    ffn(1)
    return blocks


DECAY_AT = 5
CONV_ORDER = [part * KD + n for part in (1, 0, 2) for n in range(KD)]


FILLERS = {(0, -1): ("og", 0, 0), (0, 0): ("og", 0, 1), (0, 1): ("og", 0, 2), (0, 2): ("og", 0, 3),
           (1, 0): ("og", 1, 0), (1, 1): ("og", 1, 1), (2, 0): ("og", 1, 2), (2, 1): ("og", 1, 3),
           (3, 0): ("mix", 1, 0, 0), (3, 1): ("mix", 1, 0, 1)}
TAIL_FILLERS = {0: [("mix", 0, 0, 0), ("mix", 0, 0, 1)], 1: [("mix", 1, 0, 2)]}
FILLED = set(FILLERS.values()) | set(TAIL_FILLERS[0]) | set(TAIL_FILLERS[1])
OG_ORDER = [FILLERS[k] for k in sorted(FILLERS) if FILLERS[k][0] == "og"]


def unit_plan():
    u = []
    tiles = range(NT)

    def ln(i):
        u.extend(("xT", i, k) for k in range(KD))

    def ffn(layer):
        for f in range(0, KF, 2):
            u.extend([("gate", layer, f), ("gate", layer, f + 1), ("up", layer, f), ("up", layer, f + 1)])
        for half in range(2):
            u.extend(("down", layer, half, t) for t in tiles)

    ln(0)
    u += [("skv", t) for t in tiles] + [("const", 0), ("const", 1)] + [("sq", t) for t in tiles]
    u += [("gq", 0), ("gq", 1), ("gk", 0), ("gk", 1), ("ga",)]
    for t in tiles:
        u += [("qT", t), ("kT", t)]
    u += [("a2", 0), ("a2", 1)] + [("gv", t) for t in tiles]
    for t in tiles:
        u += [("score", t, 0), ("score", t, 1), ("kd", t), ("gr", t), ("gattn", t), ("gstate", t, 0), ("gout", t),
              ("gstate", t, 1), ("probT", t, 0), ("probT", t, 1), ("sout", t)]
        if t:
            u += [("oT", 0, t - 1, 0), ("oT", 0, t - 1, 1)]
    u += TAIL_FILLERS[0] + [("oT", 0, NT - 1, 0), ("oT", 0, NT - 1, 1)]
    u += [("mix", 0, half, t) for half in range(2) for t in tiles if ("mix", 0, half, t) not in FILLED]
    ln(1)
    ffn(0)
    ln(2)
    for i, n in enumerate(CONV_ORDER):
        u.append(("conv", n))
        if i == 1:
            u.append(("ba_fm",))
        if i == 2:
            u.append(("ba",))
        if i == DECAY_AT:
            u.append(("decay",))
        if i >= 2 and CONV_ORDER[i - 2] < 2 * KD:
            u.append(("norm", CONV_ORDER[i - 2]))
    for t in tiles:
        def filler(place):
            return [FILLERS[t, place]] if (t, place) in FILLERS else []

        def both(*names):
            return [(name, t, hg) for name in names for hg in range(2)]

        u += filler(-1) + both("kTM", "vTM", "drow") + filler(0) + both("khT", "gram") + filler(1) + both("at") + filler(2)
        for b in LEVELS[1:]:
            for hg in range(2):
                u += [("m1", t, b, hg), ("tt", t, b, hg)]
            u += [("ds", t, b, 0), ("ds", t, b, 1)]
            if b == QK_AFTER:
                u += both("qk")
            if b == 8:
                u += filler(3)
        u += ([("oT", 1, t - 1, 0), ("oT", 1, t - 1, 1)] if t else []) + both("u", "w")
        u += both("ws", "o") + (both("kv") if t < NT - 1 else [])
    u += TAIL_FILLERS[1] + [("oT", 1, NT - 1, 0), ("oT", 1, NT - 1, 1)]
    u += [("mix", 1, half, t) for half in range(2) for t in tiles if ("mix", 1, half, t) not in FILLED]
    ln(3)
    ffn(1)
    return {key: i for i, key in enumerate(u)}


def trunk_kernel(nc, A, out):
    blocks = weight_plan(A)
    NB = len(blocks)
    unit = unit_plan()
    first_block = {}
    for b, blk in enumerate(blocks):
        first_block.setdefault(blk[0], b)

    ctx = ExitStack()
    with ctx:
        base = (nc.sbuf_base + 63) // 64 * 64
        here = [base]

        def sb(name, shape, dt=F32, at=None):
            size = (int(np.prod(shape[1:])) * 4 + 31) // 32 * 32
            off = here[0] if at is None else at
            if at is None:
                here[0] += size
            assert off + size <= nc.sbuf_usable_end, (name, off + size)
            return nc.alloc_sbuf_tensor_at(name, shape, dt, offset=off)

        w_raw = sb("w_raw", [P, 2, WCOLS])
        w_hi = sb("w_hi", [P, 2, WCOLS], F32R)
        w_lo = sb("w_lo", [P, 2, WCOLS], F32R)
        x_hi = sb("x_hi", [P, KD, SEQ], F32R)
        x_lo = sb("x_lo", [P, KD, SEQ], F32R)
        x_tm = sb("x_tm", [P, NT, D])
        eye = sb("eye", [P, P])
        small0 = here[0]
        lnc = sb("lnc", [P, 66])
        convw = sb("convw", [P, CONV_K * 3 * KD])
        sinks = sb("sinks", [P, QH])
        a_log = sb("a_log", [P, GDN_H])
        dt_bias = sb("dt_bias", [P, GDN_H])
        onorm_row = sb("onorm_row", [P, P])
        stats = sb("stats", [P, NT, 2, 6])
        mv = sb("mv", [P, NT, 2])
        rstd = sb("rstd", [P, NT])
        TH = NT * GDN_H
        ba = sb("ba", [P, NT, 2 * GDN_H])
        beta = sb("beta", [P, NT, GDN_H])
        gdec = sb("gdec", [P, NT, GDN_H])
        g_tmp = sb("g_tmp", [P, NT, GDN_H])
        dec = sb("dec", [P, 2, NT, GDN_H])
        to_end = sb("to_end", [P, NT, GDN_H])
        bexp = sb("bexp", [P, NT, GDN_H])
        nrm = sb("nrm", [P, 2 * KD, NT])
        edl = sb("edl", [P, GDN_H])
        oms = sb("oms", [P, GDN_H])
        ones = sb("ones", [P, 1])
        eps = sb("eps", [P, 2])
        s_max = sb("s_max", [P, QH])
        s_snk = sb("s_snk", [P, QH])
        s_den = sb("s_den", [P, QH])
        g_mu = sb("g_mu", [P, GH])
        g_var = sb("g_var", [P, GH])
        ARENA = here[0]

        q_pad = sb("q_pad", [P, GH, SEQ])
        g_q = sb("g_q", [P, 2, SEQ])
        g_k = sb("g_k", [P, 2, SEQ])
        g_kd = sb("g_kd", [P, 2, SEQ])
        g_B = sb("g_B", [P, 2, SEQ])
        g_e = sb("g_e", [P, 2, SEQ])
        g_v = sb("g_v", [P, NT, GH * GDV])
        g_r = sb("g_r", [P, NT, GH * GDV])
        g_ga = sb("g_ga", [GRANK, SEQ])
        g_a2 = sb("g_a2", [GRANK, GH * GDK])
        g_keep = sb("g_keep", [P, SEQ])
        g_norm = sb("g_norm", [P, GH * GDV])
        g_at = sb("g_at", [P, GH, P])
        g_kdt = sb("g_kdt", [P, 2, P])
        upto = sb("upto", [P, P])
        g_S = sb("g_S", [P, 2, 2, GDV])
        rope = sb("rope", [P, NT, 2, RH])
        r_tmp = sb("r_tmp", [P, 4, QH, RH])
        s_v = sb("s_v", [P, NT, KVH * HD])
        s_vsh = sb("s_vsh", [P, NT, KVH * HD])
        s_qT = sb("s_qT", [P, QH // 2, SEQ])
        s_kT = sb("s_kT", [P, 2 * KVH, CH + SEQ])
        q_rot_at = here[0]
        q_rot = sb("q_rot", [P, NT, QH * HD])
        k_pad = sb("k_pad", [P, NT, 2 * KVH, P])
        s_p = sb("s_p", [P, 2, 512], at=q_rot_at)
        s_pT = sb("s_pT", [P, 2, 512], at=q_rot_at + 4096)
        o_tm = sb("o_tm", [P, 2, D], at=q_rot_at + 8192)

        here[0] = ARENA
        h_hi = sb("h_hi", [P, KF, SEQ], F32R)
        h_lo = sb("h_lo", [P, KF, SEQ], F32R)
        ln_rows = sb("ln_rows", [P, 2, D])
        f_ab = sb("f_ab", [P, 4, SEQ])
        rows_at = ARENA + 2 * KF * SEQ * 4
        vec_rows = sb("vec_rows", [P, P], at=rows_at)
        conv_rows = sb("conv_rows", [P, P], at=rows_at + 512)

        here[0] = ARENA
        qkv = sb("qkv", [P, 3 * KD, SEQ])
        gate_s = sb("gate_s", [P, NT, D])
        o_upto = sb("o_upto", [P, P])
        o_negt = sb("o_negt", [P, P])
        o_posl = sb("o_posl", [P, P])
        o_lvl = sb("o_lvl", [P, len(LEVELS), P // 2])
        KH = sb("KH", [P, GDN_H, P])
        GU = sb("GU", [P, GDN_H, P])
        BA = 2 * GDN_H
        ba_raw = sb("ba_raw", [P, KD, P], at=here[0])
        ba_hi = sb("ba_hi", [P, KD, P], F32R, at=here[0] + KD * P * 4)
        ba_lo = sb("ba_lo", [P, KD, P], F32R, at=here[0] + 2 * KD * P * 4)
        ba_fm = sb("ba_fm", [BA, SEQ], at=here[0])
        EE = sb("EE", [P, GDN_H, P])
        GT = sb("GT", [P, GDN_H, P])
        GA = sb("GA", [P, GDN_H, P])
        TT = sb("TT", [P, GDN_H, P])
        SS = sb("SS", [P, GDN_H, P])
        M1 = sb("M1", [P, GDN_H, P])
        ST = sb("ST", [P, GDN_H, P])
        OO = sb("OO", [P, GDN_H, P])

        banks = [ctx.enter_context(nc.psum_tensor(f"bank{i}", [P, 512], F32)) for i in range(8)]

        def sem(name):
            return ctx.enter_context(nc.semaphore(name))

        bank_full = [sem(f"bank_full{i}") for i in range(8)]
        bank_taken = [sem(f"bank_taken{i}") for i in range(8)]
        w_landed = [sem(f"w_landed{i}") for i in range(2)]
        x_landed = [sem(f"x_landed{t}") for t in range(NT)]
        y_ready = [sem(f"y_ready{t}") for t in range(NT)]
        w_hi_ready = sem("w_hi_ready")
        w_lo_ready = sem("w_lo_ready")
        w_used = sem("w_used")
        consts = sem("consts")
        zeroed = sem("zeroed")

        def bank(key):
            return banks[unit[key] % 8]

        def full(e, key):
            if e is nc.vector or e is nc.scalar:
                e.drain()
            e.wait_ge(bank_full[unit[key] % 8], unit[key] // 8 + 1)

        def taken(e, key):
            e.wait_ge(bank_taken[unit[key] % 8], unit[key] // 8 + 1)

        def take(ins, key):
            ins.then_inc(bank_taken[unit[key] % 8], 1)

        def half_cols(b, half):
            _, _, nk, width, _v = blocks[b]
            return slice(0, nk // 2 * width) if half == 0 else slice(nk // 2 * width, nk * width)

        def low_part_there(e, i, k):
            e.wait_ge(s[("x_lo_even", "x_lo_odd")[k % 2]], KD // 2 * i + k // 2 + 1)

        block_end = []
        count = 0
        for b, (name, k0, nk, width, _) in enumerate(blocks):
            last = b + 1 == NB or blocks[b + 1][0] != name
            if name[0] in ("og", "gr"):
                key = max((*name, t) for t in range(NT))
                block_end.append((bank_full[unit[key] % 8], unit[key] // 8 + 1))
            elif not last:
                count += 1
                block_end.append((w_used, count))
            else:
                key = {"skv": ("skv", NT - 1), "sq": ("sq", NT - 1), "gv": ("gv", NT - 1), "gr": ("gr", NT - 1),
                       "gq": ("gq", 1), "gk": ("gk", 1), "ga": ("ga",)}.get(name[0])
                if name[0] in ("gate", "up"):
                    key = (name[0], name[1], name[2] + 1)
                elif name[0] == "conv":
                    key = ("conv", name[1] + 1)
                elif key is None:
                    key = (*name, NT - 1)
                block_end.append((bank_full[unit[key] % 8], unit[key] // 8 + 1))

        s = {n: sem(n) for n in (
            "eye_landed", "ln_landed", "x_hi_ready", "x_lo_even", "x_lo_odd", "z_norm", "half_stats", "ln_stat", "ln_var",
            "x_affine", "out_sent", "act_step", "dve_step", "o_hi_ready", "h_hi_ready", "h_lo_ready",
            "sv_copied", "sv_shifted", "k_rotated", "a2_exp", "a2_mid", "g_scan", "g_exp", "g_gate",
            "k_decayed", "q_gated", "k_gated", "s_shift", "s_prob", "o_var", "o_rstd", "o_even", "gr_ready",
            "ba_landed", "ba_hi_ready", "ba_lo_ready", "ba_exp", "ba_mid", "g_ready", "dec_ready", "dec_exp", "conv_raw", "conv_silu",
            "conv_sq", "rn_ready", "gu_ready", "e_ready", "ga_arg", "gt_arg", "ga_exp", "gt_exp", "gate_ready", "eye_ready", "s0_ready", "o_sq",
            "q_decayed", "kb_ready", "kd_ready", "state0", "ov_ready", "or_ready", "o_scaled", "o_odd",
        )}

        block_ = ctx.enter_context(nc.Block())
        Q4 = GDN_H // 2
        HALF = P // 2
        def conv_acc(i):
            return KH[:, 4 * (i % 2):4 * (i % 2) + 4, :].rearrange("p a b -> p (a b)")

        def upper_halves(ap, b):
            return ap.rearrange("p (m two b) -> p m two b", two=2, b=b)[:, :, 1, :]

        def half_product(hg):
            return M1[:, 2 * hg:2 * hg + 2, :].rearrange("p a b -> p (a b)")

        def conv_squares(i):
            return GU[:, 4 * (i % 2):4 * (i % 2) + 4, :].rearrange("p a b -> p (a b)")

        SPLIT_IN = {("og", 1): 0, ("mix", 1, 0): 2}
        SPLIT_AT = (4, 8)
        tile_cols = [slice(t * P, (t + 1) * P) for t in range(NT)]
        hsl = [slice(0, Q4), slice(Q4, GDN_H)]
        N_CONST, N_CONST_ODD = 15, 4

        @block_.sync
        def _(sp):
            def load_block(b):
                name, k0, nk, width, view = blocks[b]
                if b >= 2:
                    sp.wait_ge(w_lo_ready, 2 * (b - 1))
                dst = w_raw[:, b % 2, 0:nk * width].rearrange("p (k n) -> p k n", k=nk)
                sp.dma_start(dst, view).then_inc(w_landed[b % 2], 16)

            load_block(0)
            sp.dma_start(eye[:, :], A["c_eye"]).then_inc(s["eye_landed"], 16)
            for t in range(NT):
                sp.dma_start(x_tm[:, t, :], A["x"][0, t * P:(t + 1) * P, :]).then_inc(x_landed[t], 16)
            load_block(1)
            small = [(upto[:, :], A["c_upto"])]
            for i, nm in enumerate(("ln1_g", "ln1_b", "ln2_g", "ln2_b")):
                small.append((vec_rows[16 * i:16 * i + 16, :], A[nm].rearrange("l (k p) -> (l k) p", p=P)))
            small.append((vec_rows[64:66, :], A["ev_gla_b_a"].rearrange("l (k p) -> (l k) p", p=P)))
            small.append((conv_rows[0:96, :], A["od_conv_w"][0].rearrange("c (n p) -> (c n) p", p=P)))
            small.append((sinks[:, :], A["ev_swa_sinks"][0:1, :].broadcast_to([P, QH])))
            small.append((a_log[:, :], A["od_a_log"][0:1, :].broadcast_to([P, GDN_H])))
            small.append((dt_bias[:, :], A["od_dt_bias"][0:1, :].broadcast_to([P, GDN_H])))
            small.append((onorm_row[:, :], A["od_norm_g"][0:1, :].broadcast_to([P, P])))
            small.append((g_a2[:, :], A["ev_gla_w_a2"][0]))
            small.append((g_keep[:, :], A["c_keep"]))
            small.append((g_norm[:, :], A["ev_gla_norm_g"][0:1, :].broadcast_to([P, GH * GDV])))
            small.append((rope[:, :, :, :], A["c_rope"].rearrange("p (t c r) -> p t c r", t=NT, c=2)))
            for dst, src in small:
                sp.dma_start(dst, src).then_inc(consts, 16)
            assert len(small) == N_CONST

            def load_until(b):
                while at[0] < b:
                    load_block(at[0])
                    at[0] += 1

            def load_ln(i):
                g, v = (("ln1_g", "ln1_b"), ("ln2_g", "ln2_b"))[(i + 1) % 2]
                layer = (i - 1) // 2
                for j, nm in enumerate((g, v)):
                    sp.dma_start(ln_rows[:, j, :], A[nm][layer:layer + 1, :].broadcast_to([P, D]))\
                      .then_inc(s["ln_landed"], 16)

            at = [2]
            load_until(first_block[("gate", 0, 0)] + 1)
            taken(sp, ("oT", 0, NT - 1, 1))
            load_ln(1)
            load_until(first_block[("down", 0, 1)])
            sp.wait_ge(s["x_affine"], 2 * NT)
            load_ln(2)
            load_until(first_block[("gate", 1, 0)] + 1)
            taken(sp, ("oT", 1, NT - 1, 1))
            load_ln(3)
            load_until(first_block[("down", 1, 1)])
            sp.wait_ge(s["x_affine"], 6 * NT)
            load_ln(4)
            load_until(NB)
            for t in range(NT):
                sp.wait_ge(y_ready[t], 2)
                sp.dma_start(out[0, t * P:(t + 1) * P, :], x_tm[:, t, :]).then_inc(s["out_sent"], 16)
            sp.wait_ge(s["out_sent"], 16 * NT)

        @block_.gpsimd
        def _(pool):
            def split_lo(b):
                name, k0, nk, width, _v = blocks[b]
                for half in range(2):
                    c = half_cols(b, half)
                    pool.wait_ge(w_hi_ready, 2 * b + half + 1)
                    pool.tensor_tensor(w_lo[:, b % 2, c], w_raw[:, b % 2, c], w_hi[:, b % 2, c].bitcast(F32),
                                       ALU.subtract).then_inc(w_lo_ready, 1)

            def low_parts(i):
                for k in range(1, KD, 2):
                    pool.wait_ge(s["x_hi_ready"], KD * i + k + 1)
                    pool.tensor_tensor(x_lo[:, k, :], f_ab[:, k % 4, :], x_hi[:, k, :].bitcast(F32), ALU.subtract)\
                        .then_inc(s["x_lo_odd"], 1)

            pool.memset(q_pad[:, :, :], 0.0).then_inc(zeroed, 1)
            pool.memset(g_at[:, :, :], 0.0).then_inc(zeroed, 1)
            pool.memset(g_S[:, :, :, :], 0.0).then_inc(zeroed, 1)
            pool.memset(s_kT[:, :, 0:CH], 0.0).then_inc(zeroed, 1)
            pool.memset(s_vsh[:, :, :], 0.0).then_inc(zeroed, 1)
            pool.memset(ones[:, :], 1.0).then_inc(zeroed, 1)
            pool.memset(eps[:, 0:1], LN_EPS).then_inc(zeroed, 1)
            pool.memset(eps[:, 1:2], RMS_EPS).then_inc(zeroed, 1)
            affine, turned = {}, {}
            for i, name in ((1, ("gate", 0, 0)), (2, ("conv", KD)), (3, ("gate", 1, 0))):
                turned[first_block[name]] = i
                for t in range(NT):
                    affine[first_block[name] + 1 + t] = (i, t)
            def gate_times_norm(place, t):
                name = FILLERS.get((t, place))
                if name is not None and name[0] == "og":
                    taken(pool, name)
                    gs = gate_s[:, name[2], name[1] * 512:(name[1] + 1) * 512].rearrange("p (h n) -> p h n", h=4)
                    pool.tensor_tensor(gs, gs, onorm_row[:, :].unsqueeze(1).broadcast_to([P, 4, P]), ALU.mult)\
                        .then_inc(s["gate_ready"], 1)

            def gate_output(t):
                for hg in range(2):
                    pool.wait_ge(s["o_scaled"], 2 * t + hg + 1)
                    pool.wait_ge(s["gate_ready"], OG_ORDER.index(("og", hg, t)) + 1)
                    o = OO[:, hsl[hg], :]
                    gs = gate_s[:, t, hg * 512:(hg + 1) * 512].rearrange("p (h n) -> p h n", h=4)
                    pool.tensor_tensor(o, o, gs, ALU.mult).then_inc(s["o_odd"], 1)

            def prepare(t):
                if t:
                    full(pool, ("w", t - 1, 1))
                else:
                    full(pool, ("norm", CONV_ORDER[2 * KD - 1]))
                for hg in range(2):
                    if t:
                        taken(pool, ("ws", t - 1, hg))
                    hs = hsl[hg]
                    pool.tensor_tensor(GU[:, hs, :], o_upto[:, :].unsqueeze(1).broadcast_to([P, 4, P]),
                                       gdec[:, t, hs].unsqueeze(2).broadcast_to([P, 4, P]), ALU.mult)\
                        .then_inc(s["gu_ready"], 1)
                pool.tensor_copy(SS[:, :, :], eye[:, :].unsqueeze(1).broadcast_to([P, GDN_H, P]))\
                    .then_inc(s["eye_ready"], 1)

            def delta_rule():
                pool.wait_ge(consts, 16 * (N_CONST + N_CONST_ODD))
                pool.wait_ge(s["x_affine"], 4 * NT)
                prepare(0)
                for t in range(NT):
                    for hg in range(2):
                        taken(pool, ("drow", t, hg))
                        pool.tensor_tensor(GT[:, hsl[hg], :], GU[:, hsl[hg], :],
                                           o_negt[:, :].unsqueeze(1).broadcast_to([P, 4, P]), ALU.add)\
                            .then_inc(s["gt_arg"], 1)
                    for place in range(-1, 3):
                        gate_times_norm(place, t)
                    for hg in range(2):
                        full(pool, ("qk", t, hg))
                        pool.wait_ge(s["e_ready"], 2 * t + hg + 1)
                        q = qkv[:, 4 * hg:4 * hg + 4, tile_cols[t]]
                        pool.tensor_tensor(q, q, EE[:, hsl[hg], :], ALU.mult).then_inc(s["q_decayed"], 1)
                    if t:
                        gate_output(t - 1)
                    gate_times_norm(3, t)
                    for name in (("og", 1), ("mix", 1, 0)):
                        if t == SPLIT_IN[name]:
                            split_lo(first_block[name])
                            split_lo(first_block[name] + 1)
                    if t + 1 < NT:
                        prepare(t + 1)
                gate_output(NT - 1)

            for b in range(NB):
                if first_block[("og", 1)] <= b < first_block[("mix", 1, 1)]:
                    continue
                split_lo(b)
                if b == first_block[("gr",)] + 1:
                    for t in range(NT):
                        taken(pool, ("gr", t))
                        pool.tensor_tensor(g_r[:, t, :], g_r[:, t, :], g_norm[:, :], ALU.mult)\
                            .then_inc(s["gr_ready"], 1)
                if b in turned:
                    low_parts(turned[b])
                    if turned[b] == 2:
                        pool.wait_ge(s["ba_hi_ready"], 1)
                        pool.tensor_tensor(ba_lo[:, :, :], ba_raw[:, :, :], ba_hi[:, :, :].bitcast(F32), ALU.subtract)\
                            .then_inc(s["ba_lo_ready"], 1)
                if b in affine:
                    i, t = affine[b]
                    n = 2 * (NT * (i - 1) + t)
                    full(pool, ("xT", i, KD - 1))
                    pool.wait_ge(s["ln_landed"], 32 * i)
                    pool.tensor_tensor(x_tm[:, t, :], x_tm[:, t, :], ln_rows[:, 0, :], ALU.mult)\
                        .then_inc(s["x_affine"], 1)
                    pool.wait_ge(s["x_affine"], n + 1)
                    pool.tensor_tensor(x_tm[:, t, :], x_tm[:, t, :], ln_rows[:, 1, :], ALU.add)\
                        .then_inc(s["x_affine"], 1)
                if b + 1 == first_block[("og", 1)]:
                    delta_rule()
            pool.wait_ge(s["ln_landed"], 32 * 4)
            for t in range(NT // 2):
                pool.wait_ge(s["z_norm"], NT * 3 + t + 1)
                pool.tensor_tensor(x_tm[:, t, :], x_tm[:, t, :], ln_rows[:, 0, :], ALU.mult).then_inc(y_ready[t], 1)
                pool.wait_ge(y_ready[t], 1)
                pool.tensor_tensor(x_tm[:, t, :], x_tm[:, t, :], ln_rows[:, 1, :], ALU.add).then_inc(y_ready[t], 1)

        @block_.scalar
        def _(act):
            steps = [0]
            split = [0]

            def link(ins):
                steps[0] += 1
                ins.then_inc(s["act_step"], 1)
                act.wait_ge(s["act_step"], steps[0])

            def split_to(b):
                while split[0] <= min(b, NB - 1):
                    i = split[0]
                    act.wait_ge(w_landed[i % 2], 16 * (i // 2 + 1))
                    if i >= 2:
                        act.wait_ge(*block_end[i - 2])
                        act.wait_ge(w_lo_ready, 2 * (i - 1))
                    for half in range(2):
                        c = half_cols(i, half)
                        act.activation(w_hi[:, i % 2, c], w_raw[:, i % 2, c], ACT.Copy).then_inc(w_hi_ready, 1)
                    split[0] += 1

            def round_x(i):
                for k in range(KD):
                    if i == 0 and k == 3:
                        split_to(first_block[("sq",)])
                    taken(act, ("xT", i, k))
                    act.activation(x_hi[:, k, :], f_ab[:, k % 4, :], ACT.Copy).then_inc(s["x_hi_ready"], 1)

            def layer_norm(i):
                for t in range(NT):
                    act.wait_ge(s["ln_var"], NT * (i - 1) + t + 1)
                    act.activation(rstd[:, t:t + 1], mv[:, t, 1:2], ACT.Sqrt, bias=eps[:, 0:1])\
                       .then_inc(s["ln_stat"], 1)

            def round_o(layer, t):
                for i in range(2):
                    full(act, ("oT", layer, t, i))
                    act.activation(x_hi[:, 4 * i:4 * i + 4, tile_cols[t]], fm4(("oT", layer, t, i)),
                                   ACT.Copy).then_inc(s["o_hi_ready"], 1)

            def ffn(layer):
                for f in range(0, KF, 2):
                    b = first_block[("gate", layer, f)]
                    split_to(b + 1)
                    for j in range(2):
                        full(act, ("gate", layer, f + j))
                        if f:
                            taken(act, ("up", layer, f + j - 2))
                        take(act.activation(f_ab[:, j, :], bank(("gate", layer, f + j))[:, :], ACT.Silu),
                             ("gate", layer, f + j))
                    split_to(b + 2)
                    for j in range(2):
                        taken(act, ("up", layer, f + j))
                        act.activation(h_hi[:, f + j, :], f_ab[:, 2 + j, :], ACT.Copy).then_inc(s["h_hi_ready"], 1)
                    split_to(b + 3)

            def fm4(key):
                return bank(key)[:, :].rearrange("p (k n) -> p k n", k=4)

            act.wait_ge(zeroed, 8)
            split_to(0)
            round_x(0)
            for t in range(NT):
                full(act, ("skv", t))
                act.activation(s_v[:, t, :], bank(("skv", t))[:, KVH * HD:2 * KVH * HD], ACT.Copy)\
                   .then_inc(s["sv_copied"], 1)
            split_to(first_block[("sq",)] + 1)
            act.wait_ge(s["sv_copied"], NT)
            act.dma_start(s_vsh[CH:P, :, :], s_v[0:CH, :, :]).then_inc(s["sv_shifted"], 16)
            act.dma_start(s_vsh[0:CH, 1:NT, :], s_v[CH:P, 0:NT - 1, :]).then_inc(s["sv_shifted"], 16)
            split_to(first_block[("gk",)])
            for n in range(2):
                full(act, ("gq", n))
                take(act.activation(g_q[:, n, :], bank(("gq", n))[:, :], ACT.Copy, scale=GDK ** -0.5), ("gq", n))
            split_to(first_block[("ga",)])
            for n in range(2):
                full(act, ("gk", n))
                take(act.activation(g_k[:, n, :], bank(("gk", n))[:, :], ACT.Copy), ("gk", n))
            split_to(first_block[("gv",)])
            full(act, ("ga",))
            take(act.activation(g_ga[:, :], bank(("ga",))[0:GRANK, :], ACT.Copy), ("ga",))
            split_to(first_block[("gv",)] + 1)
            for t in range(NT):
                full(act, ("qT", t))
                take(act.activation(s_qT[:, :, tile_cols[t]], fm4(("qT", t)), ACT.Copy), ("qT", t))
                full(act, ("kT", t))
                take(act.activation(s_kT[:, :, CH + t * P:CH + (t + 1) * P], fm4(("kT", t)), ACT.Copy), ("kT", t))
            act.wait_ge(s["a2_mid"], 2)
            link(act.activation(g_e[:, :, :], g_kd[:, :, :], ACT.Exp))
            act.activation(g_e[:, :, :], g_e[:, :, :], ACT.Ln, bias=1.0).then_inc(s["a2_exp"], 1)
            act.wait_ge(s["g_scan"], 2)
            act.activation(g_e[:, :, :], g_B[:, :, :], ACT.Exp, scale=1.0 / TAU).then_inc(s["g_exp"], 1)
            act.wait_ge(s["g_gate"], 1)
            act.activation(s_p[:, :, :], s_p[:, :, :], ACT.Exp, scale=1.0 / TAU).then_inc(s["g_exp"], 1)
            act.wait_ge(s["k_decayed"], 1)
            act.activation(s_p[:, :, :], g_B[:, :, :], ACT.Exp, scale=-1.0 / TAU).then_inc(s["g_exp"], 1)
            split_to(first_block[("gr",)])
            for t in range(NT):
                full(act, ("gv", t))
                take(act.activation(g_v[:, t, :], bank(("gv", t))[:, :], ACT.Copy), ("gv", t))
            split_to(first_block[("gr",)] + 1)
            for t in range(NT):
                full(act, ("kd", t))
                take(act.activation(g_kdt[:, :, :], bank(("kd", t))[:, 0:2 * P].rearrange("p (k n) -> p k n", k=2),
                                    ACT.Copy), ("kd", t))
                for g in range(KVH):
                    act.wait_ge(s["s_shift"], KVH * t + g + 1)
                    act.activation(s_snk[:, 4 * g:4 * g + 4], s_snk[:, 4 * g:4 * g + 4], ACT.Exp)
                    act.activation(s_p[:, g, :], s_p[:, g, :], ACT.Exp).then_inc(s["s_prob"], 1)
                full(act, ("gr", t))
                take(act.activation(g_r[:, t, :], bank(("gr", t))[:, :], ACT.Silu), ("gr", t))
                if t == NT - 1:
                    split_to(first_block[("mix", 0, 0)])
                for g in range(KVH):
                    full(act, ("probT", t, g))
                    take(act.activation(s_pT[:, g, :], bank(("probT", t, g))[:, :], ACT.Copy), ("probT", t, g))
                if t == NT - 1:
                    split_to(first_block[("mix", 0, 0)] + 1)
                act.wait_ge(s["o_var"], t + 1)
                act.activation(g_var[:, :], g_var[:, :], ACT.Sqrt, scale=1.0 / GDV, bias=eps[:, 0:1])\
                   .then_inc(s["o_rstd"], 1)
                if t:
                    round_o(0, t - 1)
            round_o(0, NT - 1)
            split_to(first_block[("mix", 0, 1)])
            full(act, ("mix", 0, 0, NT - 1))
            split_to(first_block[("gate", 0, 0)])
            layer_norm(1)
            split_to(first_block[("gate", 0, 0)] + 1)
            round_x(1)
            ffn(0)
            split_to(first_block[("conv", KD)])
            layer_norm(2)
            split_to(first_block[("conv", KD)] + 1)
            act.dma_start(ba_raw[:, :, :], A["od_w_in"][0][:, BA0:BA0 + P].rearrange("(k p) n -> p k n", p=P))\
               .then_inc(s["ba_landed"], 16)
            for dst, c0, n in ((o_upto, 0, P), (o_negt, P, P), (o_posl, 2 * P, P)):
                act.dma_start(dst[:, :], A["c_odd"][:, c0:c0 + n]).then_inc(consts, 16)
            act.dma_start(o_lvl[:, :, :], A["c_odd"][:, 3 * P:].rearrange("p (l c) -> p l c", c=P // 2))\
               .then_inc(consts, 16)
            round_x(2)
            act.wait_ge(s["ba_landed"], 16)
            act.activation(ba_hi[:, :, :], ba_raw[:, :, :], ACT.Copy).then_inc(s["ba_hi_ready"], 1)

            def silu_conv(i):
                n = CONV_ORDER[i]
                taken(act, ("conv", n))
                act.activation(qkv[:, n, :], conv_acc(i), ACT.Silu).then_inc(s["conv_silu"], 1)
                if n < 2 * KD:
                    act.wait_ge(s["conv_silu"], i + 1)
                    if i >= 2:
                        full(act, ("norm", CONV_ORDER[i - 2]))
                    act.activation(conv_squares(i), qkv[:, n, :], ACT.Square).then_inc(s["conv_sq"], 1)

            for i, n in enumerate(CONV_ORDER):
                split_to(first_block[("conv", n - n % 2)] + 1)
                full(act, ("conv", n))
                act.activation(conv_acc(i), bank(("conv", n))[:, :], ACT.Copy,
                               scale=convw[:, 9 * KD + n:9 * KD + n + 1]).then_inc(s["conv_raw"], 1)
                if i:
                    silu_conv(i - 1)
                if i == 3:
                    act.wait_ge(s["ba_mid"], 1)
                    act.activation(beta[:, :, :], ba[:, :, 0:GDN_H], ACT.Exp, scale=-1.0)
                    link(act.activation(g_tmp[:, :, :], g_tmp[:, :, :], ACT.Exp))
                    act.activation(g_tmp[:, :, :], g_tmp[:, :, :], ACT.Ln, bias=1.0)
                    act.activation(a_log[:, :], a_log[:, :], ACT.Exp).then_inc(s["ba_exp"], 1)
                if i == DECAY_AT + 3:
                    act.wait_ge(s["dec_ready"], 1)
                    act.activation(to_end[:, :, :], to_end[:, :, :], ACT.Exp)
                    act.activation(bexp[:, :, :], dec[:, 0, :, :], ACT.Exp).then_inc(s["dec_exp"], 1)
            split_to(first_block[("og", 0)] + 1)
            silu_conv(len(CONV_ORDER) - 1)
            taken(act, ("norm", CONV_ORDER[2 * KD - 1]))
            act.activation(nrm[:, :, :], nrm[:, :, :], ACT.Sqrt, bias=eps[:, 1:2]).then_inc(s["rn_ready"], 1)
            def filler(t, place):
                name = FILLERS.get((t, place))
                if name is not None and name[0] == "og":
                    full(act, name)
                    take(act.activation(gate_s[:, name[2], name[1] * 512:(name[1] + 1) * 512], bank(name)[:, :],
                                        ACT.Silu), name)

            def output_rstd(t):
                act.wait_ge(s["ov_ready"], 2 * (t + 1))
                act.activation(oms[:, :], oms[:, :], ACT.Sqrt, scale=1.0 / P, bias=eps[:, 1:2])\
                   .then_inc(s["or_ready"], 1)

            for t in range(NT):
                filler(t, -1)
                for hg in range(2):
                    full(act, ("drow", t, hg))
                    act.activation(EE[:, hsl[hg], :], fm4(("drow", t, hg)), ACT.Exp).then_inc(s["e_ready"], 1)
                for hg in range(2):
                    act.wait_ge(s["ga_arg"], 2 * t + hg + 1)
                    act.activation(GA[:, hsl[hg], :], GA[:, hsl[hg], :], ACT.Exp, scale=-1.0)\
                       .then_inc(s["ga_exp"], 1)
                for hg in range(2):
                    act.wait_ge(s["gt_arg"], 2 * t + hg + 1)
                    act.activation(GT[:, hsl[hg], :], GT[:, hsl[hg], :], ACT.Exp).then_inc(s["gt_exp"], 1)
                for hg in range(2):
                    full(act, ("khT", t, hg))
                    take(act.activation(qkv[:, KD + 4 * hg:KD + 4 * hg + 4, tile_cols[t]], fm4(("khT", t, hg)),
                                        ACT.Copy), ("khT", t, hg))
                filler(t, 0)
                if t:
                    output_rstd(t - 1)
                filler(t, 1)
                filler(t, 2)
                for lv in LEVELS[1:]:
                    for hg in range(2):
                        full(act, ("tt", t, lv, hg))
                        take(act.activation(TT[:, hsl[hg], :], fm4(("tt", t, lv, hg)), ACT.Copy), ("tt", t, lv, hg))
                    if lv == 8:
                        filler(t, 3)
                    for name in SPLIT_IN:
                        if t == SPLIT_IN[name] and lv in SPLIT_AT:
                            split_to(first_block[name] + SPLIT_AT.index(lv))
                if t:
                    round_o(1, t - 1)
                for name, dst in (("u", GU), ("w", TT)):
                    for hg in range(2):
                        full(act, (name, t, hg))
                        take(act.activation(dst[:, hsl[hg], :], fm4((name, t, hg)), ACT.Copy), (name, t, hg))
                for hg in range(2):
                    taken(act, ("o", t, hg))
                    act.activation(M1[:, hsl[hg], :], OO[:, hsl[hg], :], ACT.Square).then_inc(s["o_sq"], 1)
            output_rstd(NT - 1)
            round_o(1, NT - 1)
            split_to(first_block[("mix", 1, 1)])
            full(act, ("mix", 1, 0, NT - 1))
            split_to(first_block[("gate", 1, 0)])
            layer_norm(3)
            split_to(first_block[("gate", 1, 0)] + 1)
            round_x(3)
            ffn(1)
            split_to(NB - 1)
            layer_norm(4)

        @block_.vector
        def _(dve):
            steps = [0]

            def link(ins):
                steps[0] += 1
                ins.then_inc(s["dve_step"], 1)
                dve.wait_ge(s["dve_step"], steps[0])

            def k4(key):
                return bank(key)[:, :].rearrange("p (k n) -> p k n", k=4)

            def across(col, n):
                return col.unsqueeze(2).broadcast_to([col.shape[0], col.shape[1], n])

            def over_heads(mat, heads):
                return mat.unsqueeze(1).broadcast_to([mat.shape[0], heads, mat.shape[1]])

            def round_x(i):
                gcol = 32 * ((i + 1) % 2) + 8 * ((i - 1) // 2)

                def low(k):
                    dve.wait_ge(s["x_hi_ready"], KD * i + k + 1)
                    dve.tensor_tensor(x_lo[:, k, :], f_ab[:, k % 4, :], x_hi[:, k, :].bitcast(F32), ALU.subtract)\
                       .then_inc(s[("x_lo_even", "x_lo_odd")[k % 2]], 1)

                for k in range(KD):
                    full(dve, ("xT", i, k))
                    if k >= 4:
                        low_part_there(dve, i, k - 4)
                    src = bank(("xT", i, k))[:, :]
                    if i == 0:
                        take(dve.tensor_copy(f_ab[:, k % 4, :], src), ("xT", i, k))
                    else:
                        take(dve.tensor_scalar(f_ab[:, k % 4, :], src, lnc[:, gcol + k:gcol + k + 1],
                                               lnc[:, gcol + 16 + k:gcol + 17 + k], ALU.mult, ALU.add), ("xT", i, k))
                    if k and (k % 2 or i == 0):
                        low(k - 1)
                if i == 0:
                    low(KD - 1)

            def round_o(layer, t):
                for i in range(2):
                    dve.wait_ge(s["o_hi_ready"], 2 * (NT * layer + t) + i + 1)
                    cols = x_hi[:, 4 * i:4 * i + 4, tile_cols[t]].bitcast(F32)
                    take(dve.tensor_tensor(x_lo[:, 4 * i:4 * i + 4, tile_cols[t]], k4(("oT", layer, t, i)), cols,
                                           ALU.subtract), ("oT", layer, t, i))

            def layer_norm(i, group, layer):
                def normalise(t):
                    dve.wait_ge(s["ln_stat"], NT * (i - 1) + t + 1)
                    link(dve.reciprocal(rstd[:, t:t + 1], rstd[:, t:t + 1]))
                    if i == 4 and t >= NT // 2:
                        dve.wait_ge(s["ln_landed"], 32 * 4)
                        dve.scalar_tensor_tensor(x_tm[:, t, :], x_tm[:, t, :], mv[:, t, 0:1], ln_rows[:, 0, :],
                                                 ALU.subtract, ALU.mult).then_inc(y_ready[t], 1)
                        dve.wait_ge(y_ready[t], 1)
                        dve.scalar_tensor_tensor(x_tm[:, t, :], x_tm[:, t, :], rstd[:, t:t + 1], ln_rows[:, 1, :],
                                                 ALU.mult, ALU.add).then_inc(y_ready[t], 1)
                        return
                    dve.tensor_scalar(x_tm[:, t, :], x_tm[:, t, :], mv[:, t, 0:1], rstd[:, t:t + 1],
                                      ALU.subtract, ALU.mult).then_inc(s["z_norm"], 1)

                for half in range(2):
                    for t in range(NT):
                        if (group, layer, half, t) not in FILLED:
                            add_sublayer(i, group, layer, half, t)
                        if half:
                            dve.wait_ge(s["half_stats"], 2 * NT * (i - 1) + NT + t + 1)
                            dve.bn_aggr(mv[:, t, :], stats[:, t, :, :].rearrange("p a b -> p (a b)"))\
                               .then_inc(s["ln_var"], 1)
                            if t:
                                normalise(t - 1)
                normalise(NT - 1)

            def add_sublayer(i, group, layer, half, t):
                key = (group, layer, half, t)
                if i > 1:
                    dve.wait_ge(s["x_affine"], 2 * NT * (i - 2) + 2 * (t + 1))
                full(dve, key)
                cols = x_tm[:, t, half * 512:(half + 1) * 512]
                take(dve.scalar_tensor_tensor(cols, cols, ALPHA, bank(key)[:, :], ALU.mult, ALU.add), key)
                taken(dve, key)
                dve.bn_stats(stats[:, t, half, :], cols).then_inc(s["half_stats"], 1)

            def ffn(layer):
                for f in range(KF):
                    n = layer * KF + f
                    taken(dve, ("gate", layer, f))
                    full(dve, ("up", layer, f))
                    take(dve.tensor_tensor(f_ab[:, 2 + f % 2, :], bank(("up", layer, f))[:, :], f_ab[:, f % 2, :],
                                           ALU.mult), ("up", layer, f))
                    dve.wait_ge(s["h_hi_ready"], n + 1)
                    dve.tensor_tensor(h_lo[:, f, :], f_ab[:, 2 + f % 2, :], h_hi[:, f, :].bitcast(F32), ALU.subtract)\
                       .then_inc(s["h_lo_ready"], 1)

            round_x(0)
            low_part_there(dve, 0, KD - 2)
            low_part_there(dve, 0, KD - 1)
            dve.memset(k_pad[:, :, :, :].rearrange("p a b c -> p (a b c)"), 0.0).then_inc(zeroed, 1)
            dve.wait_ge(zeroed, 9)
            dve.wait_ge(consts, 16 * N_CONST)

            def rotate(src, dst, t, heads):
                cos = over_heads(rope[:, t, 0, :], heads)
                sin = over_heads(rope[:, t, 1, :], heads)
                a, b, c, d = (r_tmp[:, i, 0:heads, :] for i in range(4))
                dve.tensor_tensor(a, src[:, :, 0:RH], cos, ALU.mult)
                dve.tensor_tensor(b, src[:, :, RH:HD], sin, ALU.mult)
                dve.tensor_tensor(c, src[:, :, RH:HD], cos, ALU.mult)
                link(dve.tensor_tensor(d, src[:, :, 0:RH], sin, ALU.mult))
                dve.tensor_tensor(dst[:, :, 0:RH], a, b, ALU.subtract)
                return dve.tensor_tensor(dst[:, :, RH:HD], c, d, ALU.add)

            for t in range(NT):
                dve.wait_ge(s["sv_copied"], t + 1)
                even = k_pad[:, t, :, :].rearrange("p (g e) c -> p g e c", e=2)
                src = bank(("skv", t))[:, 0:KVH * HD].rearrange("p (h d) -> p h d", h=KVH)
                last = rotate(src, even[:, :, 0, 0:HD], t, KVH)
                take(last, ("skv", t))
                taken(dve, ("skv", t))
                dve.tensor_copy(even[:, :, 1, HD:P], even[:, :, 0, 0:HD]).then_inc(s["k_rotated"], 1)
            for i, (dst, n) in enumerate(((lnc, 66), (convw, 96))):
                full(dve, ("const", i))
                take(dve.tensor_copy(dst[:, 0:n], bank(("const", i))[:, 0:n]), ("const", i))
            for t in range(NT):
                full(dve, ("sq", t))
                dst = q_rot[:, t, :].rearrange("p (h d) -> p h d", h=QH)
                take(rotate(bank(("sq", t))[:, :].rearrange("p (h d) -> p h d", h=QH), dst, t, QH), ("sq", t))
            for n in range(2):
                full(dve, ("a2", n))
                take(dve.tensor_scalar(g_B[:, n, :], bank(("a2", n))[:, :], lnc[:, 64 + n:65 + n], None, ALU.add),
                     ("a2", n))
                taken(dve, ("a2", n))
                dve.scalar_tensor_tensor(g_kd[:, n, :], g_B[:, n, :], -1.0, g_B[:, n, :], ALU.mult, ALU.min)\
                   .then_inc(s["a2_mid"], 1)
            dve.wait_ge(s["a2_exp"], 1)
            link(dve.scalar_tensor_tensor(g_kd[:, :, :], g_B[:, :, :], 0.0, g_e[:, :, :], ALU.min, ALU.subtract))
            for n in range(2):
                dve.tensor_tensor_scan(g_B[:, n, :], g_keep[:, :], g_kd[:, n, :], 0.0, ALU.mult, ALU.add)\
                   .then_inc(s["g_scan"], 1)
            dve.wait_ge(s["g_scan"], 2)
            full(dve, ("kT", NT - 1))
            for n in range(2):
                bv = g_B[:, n, :].rearrange("p (c l) -> p c l", l=CH)
                ins = dve.tensor_tensor(s_p[:, n, :].rearrange("p (c l) -> p c l", l=CH),
                                        bv[:, :, CH - 1:CH].broadcast_to([P, NC, CH]), bv, ALU.subtract)
            ins.then_inc(s["g_gate"], 1)
            dve.wait_ge(s["g_exp"], 1)
            taken(dve, ("gq", 1))
            for e in range(2):
                rows = slice(e * GDK, (e + 1) * GDK)
                dve.tensor_tensor(q_pad[rows, e:GH:2, :], g_q[rows, :, :], g_e[rows, :, :], ALU.mult)\
                   .then_inc(s["q_gated"], 1)
            dve.wait_ge(s["g_exp"], 2)
            taken(dve, ("gk", 1))
            dve.tensor_tensor(g_kd[:, :, :], g_k[:, :, :], s_p[:, :, :], ALU.mult).then_inc(s["k_decayed"], 1)
            dve.wait_ge(s["g_exp"], 3)
            dve.tensor_tensor(g_k[:, :, :], g_k[:, :, :], s_p[:, :, :], ALU.mult).then_inc(s["k_gated"], 1)

            def heads4(ap):
                return ap.rearrange("p (h n) -> p h n", h=4)

            for t in range(NT):
                for g in range(KVH):
                    key = ("score", t, g)
                    hs = slice(4 * g, 4 * g + 4)
                    full(dve, key)
                    if t == 0:
                        link(dve.memset(k4(key)[0:CH, :, 0:CH], NEG))
                    link(dve.tensor_reduce(s_max[:, hs], k4(key), AX, ALU.max))
                    link(dve.scalar_tensor_tensor(s_max[:, hs], s_max[:, hs], HD ** -0.5, sinks[:, hs],
                                                  ALU.mult, ALU.max))
                    take(dve.scalar_tensor_tensor(heads4(s_p[:, g, :]), k4(key), HD ** -0.5,
                                                  across(s_max[:, hs], P), ALU.mult, ALU.subtract), key)
                    dve.tensor_tensor(s_snk[:, hs], sinks[:, hs], s_max[:, hs], ALU.subtract)\
                       .then_inc(s["s_shift"], 1)
                full(dve, ("gattn", t))
                take(dve.copy_predicated(g_at[:, :, :], over_heads(upto[:, :].bitcast(I32), GH), k4(("gattn", t))),
                     ("gattn", t))
                for c in range(2):
                    key = ("gstate", t, c)
                    full(dve, key)
                    v = 2 * t + c
                    for h in range(GH):
                        rows = slice((h % 2) * GDK, (h % 2 + 1) * GDK)
                        col = (2 * t + c + 1) * CH - 1
                        ins = dve.scalar_tensor_tensor(
                            g_S[rows, (v + 1) % 2, h // 2, :], g_S[rows, v % 2, h // 2, :],
                            g_e[rows, h // 2, col:col + 1], bank(key)[rows, h * GDV:(h + 1) * GDV],
                            ALU.mult, ALU.add)
                    take(ins, key)
                    taken(dve, key)
                for g in range(KVH):
                    hs = slice(4 * g, 4 * g + 4)
                    dve.wait_ge(s["s_prob"], KVH * t + g + 1)
                    link(dve.tensor_reduce(s_den[:, hs], heads4(s_p[:, g, :]), AX, ALU.add))
                link(dve.tensor_tensor(s_den[:, :], s_den[:, :], s_snk[:, :], ALU.add))
                link(dve.reciprocal(s_den[:, :], s_den[:, :]))
                key = ("gout", t)
                full(dve, key)
                og = heads4(o_tm[:, t % 2, 0:512])
                link(dve.tensor_reduce(g_mu[:, :], k4(key), AX, ALU.add))
                link(dve.tensor_scalar(g_mu[:, :], g_mu[:, :], 1.0 / GDV, None, ALU.mult))
                take(dve.tensor_tensor(og, k4(key), across(g_mu[:, :], GDV), ALU.subtract), key)
                taken(dve, key)
                sq = r_tmp[:, 0:2, :, :].rearrange("p a b c -> p (a b c)")
                link(dve.tensor_tensor(sq, o_tm[:, t % 2, 0:512], o_tm[:, t % 2, 0:512], ALU.mult))
                dve.tensor_reduce(g_var[:, :], heads4(sq), AX, ALU.add).then_inc(s["o_var"], 1)
                dve.wait_ge(s["o_rstd"], t + 1)
                link(dve.reciprocal(g_var[:, :], g_var[:, :]))
                link(dve.tensor_tensor(og, og, across(g_var[:, :], GDV), ALU.mult))
                dve.wait_ge(s["gr_ready"], t + 1)
                dve.tensor_tensor(o_tm[:, t % 2, 0:512], o_tm[:, t % 2, 0:512], g_r[:, t, :], ALU.mult)\
                   .then_inc(s["o_even"], 1)
                key = ("sout", t)
                full(dve, key)
                take(dve.tensor_tensor(o_tm[:, t % 2, 512:D].rearrange("p (h n) -> p h n", h=QH),
                                       bank(key)[:, :].rearrange("p (h n) -> p h n", h=QH),
                                       across(s_den[:, :], HD), ALU.mult), key)
                if t:
                    round_o(0, t - 1)
            for key in TAIL_FILLERS[0]:
                add_sublayer(1, *key)
            round_o(0, NT - 1)
            layer_norm(1, "mix", 0)
            round_x(1)
            ffn(0)
            layer_norm(2, "down", 0)
            round_x(2)
            low_part_there(dve, 2, KD - 2)
            low_part_there(dve, 2, KD - 1)
            dve.memset(ST[:, :, :].rearrange("p a b -> p (a b)"), 0.0).then_inc(s["state0"], 1)
            for i, n in enumerate(CONV_ORDER):
                key = ("conv", n)
                dve.wait_ge(s["conv_raw"], i + 1)
                full(dve, key)
                for back in range(1, CONV_K):
                    tap = (CONV_K - 1 - back) * 3 * KD + n
                    dst = conv_acc(i)[:, back:]
                    ins = dve.scalar_tensor_tensor(dst, bank(key)[:, 0:SEQ - back], convw[:, tap:tap + 1], dst,
                                                   ALU.mult, ALU.add)
                    if back < CONV_K - 1:
                        link(ins)
                take(ins, key)
                if i == 1:
                    full(dve, ("ba_fm",))
                    take(dve.tensor_copy(ba_fm[:, :], bank(("ba_fm",))[0:BA, :]), ("ba_fm",))
                if i == 2:
                    full(dve, ("ba",))
                    take(dve.tensor_copy(ba[:, :, :], bank(("ba",))[:, 0:NT * 2 * GDN_H].rearrange("p (t c) -> p t c", t=NT)),
                         ("ba",))
                    taken(dve, ("ba",))
                    link(dve.tensor_tensor(gdec[:, :, :], ba[:, :, GDN_H:], over_heads(dt_bias[:, :], NT), ALU.add))
                    dve.scalar_tensor_tensor(g_tmp[:, :, :], gdec[:, :, :], -1.0, gdec[:, :, :], ALU.mult, ALU.min)\
                       .then_inc(s["ba_mid"], 1)
                if i == 4:
                    dve.wait_ge(s["ba_exp"], 1)
                    link(dve.tensor_scalar(beta[:, :, :], beta[:, :, :], 1.0, None, ALU.add))
                    link(dve.reciprocal(beta[:, :, :], beta[:, :, :]))
                    link(dve.scalar_tensor_tensor(gdec[:, :, :], gdec[:, :, :], 0.0, g_tmp[:, :, :], ALU.max, ALU.add))
                    dve.scalar_tensor_tensor(gdec[:, :, :], gdec[:, :, :], -1.0, over_heads(a_log[:, :], NT),
                                             ALU.mult, ALU.mult).then_inc(s["g_ready"], 1)
                if i == DECAY_AT:
                    full(dve, ("decay",))
                    take(dve.tensor_copy(dec[:, :, :, :].rearrange("p a t h -> p (a t h)"),
                                         bank(("decay",))[:, 0:2 * TH]), ("decay",))
                    taken(dve, ("decay",))
                    dve.tensor_tensor(to_end[:, :, :], dec[:, 1, :, :], dec[:, 0, :, :], ALU.subtract)\
                       .then_inc(s["dec_ready"], 1)
                if i >= 3 and CONV_ORDER[i - 3] < 2 * KD:
                    m = CONV_ORDER[i - 3]
                    full(dve, ("norm", m))
                    take(dve.tensor_copy(nrm[:, m, :], bank(("norm", m))[:, 0:NT]), ("norm", m))
            dve.wait_ge(s["dec_exp"], 1)
            link(dve.tensor_tensor(bexp[:, :, :], bexp[:, :, :], beta[:, :, :], ALU.mult))
            dve.wait_ge(s["rn_ready"], 1)
            link(dve.reciprocal(nrm[:, :, :], nrm[:, :, :]))
            link(dve.tensor_scalar(nrm[:, 0:GDN_H, :], nrm[:, 0:GDN_H, :], float(P) ** -0.5, None, ALU.mult))

            def out_scale(t, hg):
                dve.wait_ge(s["or_ready"], t + 1)
                if hg == 0:
                    link(dve.reciprocal(oms[:, :], oms[:, :]))
                o = OO[:, hsl[hg], :]
                dve.tensor_tensor(o, o, across(oms[:, hsl[hg]], P), ALU.mult).then_inc(s["o_scaled"], 1)

            def out_square_sum(t):
                for hg in range(2):
                    dve.wait_ge(s["o_sq"], 2 * t + hg + 1)
                    dve.tensor_reduce(oms[:, hsl[hg]], M1[:, hsl[hg], :], AX, ALU.add).then_inc(s["ov_ready"], 1)

            def filler(t, place):
                name = FILLERS.get((t, place))
                if name is not None and name[0] == "mix":
                    add_sublayer(3, *name)

            dve.wait_ge(s["x_affine"], 4 * NT)
            for t in range(NT):
                H = range(2)
                for hg in H:
                    full(dve, ("kTM", t, hg))
                    rk = nrm[:, KD + 4 * hg:KD + 4 * hg + 4, t]
                    take(dve.tensor_tensor(KH[:, hsl[hg], :], k4(("kTM", t, hg)), across(rk, P), ALU.mult),
                         ("kTM", t, hg))
                if t:
                    out_square_sum(t - 1)
                for hg in H:
                    hs = hsl[hg]
                    dve.wait_ge(s["e_ready"], 2 * t + hg + 1)
                    full(dve, ("drow", t, hg))
                    take(dve.tensor_tensor(GU[:, hs, :], k4(("drow", t, hg)), across(dec[:, 0, t, hs], P),
                                           ALU.subtract), ("drow", t, hg))
                    taken(dve, ("drow", t, hg))
                    dve.tensor_tensor(GA[:, hs, :], GU[:, hs, :], over_heads(o_posl[:, :], 4), ALU.add)\
                       .then_inc(s["ga_arg"], 1)
                for hg in H:
                    full(dve, ("vTM", t, hg))
                    take(dve.tensor_tensor(qkv[:, 2 * KD + 4 * hg:2 * KD + 4 * hg + 4, tile_cols[t]],
                                           k4(("vTM", t, hg)), across(beta[:, t, hsl[hg]], P), ALU.mult),
                         ("vTM", t, hg))
                dve.tensor_copy(edl[:, :], EE[:, :, P - 1])
                filler(t, 0)
                for hg in H:
                    full(dve, ("gram", t, hg))
                    dve.wait_ge(s["ga_exp"], 2 * t + hg + 1)
                    for h in range(4 * hg, 4 * hg + 4):
                        ins = dve.scalar_tensor_tensor(GA[:, h, :], k4(("gram", t, hg))[:, h % 4, :],
                                                       beta[:, t, h:h + 1], GA[:, h, :], ALU.mult, ALU.mult)
                    take(ins, ("gram", t, hg))
                filler(t, 1)

                def masked(ps, l, hg):
                    lv = LEVELS[l]
                    m = o_lvl[:, l, :].rearrange("p (q b) -> p q b", b=lv).unsqueeze(1)\
                        .broadcast_to([P, 4, P // 2 // lv, lv])
                    return dve.tensor_tensor(half_product(hg).rearrange("p (g q b) -> p g q b", g=4, b=lv), ps, m,
                                             ALU.mult)

                def level_step(hg, lv, product):
                    sv = upper_halves(SS[:, hsl[hg], :].rearrange("p h c -> p (h c)"), lv)
                    return dve.tensor_tensor(sv, sv, product.rearrange("p (m b) -> p m b", b=lv), ALU.subtract)

                dve.wait_ge(s["eye_ready"], t + 1)
                for hg in H:
                    key = ("at", t, hg)
                    full(dve, key)
                    ps = upper_halves(bank(key)[:, :], 1).rearrange("p (g q) b -> p g q b", g=4)
                    take(masked(ps, 0, hg), key)
                    taken(dve, key)
                    level_step(hg, 1, half_product(hg)).then_inc(s["s0_ready"], 1)
                for l, lv in enumerate(LEVELS[1:], 1):
                    for hg in H:
                        key = ("m1", t, lv, hg)
                        full(dve, key)
                        take(masked(bank(key)[:, 0:4 * HALF].rearrange("p (g q b) -> p g q b", g=4, b=lv), l, hg), key)
                    if lv == 2 * QK_AFTER:
                        for hg in H:
                            full(dve, ("qk", t, hg))
                            dve.wait_ge(s["gt_exp"], 2 * t + hg + 1)
                            take(dve.tensor_tensor(GT[:, hsl[hg], :], k4(("qk", t, hg)), GT[:, hsl[hg], :],
                                                   ALU.mult), ("qk", t, hg))
                    for hg in H:
                        key = ("ds", t, lv, hg)
                        full(dve, key)
                        take(level_step(hg, lv, bank(key)[:, 0:4 * HALF]), key)
                    if t and lv in (2, 4):
                        out_scale(t - 1, lv // 4)
                    if lv == 8:
                        filler(t, 3)
                for hg in H:
                    hs = hsl[hg]
                    dve.tensor_tensor(M1[:, hs, :], KH[:, hs, :], across(bexp[:, t, hs], P), ALU.mult)\
                       .then_inc(s["kb_ready"], 1)
                if t:
                    round_o(1, t - 1)
                for hg in H if t < NT - 1 else ():
                    hs = hsl[hg]
                    dve.tensor_tensor(KH[:, hs, :], KH[:, hs, :], across(to_end[:, t, hs], P), ALU.mult)\
                       .then_inc(s["kd_ready"], 1)
                dve.wait_ge(s["q_decayed"], 2 * t + 2)
                for hg in H:
                    key = ("ws", t, hg)
                    full(dve, key)
                    taken(dve, ("u", t, hg))
                    take(dve.tensor_tensor(EE[:, hsl[hg], :], GU[:, hsl[hg], :], k4(key), ALU.subtract), key)
                for hg in H:
                    key = ("o", t, hg)
                    full(dve, key)
                    take(dve.tensor_tensor(OO[:, hsl[hg], :], k4(key), across(nrm[:, 4 * hg:4 * hg + 4, t], P),
                                           ALU.mult), key)
                for hg in H if t < NT - 1 else ():
                    key = ("kv", t, hg)
                    full(dve, key)
                    for h in range(4 * hg, 4 * hg + 4):
                        ins = dve.scalar_tensor_tensor(ST[:, h, :], ST[:, h, :], edl[:, h:h + 1],
                                                       k4(key)[:, h % 4, :], ALU.mult, ALU.add)
                    take(ins, key)
            out_square_sum(NT - 1)
            for hg in range(2):
                out_scale(NT - 1, hg)
            for key in TAIL_FILLERS[1]:
                add_sublayer(3, *key)
            round_o(1, NT - 1)
            layer_norm(3, "mix", 1)
            round_x(3)
            ffn(1)
            layer_norm(4, "down", 1)

        @block_.tensor
        def _(pe):
            def fill(key):
                u = unit[key]
                if u >= 8:
                    pe.wait_ge(bank_taken[u % 8], u // 8)
                return bank(key)

            def done(ins, key):
                ins.then_inc(bank_full[unit[key] % 8], 1)

            def mm3(out_ap, st, mv_, start, stop):
                pe.matmul(out_ap, st[0], mv_[0], start=start, stop=False)
                pe.matmul(out_ap, st[0], mv_[1], start=False, stop=False)
                return pe.matmul(out_ap, st[1], mv_[0], start=False, stop=stop)

            def weights_there(b, kk):
                nk = blocks[b][2]
                if kk in (0, nk // 2):
                    pe.wait_ge(w_lo_ready, 2 * b + (1 if kk == 0 else 2))

            def weights(b, kk, c0, width):
                n = blocks[b][3]
                at_ = kk * n + c0
                return tuple(w[:, b % 2, at_:at_ + width] for w in (w_hi, w_lo))

            def xcols(k, cols):
                return x_hi[:, k, cols], x_lo[:, k, cols]

            def hcols(k, cols):
                return h_hi[:, k, cols], h_lo[:, k, cols]

            ALL = slice(0, SEQ)

            def fm_block(b, keys, fresh=None, width=P):
                steps = [(n, k) for n in range(len(keys)) for k in range(KD)]
                if fresh is not None:
                    steps = [(n, k) for k in range(KD) for n in range(len(keys))]
                for n, k in steps:
                    if n == 0:
                        weights_there(b, k)
                    if fresh is not None and n == 0:
                        low_part_there(pe, fresh, k)
                    ps = fill(keys[n]) if k == 0 else bank(keys[n])
                    ins = mm3(ps[:, :], weights(b, k, n * P, P), xcols(k, ALL), k == 0, k == KD - 1)
                    if k == KD - 1:
                        done(ins, keys[n])

            def tm_group(name, wait_k, src=xcols, kt=KD, in_turn=False, tiles=range(NT)):
                b = first_block[name]
                while b < NB and blocks[b][0] == name:
                    _, k0, nk, width, _v = blocks[b]
                    steps = [(kk, t) for kk in range(nk) for t in tiles]
                    if in_turn and k0 + nk == kt:
                        steps = [(kk, t) for t in tiles for kk in range(nk)]
                    waited = -1
                    for kk, t in steps:
                        if kk > waited:
                            weights_there(b, kk)
                            wait_k(k0 + kk)
                            waited = kk
                        key = (*name, t)
                        ps = fill(key) if k0 + kk == 0 else bank(key)
                        ins = mm3(ps[:, 0:width], src(k0 + kk, tile_cols[t]), weights(b, kk, 0, width),
                                  k0 + kk == 0, k0 + kk == kt - 1)
                        if k0 + kk == kt - 1:
                            done(ins, key)
                    if k0 + nk < kt:
                        ins.then_inc(w_used, 1)
                    b += 1

            def no_wait(k):
                pass

            def tile_of(key):
                b = first_block[key[:-1]]
                if key[0] == "mix":
                    for i in range(2):
                        taken(pe, ("oT", key[1], key[-1], i))
                ps = fill(key)
                for k in range(KD):
                    weights_there(b + k // 4, k % 4)
                    ins = mm3(ps[:, :], xcols(k, tile_cols[key[-1]]), weights(b + k // 4, k % 4, 0, 512),
                              k == 0, k == KD - 1)
                done(ins, key)

            def filler(t, place):
                if (t, place) in FILLERS:
                    tile_of(FILLERS[t, place])

            def turn_x(i):
                for t in range(NT):
                    if i == 0:
                        pe.wait_ge(x_landed[t], 16)
                    else:
                        pe.wait_ge(s["z_norm"], NT * (i - 1) + t + 1)
                    for k in range(KD):
                        ps = fill(("xT", i, k)) if t == 0 else bank(("xT", i, k))
                        ins = pe.transpose(ps[:, tile_cols[t]], x_tm[:, t, k * P:(k + 1) * P], eye[:, :])
                        if t == NT - 1:
                            done(ins, ("xT", i, k))

            def turn_o(layer, t):
                for i in range(2):
                    if layer == 0:
                        pe.wait_ge(s["o_even"], t + 1)
                        taken(pe, ("sout", t))
                    else:
                        pe.wait_ge(s["o_odd"], 2 * t + i + 1)
                    ps = fill(("oT", layer, t, i))
                    for j in range(4):
                        k = 4 * i + j
                        src = o_tm[:, t % 2, k * P:(k + 1) * P] if layer == 0 else OO[:, k, :]
                        ins = pe.transpose(ps[:, j * P:(j + 1) * P], src, eye[:, :])
                    done(ins, ("oT", layer, t, i))

            def mix_and_norm(layer):
                def have(k):
                    taken(pe, ("oT", layer, NT - 1, k // 4))
                for half in range(2):
                    tiles = [t for t in range(NT) if ("mix", layer, half, t) not in FILLED]
                    tm_group(("mix", layer, half), have, in_turn=half == 1, tiles=tiles)
                turn_x(2 * layer + 1)

            def ffn(layer):
                for f in range(0, KF, 2):
                    fresh = 2 * layer + 1 if f == 0 else None
                    b = first_block[("gate", layer, f)]
                    fm_block(b, [("gate", layer, f), ("gate", layer, f + 1)], fresh)
                    fm_block(b + 1, [("up", layer, f), ("up", layer, f + 1)])

                def have(k):
                    pe.wait_ge(s["h_lo_ready"], layer * KF + k + 1)
                for half in range(2):
                    tm_group(("down", layer, half), have, hcols, KF, in_turn=half == 1)

            pe.wait_ge(s["eye_landed"], 16)
            turn_x(0)
            tm_group(("skv",), lambda k: low_part_there(pe, 0, k))
            pe.wait_ge(consts, 16 * N_CONST)
            for i, (src, n) in enumerate(((vec_rows, 66), (conv_rows, 96))):
                ps = fill(("const", i))
                done(pe.transpose(ps[:, 0:n], src[0:n, :], eye[0:n, 0:n]), ("const", i))
            tm_group(("sq",), no_wait)
            fm_block(first_block[("gq",)], [("gq", 0), ("gq", 1)])
            fm_block(first_block[("gk",)], [("gk", 0), ("gk", 1)])
            fm_block(first_block[("ga",)], [("ga",)])
            for t in range(NT):
                ps = fill(("qT", t))
                taken(pe, ("sq", t))
                for j in range(4):
                    ins = pe.transpose(ps[:, j * P:(j + 1) * P], q_rot[:, t, j * P:(j + 1) * P], eye[:, :])
                done(ins, ("qT", t))
                ps = fill(("kT", t))
                pe.wait_ge(s["k_rotated"], t + 1)
                for j in range(4):
                    ins = pe.transpose(ps[:, j * P:(j + 1) * P], k_pad[:, t, j, :], eye[:, :])
                done(ins, ("kT", t))
            taken(pe, ("ga",))
            for n in range(2):
                ps = fill(("a2", n))
                done(pe.matmul(ps[:, :], g_a2[:, n * P:(n + 1) * P], g_ga[:, :], start=True, stop=True), ("a2", n))
            tm_group(("gv",), no_wait)
            pe.wait_ge(s["k_gated"], 1)
            pe.wait_ge(s["k_decayed"], 1)
            pe.wait_ge(s["q_gated"], 2)
            pe.wait_ge(s["sv_shifted"], 32)
            taken(pe, ("kT", NT - 1))
            taken(pe, ("qT", NT - 1))
            taken(pe, ("gv", NT - 1))

            def across_chunks(t, c, ps, start):
                rows = slice(c * CH, (c + 1) * CH)
                cols = slice(t * P + c * CH, t * P + (c + 1) * CH)
                for h in range(GH):
                    pe.matmul(ps[rows, h * GDV:(h + 1) * GDV], q_pad[:, h, cols], g_S[:, c, h // 2, :],
                              start=h == 0, stop=False, skip_group_check=True)

            def chunk_state(t, c):
                rows = slice(c * CH, (c + 1) * CH)
                ps = fill(("gstate", t, c))
                for h in range(GH):
                    ins = pe.matmul(ps[:, h * GDV:(h + 1) * GDV], g_kdt[rows, h // 2, :],
                                    g_v[rows, t, h * GDV:(h + 1) * GDV], start=True, stop=True)
                done(ins, ("gstate", t, c))

            for t in range(NT):
                for g in range(KVH):
                    ps = fill(("score", t, g))
                    for hh in range(4):
                        h = 4 * g + hh
                        for c in range(2):
                            chunk = 2 * t + c
                            ins = pe.matmul(ps[c * CH:(c + 1) * CH, hh * P:(hh + 1) * P],
                                            s_qT[:, h // 2, chunk * CH:(chunk + 1) * CH],
                                            s_kT[:, 2 * g + h % 2, chunk * CH:chunk * CH + 2 * CH],
                                            start=True, stop=True)
                    done(ins, ("score", t, g))
                ps = fill(("kd", t))
                for n in range(2):
                    ins = pe.transpose(ps[:, n * P:(n + 1) * P], g_kd[:, n, tile_cols[t]], eye[:, :])
                done(ins, ("kd", t))
                tile_of(("gr", t))
                ps = fill(("gattn", t))
                for h in range(GH):
                    ins = pe.matmul(ps[:, h * P:(h + 1) * P], g_k[:, h // 2, tile_cols[t]],
                                    q_pad[:, h, tile_cols[t]], start=True, stop=True)
                done(ins, ("gattn", t))
                taken(pe, ("kd", t))
                chunk_state(t, 0)
                go = fill(("gout", t))
                if t:
                    taken(pe, ("gstate", t - 1, 1))
                across_chunks(t, 0, go, True)
                chunk_state(t, 1)
                taken(pe, ("gstate", t, 0))
                across_chunks(t, 1, go, True)
                taken(pe, ("gattn", t))
                for h in range(GH):
                    ins = pe.matmul(go[:, h * GDV:(h + 1) * GDV], g_at[:, h, :], g_v[:, t, h * GDV:(h + 1) * GDV],
                                    start=False, stop=h == GH - 1, skip_group_check=True)
                done(ins, ("gout", t))
                for g in range(KVH):
                    pe.wait_ge(s["s_prob"], KVH * t + g + 1)
                    ps = fill(("probT", t, g))
                    for j in range(4):
                        ins = pe.transpose(ps[:, j * P:(j + 1) * P], s_p[:, g, j * P:(j + 1) * P], eye[:, :])
                    done(ins, ("probT", t, g))
                ps = fill(("sout", t))
                for g in range(KVH):
                    taken(pe, ("probT", t, g))
                    for hh in range(4):
                        h = 4 * g + hh
                        for c in range(2):
                            vals = s_vsh if c == 0 else s_v
                            ins = pe.matmul(ps[c * CH:(c + 1) * CH, h * HD:(h + 1) * HD],
                                            s_pT[:, g, hh * P + c * CH:hh * P + (c + 1) * CH],
                                            vals[:, t, g * HD:(g + 1) * HD], start=True, stop=True)
                done(ins, ("sout", t))
                if t:
                    turn_o(0, t - 1)
            for key in TAIL_FILLERS[0]:
                tile_of(key)
            turn_o(0, NT - 1)
            mix_and_norm(0)
            ffn(0)
            turn_x(2)
            fm_block(first_block[("conv", KD)], [("conv", KD), ("conv", KD + 1)], fresh=2)
            for i, n in enumerate(CONV_ORDER):
                b = first_block[("conv", n - n % 2)]
                if i >= 2:
                    ps = fill(("conv", n))
                    for k in range(KD):
                        if n % 2 == 0:
                            weights_there(b, k)
                        ins = mm3(ps[:, :], weights(b, k, (n % 2) * P, P), xcols(k, ALL), k == 0, k == KD - 1)
                    done(ins, ("conv", n))
                if i == 1:
                    ps = fill(("ba_fm",))
                    pe.wait_ge(s["ba_lo_ready"], 1)
                    for k in range(KD):
                        ins = mm3(ps[:, :], (ba_hi[:, k, :], ba_lo[:, k, :]), xcols(k, ALL), k == 0, k == KD - 1)
                    done(ins, ("ba_fm",))
                if i == 2:
                    taken(pe, ("ba_fm",))
                    ps = fill(("ba",))
                    for t in range(NT):
                        ins = pe.transpose(ps[:, t * BA:(t + 1) * BA], ba_fm[:, tile_cols[t]], eye[0:BA, 0:BA])
                    done(ins, ("ba",))
                if i == DECAY_AT:
                    ps = fill(("decay",))
                    pe.wait_ge(s["g_ready"], 1)
                    pe.wait_ge(consts, 16 * (N_CONST + N_CONST_ODD))
                    g = gdec[:, :, :].rearrange("p t h -> p (t h)")
                    pe.matmul(ps[:, 0:TH], o_upto[:, :], g, start=True, stop=True)
                    done(pe.matmul(ps[:, TH:2 * TH], ones[:, :].broadcast_to([P, P]), g, start=True, stop=True), ("decay",))
                if i >= 2 and CONV_ORDER[i - 2] < 2 * KD:
                    m = CONV_ORDER[i - 2]
                    ps = fill(("norm", m))
                    pe.wait_ge(s["conv_sq"], i - 1)
                    for t in range(NT):
                        ins = pe.matmul(ps[:, t:t + 1], conv_squares(i - 2)[:, tile_cols[t]], ones[:, :],
                                        start=True, stop=True)
                    done(ins, ("norm", m))

            def per_head(key, fn):
                ps = fill(key)
                for q in range(4):
                    ins = fn(ps[:, q * P:(q + 1) * P], 4 * key[-1] + q)
                done(ins, key)

            def mul(o, a, b_):
                return pe.matmul(o, a, b_, start=True, stop=True)

            for t in range(NT):
                tc_ = tile_cols[t]
                H = range(2)
                filler(t, -1)
                if t == 0:
                    pe.wait_ge(s["conv_silu"], len(CONV_ORDER))
                for hg in H:
                    per_head(("kTM", t, hg), lambda o, h: pe.transpose(o, qkv[:, KD + h, tc_], eye[:, :]))
                for hg in H:
                    per_head(("vTM", t, hg), lambda o, h: pe.transpose(o, qkv[:, 2 * KD + h, tc_], eye[:, :]))
                for hg in H:
                    pe.wait_ge(s["gu_ready"], 2 * t + hg + 1)
                    ps = fill(("drow", t, hg))
                    done(mul(ps[:, :], ones[:, :].broadcast_to([P, P]),
                             GU[:, hsl[hg], :].rearrange("p a b -> p (a b)")), ("drow", t, hg))
                filler(t, 0)
                for hg in H:
                    taken(pe, ("kTM", t, hg))
                    per_head(("khT", t, hg), lambda o, h: pe.transpose(o, KH[:, h, :], eye[:, :]))
                for hg in H:
                    taken(pe, ("khT", t, hg))
                    per_head(("gram", t, hg), lambda o, h: mul(o, qkv[:, KD + h, tc_], qkv[:, KD + h, tc_]))
                filler(t, 1)
                for hg in H:
                    taken(pe, ("gram", t, hg))
                    per_head(("at", t, hg), lambda o, h: pe.transpose(o, GA[:, h, :], eye[:, :]))
                filler(t, 2)
                for l, lv in enumerate(LEVELS[1:]):
                    for hg in H:
                        if l:
                            taken(pe, ("ds", t, LEVELS[l], hg))
                        else:
                            pe.wait_ge(s["s0_ready"], 2 * t + hg + 1)
                        ps = fill(("m1", t, lv, hg))
                        for q in range(4):
                            ins = mul(ps[:, q * HALF:(q + 1) * HALF], GA[:, 4 * hg + q, :],
                                      upper_halves(SS[:, 4 * hg + q, :], lv))
                        done(ins, ("m1", t, lv, hg))
                        per_head(("tt", t, lv, hg), lambda o, h: pe.transpose(o, SS[:, h, :], eye[:, :]))
                    for hg in H:
                        taken(pe, ("m1", t, lv, hg))
                        taken(pe, ("tt", t, lv, hg))
                        ps = fill(("ds", t, lv, hg))
                        for q in range(4):
                            ins = mul(ps[:, q * HALF:(q + 1) * HALF], TT[:, 4 * hg + q, :],
                                      half_product(hg)[:, q * HALF:(q + 1) * HALF])
                        done(ins, ("ds", t, lv, hg))
                    if lv == QK_AFTER:
                        for hg in H:
                            per_head(("qk", t, hg), lambda o, h: mul(o, qkv[:, KD + h, tc_], qkv[:, h, tc_]))
                    if lv == 8:
                        filler(t, 3)
                if t:
                    turn_o(1, t - 1)
                for hg in H:
                    taken(pe, ("ds", t, LEVELS[-1], hg))
                    taken(pe, ("vTM", t, hg))
                    per_head(("u", t, hg), lambda o, h: mul(o, SS[:, h, :], qkv[:, 2 * KD + h, tc_]))
                for hg in H:
                    pe.wait_ge(s["kb_ready"], 2 * t + hg + 1)
                    per_head(("w", t, hg), lambda o, h: mul(o, M1[:, h, :], SS[:, h, :]))
                for hg in H:
                    if t:
                        taken(pe, ("kv", t - 1, hg))
                    else:
                        pe.wait_ge(s["state0"], 1)
                    taken(pe, ("w", t, hg))
                    per_head(("ws", t, hg), lambda o, h: mul(o, TT[:, h, :], ST[:, h, :]))
                pe.wait_ge(s["q_decayed"], 2 * t + 2)
                for hg in H:
                    ps = fill(("o", t, hg))
                    for q in range(4):
                        pe.matmul(ps[:, q * P:(q + 1) * P], qkv[:, 4 * hg + q, tc_], ST[:, 4 * hg + q, :],
                                  start=q == 0, stop=False, skip_group_check=True)
                for hg in H:
                    taken(pe, ("ws", t, hg))
                    taken(pe, ("qk", t, hg))
                    ps = bank(("o", t, hg))
                    for q in range(4):
                        h = 4 * hg + q
                        ins = pe.matmul(ps[:, q * P:(q + 1) * P], GT[:, h, :], EE[:, h, :],
                                        start=False, stop=q == 3, skip_group_check=True)
                    done(ins, ("o", t, hg))
                for hg in H if t < NT - 1 else ():
                    pe.wait_ge(s["kd_ready"], 2 * t + hg + 1)
                    per_head(("kv", t, hg), lambda o, h: mul(o, KH[:, h, :], EE[:, h, :]))
            for key in TAIL_FILLERS[1]:
                tile_of(key)
            turn_o(1, NT - 1)
            mix_and_norm(1)
            ffn(1)


_INS = ["x", "ev_w_in", "ev_gla_w_a2", "ev_gla_b_a", "ev_gla_norm_g", "ev_swa_sinks", "ev_w_out", "od_w_in",
        "od_conv_w", "od_a_log", "od_dt_bias", "od_norm_g", "od_w_out", "ffn_w_gate", "ffn_w_up", "ffn_w_down",
        "ln1_g", "ln1_b", "ln2_g", "ln2_b"]


def kernel(**inputs):
    import concourse.bacc as bacc
    from concourse.bass_utils import run_bass_kernel_spmd

    nc = bacc.Bacc("TRN2", target_bir_lowering=False, num_devices=1)
    arrays, views = {}, {}
    given = {n: np.ascontiguousarray(inputs[n]) for n in _INS}
    given.update(shape_constants())
    for name, a in given.items():
        arrays[name + "_dram"] = a
        views[name] = nc.dram_tensor(name + "_dram", a.shape, mybir.dt.from_np(a.dtype), kind="ExternalInput").ap()
    out = nc.dram_tensor("out_dram", (1, SEQ, D), F32, kind="ExternalOutput").ap()
    trunk_kernel(nc, views, out)
    r = run_bass_kernel_spmd(nc, [arrays], core_ids=[0])
    return r.results[0]["out_dram"]
```
